# Optimizing a Trainium2 kernel written in Bass

```python
import math
import jax, jax.numpy as jnp
from jax import lax
import numpy as np

D_MODEL = 1024
BATCH = 1
SEQ = 512
DEPTH = 1

HEAD_DIM = 64
FOX_HEADS = 4
FOX_W = FOX_HEADS * HEAD_DIM
CONV_W = 256
CONV_K = 3
MLSTM_HEADS = 4
MLSTM_W = MLSTM_HEADS * HEAD_DIM
MLSTM_CHUNK = 64
SWA_Q_HEADS = 8
SWA_KV_HEADS = 2
SWA_W = SWA_Q_HEADS * HEAD_DIM
SWA_KV_W = SWA_KV_HEADS * HEAD_DIM
WINDOW = 128
Q_BLOCK = 128
REL_BUCKETS = 32
REL_MAX_DIST = 128
N_BRANCH = 4
D_FF = -(-8 * D_MODEL // (3 * 256)) * 256
EPS = 1e-6

SPLIT_SIZES = (FOX_W, FOX_W, FOX_W, FOX_HEADS,
               CONV_W, CONV_W, CONV_W,
               MLSTM_W, MLSTM_W, MLSTM_W, MLSTM_HEADS, MLSTM_HEADS, MLSTM_W,
               SWA_W, SWA_KV_W, SWA_KV_W,
               N_BRANCH * D_MODEL)
IN_COLS = sum(SPLIT_SIZES)


def rms_norm(x, gain):
    xf = x.astype(jnp.float32)
    y = xf * lax.rsqrt(jnp.mean(xf * xf, axis=-1, keepdims=True) + EPS)
    return (y * gain.astype(jnp.float32)).astype(x.dtype)

def t5_bucket(n):
    max_exact = REL_BUCKETS // 2
    nf = jnp.maximum(n, 1).astype(jnp.float32)
    large = max_exact + (jnp.log(nf / max_exact) / math.log(REL_MAX_DIST / max_exact)
                         * (REL_BUCKETS - max_exact)).astype(jnp.int32)
    large = jnp.minimum(large, REL_BUCKETS - 1)
    return jnp.where(n < max_exact, n, large)

def fox_attention(q, k, v, f_logit):
    B, S, H, d = q.shape
    nblk = S // Q_BLOCK
    c = jnp.cumsum(jax.nn.log_sigmoid(f_logit.astype(jnp.float32)), axis=1)
    c_t = c.transpose(0, 2, 1)
    qb = q.reshape(B, nblk, Q_BLOCK, H, d).transpose(1, 0, 2, 3, 4)
    cb = c.reshape(B, nblk, Q_BLOCK, H).transpose(1, 0, 3, 2)
    key_pos = jnp.arange(S)
    scale = d ** -0.5

    def block(args):
        qi, ci, bi = args
        s = jnp.einsum('bqhd,bkhd->bhqk', qi, k).astype(jnp.float32) * scale
        s = s + (ci[..., :, None] - c_t[..., None, :])
        q_pos = bi * Q_BLOCK + jnp.arange(Q_BLOCK)
        s = jnp.where(key_pos[None, :] <= q_pos[:, None], s, -jnp.inf)
        p = jax.nn.softmax(s, axis=-1).astype(v.dtype)
        return jnp.einsum('bhqk,bkhd->bqhd', p, v)

    out = lax.map(block, (qb, cb, jnp.arange(nblk)))
    return out.transpose(1, 0, 2, 3, 4).reshape(B, S, H * d)

def short_conv_mixer(u, b_gate, c_gate, w):
    z = c_gate * u
    y = lax.conv_general_dilated(z, w[:, None, :], window_strides=(1,),
                                 padding=[(CONV_K - 1, 0)],
                                 dimension_numbers=('NWC', 'WIO', 'NWC'),
                                 feature_group_count=z.shape[-1])
    return b_gate * y

def mlstm_chunkwise(q, k, v, i_pre, f_pre):
    out_dtype = q.dtype
    f32 = jnp.float32
    B, S, H, d = q.shape
    L = MLSTM_CHUNK
    nc = S // L
    q = q.astype(f32).reshape(B, nc, L, H, d) * d ** -0.5
    k = k.astype(f32).reshape(B, nc, L, H, d)
    v = v.astype(f32).reshape(B, nc, L, H, d)
    log_i = i_pre.astype(f32).reshape(B, nc, L, H)
    log_f = jax.nn.log_sigmoid(f_pre.astype(f32)).reshape(B, nc, L, H)
    b = jnp.cumsum(log_f, axis=2)
    b_last = b[:, :, -1]

    a = b_last[:, :, None] - b + log_i
    m_loc = a.max(axis=2)
    w_state = jnp.exp(a - m_loc[:, :, None])
    c_loc = jnp.einsum('bclh,bclhd,bclhe->bchde', w_state, k, v)
    n_loc = jnp.einsum('bclh,bclhd->bchd', w_state, k)

    def step(carry, xs):
        c_st, n_st, m_st = carry
        bl, ml, cl, nl = xs
        m_new = jnp.maximum(bl + m_st, ml)
        decay = jnp.exp(bl + m_st - m_new)
        wl = jnp.exp(ml - m_new)
        c_new = decay[..., None, None] * c_st + wl[..., None, None] * cl
        n_new = decay[..., None] * n_st + wl[..., None] * nl
        return (c_new, n_new, m_new), (c_st, n_st, m_st)

    init = (jnp.zeros((B, H, d, d), f32), jnp.zeros((B, H, d), f32), jnp.zeros((B, H), f32))
    xs = (jnp.moveaxis(b_last, 1, 0), jnp.moveaxis(m_loc, 1, 0),
          jnp.moveaxis(c_loc, 1, 0), jnp.moveaxis(n_loc, 1, 0))
    _, (c_prev, n_prev, m_prev) = lax.scan(step, init, xs)
    c_prev = jnp.moveaxis(c_prev, 0, 1)
    n_prev = jnp.moveaxis(n_prev, 0, 1)
    m_prev = jnp.moveaxis(m_prev, 0, 1)

    g = b + m_prev[:, :, None, :]
    dmat = b[:, :, :, None, :] - b[:, :, None, :, :] + log_i[:, :, None, :, :]
    causal = jnp.tril(jnp.ones((L, L), dtype=bool))
    dmat = jnp.where(causal[None, None, :, :, None], dmat, -jnp.inf)
    m_t = jnp.maximum(g, dmat.max(axis=3))
    s_w = jnp.einsum('bcthd,bcshd->bctsh', q, k) * jnp.exp(dmat - m_t[:, :, :, None, :])
    inter = jnp.exp(g - m_t)
    num = (jnp.einsum('bctsh,bcshe->bcthe', s_w, v)
           + inter[..., None] * jnp.einsum('bcthd,bchde->bcthe', q, c_prev))
    den = s_w.sum(axis=3) + inter * jnp.einsum('bcthd,bchd->bcth', q, n_prev)
    h = num / jnp.maximum(jnp.abs(den), jnp.exp(-m_t))[..., None]
    return h.reshape(B, S, H, d).astype(out_dtype)

def swa_attention(q, k, v, sinks, bias):
    B, S, Hq, d = q.shape
    Hkv = k.shape[2]
    G = Hq // Hkv
    W = WINDOW
    nb = S // W
    qb = q.reshape(B, nb, W, Hkv, G, d)

    def band(t):
        tp = jnp.pad(t, ((0, 0), (W, 0), (0, 0), (0, 0))).reshape(B, nb + 1, W, Hkv, d)
        return jnp.concatenate([tp[:, :-1], tp[:, 1:]], axis=2)

    kb, vb = band(k), band(v)
    s = jnp.einsum('bnqhgd,bnjhd->bnhgqj', qb, kb).astype(jnp.float32) * d ** -0.5
    s = s + bias.astype(jnp.float32).reshape(Hkv, G, W, 2 * W)
    qi = jnp.arange(W)[:, None]
    kj = jnp.arange(2 * W)[None, :]
    dist = qi + W - kj
    in_window = (dist >= 0) & (dist < WINDOW)
    key_pos = jnp.arange(nb)[:, None, None] * W - W + kj[None]
    valid = in_window[None] & (key_pos >= 0)
    s = jnp.where(valid[None, :, None, None], s, -jnp.inf)
    sink = jnp.broadcast_to(sinks.astype(jnp.float32).reshape(1, 1, Hkv, G, 1, 1),
                            s.shape[:-1] + (1,))
    p = jax.nn.softmax(jnp.concatenate([s, sink], axis=-1), axis=-1)[..., :-1]
    out = jnp.einsum('bnhgqj,bnjhd->bnqhgd', p.astype(v.dtype), vb)
    return out.reshape(B, S, Hq * d)

def first_inputs(seed: int = 0) -> dict:
    key = jax.random.key(seed)
    ks = jax.random.split(key, 24)

    def nrm(k, shape, scale):
        return jax.random.normal(k, shape, jnp.float32) * scale

    return {
        'x': nrm(ks[0], (BATCH, SEQ, D_MODEL), 1.0),
        'rel_bias': nrm(ks[1], (REL_BUCKETS, SWA_Q_HEADS), 0.5),
        'attn_norm': 1.0 + nrm(ks[2], (DEPTH, D_MODEL), 0.05),
        'w_in': nrm(ks[3], (DEPTH, D_MODEL, IN_COLS), D_MODEL ** -0.5),
        'fox_f_bias': 3.0 + nrm(ks[4], (DEPTH, FOX_HEADS), 1.0),
        'fox_q_gain': 1.0 + nrm(ks[5], (DEPTH, HEAD_DIM), 0.05),
        'fox_k_gain': 1.0 + nrm(ks[6], (DEPTH, HEAD_DIM), 0.05),
        'conv_w': nrm(ks[7], (DEPTH, CONV_K, CONV_W), CONV_K ** -0.5),
        'mlstm_i_bias': nrm(ks[8], (DEPTH, MLSTM_HEADS), 0.1),
        'mlstm_f_bias': 4.0 + nrm(ks[9], (DEPTH, MLSTM_HEADS), 1.0),
        'mlstm_h_gain': 1.0 + nrm(ks[10], (DEPTH, MLSTM_W), 0.05),
        'swa_q_gain': 1.0 + nrm(ks[11], (DEPTH, HEAD_DIM), 0.05),
        'swa_k_gain': 1.0 + nrm(ks[12], (DEPTH, HEAD_DIM), 0.05),
        'swa_sinks': nrm(ks[13], (DEPTH, SWA_Q_HEADS), 1.0),
        'w_fox_out': nrm(ks[14], (DEPTH, FOX_W, D_MODEL), FOX_W ** -0.5),
        'w_conv_out': nrm(ks[15], (DEPTH, CONV_W, D_MODEL), CONV_W ** -0.5),
        'w_mlstm_out': nrm(ks[16], (DEPTH, MLSTM_W, D_MODEL), MLSTM_W ** -0.5),
        'w_swa_out': nrm(ks[17], (DEPTH, SWA_W, D_MODEL), SWA_W ** -0.5),
        'w_merge_out': nrm(ks[18], (DEPTH, D_MODEL, D_MODEL), D_MODEL ** -0.5),
        'ffn_norm': 1.0 + nrm(ks[19], (DEPTH, D_MODEL), 0.05),
        'w_gate': nrm(ks[20], (DEPTH, D_MODEL, D_FF), D_MODEL ** -0.5),
        'w_up': nrm(ks[21], (DEPTH, D_MODEL, D_FF), D_MODEL ** -0.5),
        'w_down': nrm(ks[22], (DEPTH, D_FF, D_MODEL), D_FF ** -0.5),
    }

def first_block(x, rel_bias, attn_norm, w_in, fox_f_bias, fox_q_gain, fox_k_gain, conv_w,
              mlstm_i_bias, mlstm_f_bias, mlstm_h_gain, swa_q_gain, swa_k_gain, swa_sinks,
              w_fox_out, w_conv_out, w_mlstm_out, w_swa_out, w_merge_out, ffn_norm,
              w_gate, w_up, w_down):
    B, S, _ = x.shape
    split_points = np.cumsum(SPLIT_SIZES)[:-1].tolist()

    dist = jnp.arange(WINDOW)[:, None] + WINDOW - jnp.arange(2 * WINDOW)[None, :]
    swa_bias = rel_bias[t5_bucket(jnp.maximum(dist, 0))].transpose(2, 0, 1)

    for l in range(DEPTH):
        h = rms_norm(x, attn_norm[l])
        proj = jnp.einsum('bsd,dc->bsc', h, w_in[l])
        (fq, fk, fv, ff, cu, cb, cc, mq, mk, mv, mi, mf, mo, sq, sk, sv,
         gates) = jnp.split(proj, split_points, axis=-1)

        fq = rms_norm(fq.reshape(B, S, FOX_HEADS, HEAD_DIM), fox_q_gain[l])
        fk = rms_norm(fk.reshape(B, S, FOX_HEADS, HEAD_DIM), fox_k_gain[l])
        fv = fv.reshape(B, S, FOX_HEADS, HEAD_DIM)
        y_fox = fox_attention(fq, fk, fv, ff + fox_f_bias[l])

        y_conv = short_conv_mixer(cu, cb, cc, conv_w[l])

        hm = mlstm_chunkwise(mq.reshape(B, S, MLSTM_HEADS, HEAD_DIM),
                             mk.reshape(B, S, MLSTM_HEADS, HEAD_DIM),
                             mv.reshape(B, S, MLSTM_HEADS, HEAD_DIM),
                             mi + mlstm_i_bias[l], mf + mlstm_f_bias[l])
        hm = rms_norm(hm, mlstm_h_gain[l].reshape(MLSTM_HEADS, HEAD_DIM))
        y_mlstm = jax.nn.sigmoid(mo) * hm.reshape(B, S, MLSTM_W)

        sq = rms_norm(sq.reshape(B, S, SWA_Q_HEADS, HEAD_DIM), swa_q_gain[l])
        sk = rms_norm(sk.reshape(B, S, SWA_KV_HEADS, HEAD_DIM), swa_k_gain[l])
        sv = sv.reshape(B, S, SWA_KV_HEADS, HEAD_DIM)
        y_swa = swa_attention(sq, sk, sv, swa_sinks[l], swa_bias)

        g = jax.nn.sigmoid(gates.reshape(B, S, N_BRANCH, D_MODEL))
        merged = (g[:, :, 0] * jnp.einsum('bsw,wd->bsd', y_fox, w_fox_out[l])
                  + g[:, :, 1] * jnp.einsum('bsw,wd->bsd', y_conv, w_conv_out[l])
                  + g[:, :, 2] * jnp.einsum('bsw,wd->bsd', y_mlstm, w_mlstm_out[l])
                  + g[:, :, 3] * jnp.einsum('bsw,wd->bsd', y_swa, w_swa_out[l]))
        x = x + jnp.einsum('bsd,de->bse', merged, w_merge_out[l])

        h = rms_norm(x, ffn_norm[l])
        act = jax.nn.silu(jnp.einsum('bsd,df->bsf', h, w_gate[l])) * jnp.einsum('bsd,df->bsf', h, w_up[l])
        x = x + jnp.einsum('bsf,fd->bsd', act, w_down[l])
    return x


N_MIXERS = 3
N_LAYERS_NSA = len(range(0, DEPTH, N_MIXERS))
N_LAYERS_GDN = len(range(1, DEPTH, N_MIXERS))
N_LAYERS_DIFF = len(range(2, DEPTH, N_MIXERS))

NSA_HEADS = 16
NSA_GROUPS = 4
NSA_HPG = NSA_HEADS // NSA_GROUPS
NSA_HEAD_DIM = D_MODEL // NSA_HEADS
NSA_KV_WIDTH = NSA_GROUPS * NSA_HEAD_DIM
NSA_IN_WIDTH = D_MODEL + 6 * NSA_KV_WIDTH + 3 * NSA_HEADS
CMP_BLOCK = 32
CMP_STRIDE = 16
CMP_HIDDEN = 256
SEL_BLOCK = 64
N_SEL_BLOCKS = 16
WINDOW_2 = 512
NSA_QBLOCK = 32

GDN_HEADS = 8
GDN_HEAD_DIM = D_MODEL // GDN_HEADS
GDN_WIDTH = GDN_HEADS * GDN_HEAD_DIM
GDN_IN_WIDTH = 4 * GDN_WIDTH + 2 * GDN_HEADS
GDN_CONV = 4
GDN_CHUNK = 64

DIFF_HEADS = 8
DIFF_HEAD_DIM = D_MODEL // (2 * DIFF_HEADS)
DIFF_IN_WIDTH = 3 * D_MODEL
ATTN_QBLOCK = 128

MEM_TOKENS = 256
MEM_HEADS = 4
MEM_HEAD_DIM = D_MODEL // MEM_HEADS

D_FF_2 = 2816
FFN_CONV = 3

RMS_EPS = 1e-6
NEG_INF = -1e30
FORCE_SCORE = 1e4


def rmsnorm(x, w):
    xf = x.astype(jnp.float32)
    y = xf * lax.rsqrt(jnp.mean(xf * xf, axis=-1, keepdims=True) + RMS_EPS)
    return (y * w.astype(jnp.float32)).astype(x.dtype)

def l2norm(x):
    return x * lax.rsqrt(jnp.sum(x * x, axis=-1, keepdims=True) + RMS_EPS)

def masked_softmax(s, mask):
    s = s.astype(jnp.float32)
    m = jnp.max(jnp.where(mask, s, NEG_INF), axis=-1, keepdims=True)
    e = jnp.exp(jnp.where(mask, s - m, NEG_INF))
    denom = jnp.sum(e, axis=-1, keepdims=True)
    return e / jnp.where(denom > 0, denom, 1.0)

def causal_dwconv(x, w):
    K = w.shape[0]
    S = x.shape[1]
    xp = jnp.pad(x, ((0, 0), (K - 1, 0), (0, 0)))
    return sum(xp[:, j:j + S] * w[j] for j in range(K))

def _compress(t, pe, w1, w2):
    B, S, G, dk = t.shape
    n_chunks = S // CMP_STRIDE
    r = CMP_BLOCK // CMP_STRIDE
    n_cmp = n_chunks - r + 1
    c = t.reshape(B, n_chunks, CMP_STRIDE, G, dk)
    blk = jnp.concatenate([c[:, j:j + n_cmp] for j in range(r)], axis=2)
    blk = (blk + pe[:, None, :]).transpose(0, 1, 3, 2, 4).reshape(B, n_cmp, G, CMP_BLOCK * dk)
    return jax.nn.gelu(blk @ w1) @ w2

def nsa_mixer(h, w_in, pe_k, pe_v, ck_w1, ck_w2, cv_w1, cv_w2, w_out):
    B, S, _ = h.shape
    G, Hg, dk, QB = NSA_GROUPS, NSA_HPG, NSA_HEAD_DIM, NSA_QBLOCK
    cuts = [D_MODEL + i * NSA_KV_WIDTH for i in range(7)]
    q, kc, vc, ks, vs, kw, vw, gl = jnp.split(h @ w_in, cuts, axis=-1)
    q = q.reshape(B, S, G, Hg, dk) * dk ** -0.5
    gates = jax.nn.sigmoid(gl).reshape(B, S, G, Hg, 3)

    def kv(t):
        return t.reshape(B, S, G, dk)

    k_cmp = _compress(kv(kc), pe_k, ck_w1, ck_w2)
    v_cmp = _compress(kv(vc), pe_v, cv_w1, cv_w2)
    n_cmp = k_cmp.shape[1]
    n_blk = S // SEL_BLOCK
    n_sel = min(N_SEL_BLOCKS, n_blk)
    k_sel = kv(ks).reshape(B, n_blk, SEL_BLOCK, G, dk).transpose(0, 3, 1, 2, 4)
    v_sel = kv(vs).reshape(B, n_blk, SEL_BLOCK, G, dk).transpose(0, 3, 1, 2, 4)
    pad = ((0, 0), (WINDOW_2, 0), (0, 0), (0, 0))
    k_win = jnp.pad(kv(kw), pad)
    v_win = jnp.pad(kv(vw), pad)

    cmp_end = jnp.arange(n_cmp) * CMP_STRIDE + CMP_BLOCK - 1
    sel_start = jnp.arange(n_blk) * SEL_BLOCK
    overlap = ((cmp_end[:, None] - CMP_BLOCK + 1 <= sel_start[None, :] + SEL_BLOCK - 1)
               & (cmp_end[:, None] >= sel_start[None, :])).astype(jnp.float32)
    b_idx = jnp.arange(B)[:, None, None]
    g_idx = jnp.arange(G)[None, :, None]
    blk_ids = jnp.arange(n_blk)[None, :]

    def one_block(args):
        q_blk, g_blk, blk = args
        t = blk * QB + jnp.arange(QB)
        qg = q_blk.transpose(0, 2, 3, 1, 4)
        p_cmp = masked_softmax(jnp.einsum('bghtd,bngd->bghtn', qg, k_cmp), cmp_end[None, :] <= t[:, None])
        o_cmp = jnp.einsum('bghtn,bngd->btghd', p_cmp.astype(v_cmp.dtype), v_cmp)
        imp = jnp.einsum('bghtn,nj->btgj', p_cmp, overlap)
        cur = (t // SEL_BLOCK)[:, None]
        forced = ((blk_ids == 0) | (blk_ids == cur) | (blk_ids == cur - 1))[:, None, :]
        valid = (sel_start[None, :] <= t[:, None])[:, None, :]
        imp = jnp.where(forced, FORCE_SCORE, jnp.where(valid, imp, -FORCE_SCORE))
        _, top = lax.top_k(imp, n_sel)
        top = top.transpose(0, 2, 1, 3)
        flat = top.reshape(B, G, QB * n_sel)
        k_g = k_sel[b_idx, g_idx, flat].reshape(B, G, QB, n_sel * SEL_BLOCK, dk)
        v_g = v_sel[b_idx, g_idx, flat].reshape(B, G, QB, n_sel * SEL_BLOCK, dk)
        pos = (top[..., None] * SEL_BLOCK + jnp.arange(SEL_BLOCK)).reshape(B, G, QB, n_sel * SEL_BLOCK)
        p_sel = masked_softmax(jnp.einsum('bghtd,bgtkd->bghtk', qg, k_g), (pos <= t[:, None])[:, :, None])
        o_sel = jnp.einsum('bghtk,bgtkd->btghd', p_sel.astype(v_g.dtype), v_g)
        start = blk * QB
        k_w = lax.dynamic_slice_in_dim(k_win, start, WINDOW_2 + QB, axis=1)
        v_w = lax.dynamic_slice_in_dim(v_win, start, WINDOW_2 + QB, axis=1)
        wpos = start - WINDOW_2 + jnp.arange(WINDOW_2 + QB)
        wmask = ((wpos[None, :] <= t[:, None]) & (wpos[None, :] > t[:, None] - WINDOW_2)
                 & (wpos[None, :] >= 0))
        p_win = masked_softmax(jnp.einsum('bghtd,bkgd->bghtk', qg, k_w), wmask)
        o_win = jnp.einsum('bghtk,bkgd->btghd', p_win.astype(v_w.dtype), v_w)
        o = g_blk[..., 0:1] * o_cmp + g_blk[..., 1:2] * o_sel + g_blk[..., 2:3] * o_win
        return o.reshape(B, QB, G * Hg * dk)

    nqb = S // QB
    q_blocks = q.reshape(B, nqb, QB, G, Hg, dk).transpose(1, 0, 2, 3, 4, 5)
    g_blocks = gates.reshape(B, nqb, QB, G, Hg, 3).transpose(1, 0, 2, 3, 4, 5)
    o = lax.map(one_block, (q_blocks, g_blocks, jnp.arange(nqb)))
    o = o.transpose(1, 0, 2, 3).reshape(B, S, D_MODEL)
    return o @ w_out

def chunk_gated_delta_rule(q, k, v, g, beta):
    B, S, H, dk = q.shape
    dv = v.shape[-1]
    C = GDN_CHUNK
    N = S // C

    def to_chunks(t):
        return t.reshape(B, N, C, H, t.shape[-1]).transpose(0, 3, 1, 2, 4)

    q, k, v = to_chunks(q), to_chunks(k), to_chunks(v)
    g = g.reshape(B, N, C, H).transpose(0, 3, 1, 2)
    beta = beta.reshape(B, N, C, H).transpose(0, 3, 1, 2)
    gc = jnp.cumsum(g, axis=-1)
    tri = jnp.tril(jnp.ones((C, C), dtype=bool))
    strict = jnp.tril(jnp.ones((C, C), dtype=bool), -1)
    diff = gc[..., :, None] - gc[..., None, :]
    decay = jnp.where(tri, jnp.exp(jnp.where(tri, diff, 0.0)), 0.0)
    kb = k * beta[..., None]
    vb = v * beta[..., None]
    a_mat = jnp.where(strict, jnp.einsum('bhncd,bhnmd->bhncm', kb, k) * decay, 0.0) + jnp.eye(C, dtype=q.dtype)
    rhs = jnp.concatenate([vb, kb * jnp.exp(gc)[..., None]], axis=-1)
    sol = lax.linalg.triangular_solve(a_mat, rhs, left_side=True, lower=True, unit_diagonal=True)
    u, w = sol[..., :dv], sol[..., dv:]
    qk = jnp.einsum('bhncd,bhnmd->bhncm', q, k) * decay
    q_dec = q * jnp.exp(gc)[..., None]
    k_dec = k * jnp.exp(gc[..., -1:] - gc)[..., None]
    g_last = jnp.exp(gc[..., -1])
    xs = (jnp.moveaxis(q_dec, 2, 0), jnp.moveaxis(k_dec, 2, 0), jnp.moveaxis(u, 2, 0),
          jnp.moveaxis(w, 2, 0), jnp.moveaxis(qk, 2, 0), jnp.moveaxis(g_last, 2, 0))

    def step(state, inp):
        qd, kd, uc, wc, qkc, gl = inp
        v_new = uc - jnp.einsum('bhcd,bhde->bhce', wc, state)
        o = jnp.einsum('bhcd,bhde->bhce', qd, state) + jnp.einsum('bhcm,bhme->bhce', qkc, v_new)
        state = state * gl[..., None, None] + jnp.einsum('bhcd,bhce->bhde', kd, v_new)
        return state, o

    _, o = lax.scan(step, jnp.zeros((B, H, dk, dv), q.dtype), xs)
    return o.transpose(1, 0, 3, 2, 4).reshape(B, S, H, dv)

def gdn_mixer(h, w_in, conv_w, a_log, dt_bias, norm_w, w_out):
    B, S, _ = h.shape
    H, d = GDN_HEADS, GDN_HEAD_DIM
    qkv, z, b_raw, a_raw = jnp.split(h @ w_in, [3 * GDN_WIDTH, 4 * GDN_WIDTH, 4 * GDN_WIDTH + H], axis=-1)
    qkv = jax.nn.silu(causal_dwconv(qkv, conv_w)).astype(jnp.float32)
    q, k, v = jnp.split(qkv, 3, axis=-1)
    q = l2norm(q.reshape(B, S, H, d)) * d ** -0.5
    k = l2norm(k.reshape(B, S, H, d))
    v = v.reshape(B, S, H, d)
    beta = jax.nn.sigmoid(b_raw.astype(jnp.float32))
    g = -jnp.exp(a_log.astype(jnp.float32)) * jax.nn.softplus(a_raw.astype(jnp.float32) + dt_bias.astype(jnp.float32))
    o = chunk_gated_delta_rule(q, k, v, g, beta)
    o = rmsnorm(o, norm_w) * jax.nn.silu(z.reshape(B, S, H, d).astype(jnp.float32))
    return o.reshape(B, S, GDN_WIDTH).astype(h.dtype) @ w_out

def diff_mixer(h, w_in, lq1, lk1, lq2, lk2, subln_w, w_out, lambda_init):
    B, S, _ = h.shape
    H, dh, QB = DIFF_HEADS, DIFF_HEAD_DIM, ATTN_QBLOCK
    q, k, v = jnp.split(h @ w_in, 3, axis=-1)
    q = q.reshape(B, S, H, 2, dh) * dh ** -0.5
    k = k.reshape(B, S, H, 2, dh)
    v = v.reshape(B, S, H, 2 * dh)
    f32 = jnp.float32
    lam = (jnp.exp(jnp.sum(lq1.astype(f32) * lk1.astype(f32))) - jnp.exp(jnp.sum(lq2.astype(f32) * lk2.astype(f32)))
           + lambda_init)
    kpos = jnp.arange(S)

    def one_block(args):
        q_blk, blk = args
        t = blk * QB + jnp.arange(QB)
        p = masked_softmax(jnp.einsum('bqhcd,bkhcd->bhcqk', q_blk, k), kpos[None, :] <= t[:, None])
        a = p[:, :, 0] - lam * p[:, :, 1]
        return jnp.einsum('bhqk,bkhd->bqhd', a.astype(v.dtype), v)

    nqb = S // QB
    q_blocks = q.reshape(B, nqb, QB, H, 2, dh).transpose(1, 0, 2, 3, 4, 5)
    o = lax.map(one_block, (q_blocks, jnp.arange(nqb)))
    o = o.transpose(1, 0, 2, 3, 4).reshape(B, S, H, 2 * dh)
    o = rmsnorm(o, subln_w) * (1.0 - lambda_init)
    return o.reshape(B, S, D_MODEL) @ w_out

def memory_cross_attention(h, mem_n, wq, wkv, wo):
    B, S, _ = h.shape
    M = mem_n.shape[1]
    q = (h @ wq).reshape(B, S, MEM_HEADS, MEM_HEAD_DIM) * MEM_HEAD_DIM ** -0.5
    k, v = jnp.split(mem_n @ wkv, 2, axis=-1)
    k = k.reshape(B, M, MEM_HEADS, MEM_HEAD_DIM)
    v = v.reshape(B, M, MEM_HEADS, MEM_HEAD_DIM)
    p = jax.nn.softmax(jnp.einsum('bshd,bmhd->bhsm', q, k).astype(jnp.float32), axis=-1)
    o = jnp.einsum('bhsm,bmhd->bshd', p.astype(v.dtype), v)
    return o.reshape(B, S, D_MODEL) @ wo

def conv_ffn(h, w_up, conv_w, w_down):
    gate, val = jnp.split(h @ w_up, 2, axis=-1)
    return (jax.nn.silu(causal_dwconv(gate, conv_w)) * val) @ w_down

def second_inputs(seed: int = 0) -> dict:
    key = jax.random.key(seed)
    keys = iter(jax.random.split(key, 48))

    def nrm(shape, scale):
        return scale * jax.random.normal(next(keys), shape, jnp.float32)

    def gain(shape):
        return 1.0 + nrm(shape, 0.02)

    D = D_MODEL
    nA, nB, nC = N_LAYERS_NSA, N_LAYERS_GDN, N_LAYERS_DIFF
    dk = NSA_HEAD_DIM
    inp = {}
    inp['x'] = nrm((BATCH, SEQ, D), 1.0)
    inp['mem'] = nrm((BATCH, MEM_TOKENS, D), 1.0)
    inp['mem_norm_w'] = gain((D,))
    inp['final_norm_w'] = gain((D,))
    inp['norm_mix_w'] = gain((DEPTH, D))
    inp['norm_cross_w'] = gain((DEPTH, D))
    inp['norm_ffn_w'] = gain((DEPTH, D))
    inp['ca_wq'] = nrm((DEPTH, D, D), D ** -0.5)
    inp['ca_wkv'] = nrm((DEPTH, D, 2 * D), D ** -0.5)
    inp['ca_wo'] = nrm((DEPTH, D, D), D ** -0.5)
    inp['ffn_w_up'] = nrm((DEPTH, D, 2 * D_FF_2), D ** -0.5)
    inp['ffn_conv_w'] = nrm((DEPTH, FFN_CONV, D_FF_2), FFN_CONV ** -0.5)
    inp['ffn_w_down'] = nrm((DEPTH, D_FF_2, D), D_FF_2 ** -0.5)
    inp['nsa_w_in'] = nrm((nA, D, NSA_IN_WIDTH), D ** -0.5)
    inp['nsa_pe_k'] = nrm((nA, CMP_BLOCK, dk), 0.02)
    inp['nsa_pe_v'] = nrm((nA, CMP_BLOCK, dk), 0.02)
    inp['nsa_ck_w1'] = nrm((nA, CMP_BLOCK * dk, CMP_HIDDEN), (CMP_BLOCK * dk) ** -0.5)
    inp['nsa_ck_w2'] = nrm((nA, CMP_HIDDEN, dk), CMP_HIDDEN ** -0.5)
    inp['nsa_cv_w1'] = nrm((nA, CMP_BLOCK * dk, CMP_HIDDEN), (CMP_BLOCK * dk) ** -0.5)
    inp['nsa_cv_w2'] = nrm((nA, CMP_HIDDEN, dk), CMP_HIDDEN ** -0.5)
    inp['nsa_w_out'] = nrm((nA, D, D), D ** -0.5)
    inp['gdn_w_in'] = nrm((nB, D, GDN_IN_WIDTH), D ** -0.5)
    inp['gdn_conv_w'] = nrm((nB, GDN_CONV, 3 * GDN_WIDTH), GDN_CONV ** -0.5)
    inp['gdn_a_log'] = jnp.log(jax.random.uniform(next(keys), (nB, GDN_HEADS), jnp.float32, 1.0, 16.0))
    dt = jnp.exp(jax.random.uniform(next(keys), (nB, GDN_HEADS), jnp.float32, math.log(1e-3), math.log(1e-1)))
    inp['gdn_dt_bias'] = dt + jnp.log(-jnp.expm1(-dt))
    inp['gdn_norm_w'] = gain((nB, GDN_HEAD_DIM))
    inp['gdn_w_out'] = nrm((nB, GDN_WIDTH, D), GDN_WIDTH ** -0.5)
    inp['diff_w_in'] = nrm((nC, D, DIFF_IN_WIDTH), D ** -0.5)
    inp['diff_lq1'] = nrm((nC, DIFF_HEAD_DIM), 0.1)
    inp['diff_lk1'] = nrm((nC, DIFF_HEAD_DIM), 0.1)
    inp['diff_lq2'] = nrm((nC, DIFF_HEAD_DIM), 0.1)
    inp['diff_lk2'] = nrm((nC, DIFF_HEAD_DIM), 0.1)
    inp['diff_subln_w'] = gain((nC, 2 * DIFF_HEAD_DIM))
    inp['diff_w_out'] = nrm((nC, D, D), D ** -0.5)
    return inp

def second_block(x, mem, mem_norm_w, final_norm_w, norm_mix_w, norm_cross_w, norm_ffn_w,
              ca_wq, ca_wkv, ca_wo, ffn_w_up, ffn_conv_w, ffn_w_down,
              nsa_w_in, nsa_pe_k, nsa_pe_v, nsa_ck_w1, nsa_ck_w2, nsa_cv_w1, nsa_cv_w2, nsa_w_out,
              gdn_w_in, gdn_conv_w, gdn_a_log, gdn_dt_bias, gdn_norm_w, gdn_w_out,
              diff_w_in, diff_lq1, diff_lk1, diff_lq2, diff_lk2, diff_subln_w, diff_w_out):
    mem_n = rmsnorm(mem, mem_norm_w)
    for i in range(DEPTH):
        kind, j = i % N_MIXERS, i // N_MIXERS
        h = rmsnorm(x, norm_mix_w[i])
        if kind == 0:
            y = nsa_mixer(h, nsa_w_in[j], nsa_pe_k[j], nsa_pe_v[j], nsa_ck_w1[j], nsa_ck_w2[j],
                          nsa_cv_w1[j], nsa_cv_w2[j], nsa_w_out[j])
        elif kind == 1:
            y = gdn_mixer(h, gdn_w_in[j], gdn_conv_w[j], gdn_a_log[j], gdn_dt_bias[j], gdn_norm_w[j], gdn_w_out[j])
        else:
            lambda_init = 0.8 - 0.6 * math.exp(-0.3 * i)
            y = diff_mixer(h, diff_w_in[j], diff_lq1[j], diff_lk1[j], diff_lq2[j], diff_lk2[j],
                           diff_subln_w[j], diff_w_out[j], lambda_init)
        x = x + y
        x = x + memory_cross_attention(rmsnorm(x, norm_cross_w[i]), mem_n, ca_wq[i], ca_wkv[i], ca_wo[i])
        x = x + conv_ffn(rmsnorm(x, norm_ffn_w[i]), ffn_w_up[i], ffn_conv_w[i], ffn_w_down[i])
    return rmsnorm(x, final_norm_w)


def setup_inputs(seed=0):
    out = dict(first_inputs(seed))
    for name, value in second_inputs(seed + 1).items():
        if name != "x":
            out[name + "_2"] = value
    return out


def reference(
    x, rel_bias, attn_norm, w_in, fox_f_bias, fox_q_gain, fox_k_gain, conv_w, mlstm_i_bias,
    mlstm_f_bias, mlstm_h_gain, swa_q_gain, swa_k_gain, swa_sinks, w_fox_out, w_conv_out,
    w_mlstm_out, w_swa_out, w_merge_out, ffn_norm, w_gate, w_up, w_down, mem_2, mem_norm_w_2,
    final_norm_w_2, norm_mix_w_2, norm_cross_w_2, norm_ffn_w_2, ca_wq_2, ca_wkv_2, ca_wo_2,
    ffn_w_up_2, ffn_conv_w_2, ffn_w_down_2, nsa_w_in_2, nsa_pe_k_2, nsa_pe_v_2, nsa_ck_w1_2,
    nsa_ck_w2_2, nsa_cv_w1_2, nsa_cv_w2_2, nsa_w_out_2, gdn_w_in_2, gdn_conv_w_2, gdn_a_log_2,
    gdn_dt_bias_2, gdn_norm_w_2, gdn_w_out_2, diff_w_in_2, diff_lq1_2, diff_lk1_2, diff_lq2_2,
    diff_lk2_2, diff_subln_w_2, diff_w_out_2,
):
    x = first_block(
        x, rel_bias, attn_norm, w_in, fox_f_bias, fox_q_gain, fox_k_gain, conv_w, mlstm_i_bias,
        mlstm_f_bias, mlstm_h_gain, swa_q_gain, swa_k_gain, swa_sinks, w_fox_out, w_conv_out,
        w_mlstm_out, w_swa_out, w_merge_out, ffn_norm, w_gate, w_up, w_down,
    )
    return second_block(
        x, mem_2, mem_norm_w_2, final_norm_w_2, norm_mix_w_2, norm_cross_w_2, norm_ffn_w_2,
        ca_wq_2, ca_wkv_2, ca_wo_2, ffn_w_up_2, ffn_conv_w_2, ffn_w_down_2, nsa_w_in_2,
        nsa_pe_k_2, nsa_pe_v_2, nsa_ck_w1_2, nsa_ck_w2_2, nsa_cv_w1_2, nsa_cv_w2_2, nsa_w_out_2,
        gdn_w_in_2, gdn_conv_w_2, gdn_a_log_2, gdn_dt_bias_2, gdn_norm_w_2, gdn_w_out_2,
        diff_w_in_2, diff_lq1_2, diff_lk1_2, diff_lq2_2, diff_lk2_2, diff_subln_w_2,
        diff_w_out_2,
    )


_drawn_inputs = setup_inputs


def setup_inputs(seed=0):
    import zlib

    import numpy as np

    out = dict(_drawn_inputs(seed))
    spreads = {}
    factors = {'fox_q_gain': 6.518,
     'fox_k_gain': 6.408,
     'mlstm_i_bias': 64.0,
     'mlstm_h_gain': 3.758,
     'swa_q_gain': 8.0,
     'swa_k_gain': 8.0,
     'swa_sinks': 8.0,
     'mem_norm_w_2': 8.0,
     'final_norm_w_2': 8.124,
     'norm_mix_w_2': 8.0,
     'norm_cross_w_2': 8.0,
     'norm_ffn_w_2': 4.981,
     'nsa_pe_k_2': 8.0,
     'nsa_pe_v_2': 8.0}
    for name, (base, spread) in spreads.items():
        noise = np.random.default_rng([zlib.crc32(name.encode()), seed]).standard_normal(out[name].shape)
        drawn = base * np.exp(spread * noise) if base else spread * noise
        out[name] = __import__('jax').numpy.asarray(drawn.astype(out[name].dtype))
    for name, factor in factors.items():
        out[name] = (out[name] * factor).astype(out[name].dtype)
    return out
```

```python
from contextlib import ExitStack

import numpy as np

import concourse.bass as bass
from concourse import mybir

F32 = mybir.dt.float32
ALU = mybir.AluOpType
ACT = mybir.ActivationFunctionType
AXX = mybir.AxisListType.X

P = 128
S = 512
D = 1024
NT = S // P
ND = D // P
BANK = 512
EPS = 1e-6
NEG = -1e30
HD = 64

FQ, FK, FV, FF = 0, 256, 512, 768
CU, CB, CC = 772, 1028, 1284
MQ, MK, MV, MI, MF, MO = 1540, 1796, 2052, 2308, 2312, 2316
SQ, SK, SV, GATES = 2572, 3084, 3212, 3340
FOX_H, ML_H, SWA_H = 4, 4, 8
N_BRANCH = 4
DFF = 2816
NF = DFF // P
BUCKETS = 32

NQ, NKC, NVC, NKS, NVS, NKW, NVW, NGL = 0, 1024, 1280, 1536, 1792, 2048, 2304, 2560
NSA_H, NSA_G, HPG = 16, 4, 4
CMP_N = 31
CMP_HID = 256
MEM = 256
CA_H, CA_D = 4, 256

RING = 12

C_ID, C_ANTI, C_MQ, C_MT = 0, P, 2 * P, 3 * P
C_CMP = 4 * P
C_VALID = C_CMP + NT * 32
C_SEL = C_VALID + NT
C_OH = C_SEL + 4 * P
C_ONE = C_OH + 384
C_END = C_ONE + P

(K_ANORM, K_FNORM, K_MIX, K_CROSS, K_FFN2, K_MEM) = (8 * i for i in range(6))
K_FQ, K_FK, K_SQ, K_SK = 48, 49, 50, 51
K_CONV = 52
K_BIAS = 58
K_CONV2 = 60
K_PEK = K_CONV2 + 66
K_PEV = K_PEK + 16
K_END = K_PEV + 16


def shape_constants():
    c = np.zeros((P, C_END), np.float32)
    i = np.arange(P)
    c[:, C_ID:C_ID + P] = np.eye(P)
    c[:, C_ANTI:C_ANTI + P] = np.eye(P)[::-1]
    c[:, C_MQ:C_MQ + P] = np.where(i[None, :] <= i[:, None], 0, NEG)
    c[:, C_MT:C_MT + P] = np.where(i[:, None] <= i[None, :], 0, NEG)
    n = np.arange(32)
    for t in range(NT):
        tok = t * P + i
        seen = (16 * n[None, :] + 31 <= tok[:, None]) & (n[None, :] < CMP_N)
        c[:, C_CMP + 32 * t:C_CMP + 32 * t + 32] = np.where(seen, 0, NEG)
        c[:, C_VALID + t] = tok >= 31
    for h in range(4):
        c[h, C_SEL + h * P:C_SEL + (h + 1) * P] = 1
        c[32 + h, C_SEL + h * P:C_SEL + (h + 1) * P] = 1
    dist = 255 - np.arange(384)
    n1 = np.maximum(dist, 1).astype(np.float32)
    large = 16 + (np.log(n1 / np.float32(16)) / np.float32(np.log(8.0)) * np.float32(16)).astype(np.int32)
    bucket = np.where(dist < 16, dist, np.minimum(large, BUCKETS - 1))
    for u in range(384):
        if 0 <= dist[u] < 128:
            c[bucket[u], C_OH + u] = 1
        else:
            c[BUCKETS, C_OH + u] = NEG
    c[:, C_ONE:C_ONE + P] = 1
    return c


def pack_params(a):
    k = np.zeros((P, K_END), np.float32)

    def tiles(v):
        return np.asarray(v).reshape(-1, P).T

    for at, name in ((K_ANORM, 'attn_norm'), (K_FNORM, 'ffn_norm'), (K_MIX, 'norm_mix_w_2'),
                     (K_CROSS, 'norm_cross_w_2'), (K_FFN2, 'norm_ffn_w_2'), (K_MEM, 'mem_norm_w_2')):
        k[:, at:at + 8] = tiles(a[name])
    for at, name in ((K_FQ, 'fox_q_gain'), (K_FK, 'fox_k_gain'), (K_SQ, 'swa_q_gain'), (K_SK, 'swa_k_gain')):
        k[0:HD, at] = a[name][0]
        k[HD:P, at] = a[name][0]
    k[:, K_CONV:K_CONV + 6] = tiles(a['conv_w'])
    k[0:4, K_BIAS] = a['fox_f_bias'][0]
    k[32:36, K_BIAS] = a['mlstm_i_bias'][0]
    k[64:68, K_BIAS] = a['mlstm_f_bias'][0]
    k[:, K_CONV2:K_CONV2 + 66] = tiles(a['ffn_conv_w_2'])
    k[:, K_PEK:K_PEK + 16] = tiles(a['nsa_pe_k_2'])
    k[:, K_PEV:K_PEV + 16] = tiles(a['nsa_pe_v_2'])
    return k


def pair_heads(weight, at, blocks, per):
    m = weight.copy()
    n = blocks * 2 * per * HD
    q = m[:, at:at + n].reshape(-1, blocks, 2, per, HD)
    m[:, at:at + n] = q.transpose(0, 1, 3, 2, 4).reshape(-1, n)
    return m


class Chain:

    def __init__(self, eng, sem):
        self.eng, self.sem, self.n = eng, sem, 0

    def __call__(self, ins):
        self.n += 1
        ins.then_inc(self.sem, 1)
        self.eng.wait_ge(self.sem, self.n)


def build(nc, w, out):
    ctx = ExitStack()
    with ctx:
        def sb(name, shape, scope=ctx, dt=F32):
            return scope.enter_context(nc.sbuf_tensor(name, list(shape), dt))

        stage_sems = []

        def sem(name, scope=ctx):
            if scope is ctx:
                return ctx.enter_context(nc.semaphore(name))
            stage_sems.append(nc.alloc_semaphore(name))
            return stage_sems[-1]

        def clear_stage():
            with nc.Block() as block:
                @block.gpsimd
                def _(g):
                    nc.clear_and_free_semaphores(list(stage_sems))
            stage_sems.clear()

        bank = [ctx.enter_context(nc.psum_tensor(f"bank{i}", [P, BANK], F32)) for i in range(8)]
        const = sb("const", [P, C_END])
        par = sb("par", [P, K_END])
        x = sb("x", [P, NT, D])
        hT = sb("hT", [P, ND, S])
        ring = sb("ring", [P, RING, 1024])
        stat = sb("stat", [P, 160])

        ident = const[:, C_ID:C_ID + P]
        anti = const[:, C_ANTI:C_ANTI + P]
        mask_q = const[:, C_MQ:C_MQ + P]
        mask_t = const[:, C_MT:C_MT + P]
        eps = stat[:, 150:151]

        w_ready = [sem(f"w_ready{i}") for i in range(RING)]
        w_used = sem("w_used")
        stored = sem("stored")
        plan = []

        def cols(name, c0, n=P):
            m = w[name]
            per = 1024 // n
            kt = m.shape[0] // P
            for k0 in range(0, kt, per):
                k = min(per, kt - k0)
                src = m[k0 * P:(k0 + k) * P, c0:c0 + n].rearrange("(k p) c -> p k c", p=P)
                plan.append((name, src, k, n))

        def weight_plan():
            for c0, n in TOKEN_CHUNKS_A:
                cols('w_in', c0, n)
            for c0 in FEATURE_TILES_A:
                cols('w_in', c0)
            for d in range(ND):
                for b in range(N_BRANCH):
                    cols('w_in', GATES + b * D + d * P)
                for b in range(N_BRANCH):
                    cols(('w_fox_out', 'w_conv_out', 'w_mlstm_out', 'w_swa_out')[b], d * P)
            for half in range(2):
                cols('w_merge_out', half * BANK, BANK)
            for f in range(NF):
                cols('w_gate', f * P)
                cols('w_up', f * P)
            for half in range(2):
                cols('w_down', half * BANK, BANK)
            for half in range(2):
                cols('nsa_w_in_2', half * BANK, BANK)
            for c0 in FEATURE_TILES_N:
                cols('nsa_w_in_2', c0)
            for c0, n in TOKEN_CHUNKS_N:
                cols('nsa_w_in_2', c0, n)
            cols('nsa_ck_w1_2', 0, CMP_HID)
            cols('nsa_cv_w1_2', 0, CMP_HID)
            for half in range(2):
                cols('nsa_w_out_2', half * BANK, BANK)
            for d in range(ND):
                cols('ca_wkv_2', d * P)
            for half in range(2):
                cols('ca_wkv_2', D + half * BANK, BANK)
            for d in range(ND):
                cols('ca_wq_2', d * P)
            for half in range(2):
                cols('ca_wo_2', half * BANK, BANK)
            for f in range(NF):
                cols('ffn_w_up_2', f * P)
                cols('ffn_w_up_2', DFF + f * P)
            for half in range(2):
                cols('ffn_w_down_2', half * BANK, BANK)

        TOKEN_CHUNKS_A = [(FQ, 512), (FV, 256), (MV, 256), (MO, 256), (SQ, 512), (SK, 256)]
        FEATURE_TILES_A = [c + P * i for c in (MQ, MK, CU, CC, CB) for i in range(2)]
        FEATURE_TILES_N = [c + P * i for c in (NKC, NVC, NKS, NKW) for i in range(2)]
        TOKEN_CHUNKS_N = [(NVS, 256), (NVW, 304)]
        weight_plan()
        state = {"issued": 0, "used": 0}

        def slot_of(n, k, width):
            return ring[:, n % RING, 0:k * width].rearrange("p (k c) -> p k c", c=width)

        def load_weights(sp, through):
            while state["issued"] < min(through + RING, len(plan)):
                n = state["issued"]
                _, src, k, width = plan[n]
                if n >= RING:
                    sp.wait_ge(w_used, n - RING + 1)
                sp.dma_start(slot_of(n, k, width), src).then_inc(w_ready[n % RING], 16)
                state["issued"] += 1

        def tile_for(pe, n, name):
            assert plan[n][0] == name, (plan[n][0], name, n)
            pe.wait_ge(w_ready[n % RING], 16 * (n // RING + 1))
            return slot_of(n, plan[n][2], plan[n][3])

        def copy(vector, dst, src):
            if vector:
                return nc.vector.tensor_copy(dst, src)
            return nc.scalar.activation(dst, src, ACT.Copy)

        def scaled(vector, dst, src, by):
            if vector:
                return nc.vector.tensor_scalar(dst, src, by, None, ALU.mult)
            return nc.scalar.activation(dst, src, ACT.Copy, scale=by)

        def load_stage():
            with nc.Block() as block, ExitStack() as sc:
                loaded = sem("loaded", sc)

                @block.sync
                def _(sp):
                    sp.dma_start(x[:, :, :], w['x'].rearrange("o (t p) d -> p (o t) d", p=P)).then_inc(loaded, 16)
                    sp.dma_start(const[:, :], w['const']).then_inc(loaded, 16)
                    sp.dma_start(par[:, :], w['par']).then_inc(loaded, 16)
                    load_weights(sp, 0)
                    sp.wait_ge(loaded, 48)

                @block.vector
                def _(v):
                    nc.vector.memset(eps, EPS)

        def norm_stage(name, src, tiles, gain, dst, scope_bytes=None):
            with ExitStack() as sc:
                h = sb(f"{name}_h", [P, tiles, D], sc)
                sq = sb(f"{name}_sq", [P, D], sc)
                squared, rooted, scaled_h = (sem(f"{name}_{s}", sc) for s in ("squared", "rooted", "scaled"))
                turned, out_v, out_a, chain = (sem(f"{name}_{s}", sc) for s in ("turned", "outv", "outa", "chain"))
                with nc.Block() as block:
                    @block.scalar
                    def _(a):
                        link = Chain(a, squared)
                        for t in range(tiles):
                            link(nc.scalar.activation(sq[:, :], src[:, t, :], ACT.Square, accum_out=stat[:, t:t + 1]))
                        nc.scalar.activation(stat[:, 8:8 + tiles], stat[:, 0:tiles], ACT.Sqrt, bias=eps,
                                             scale=1.0 / D).then_inc(rooted, 1)
                        for d in range(1, ND, 2):
                            a.wait_ge(turned, d + 1)
                            scaled(False, dst[:, d, 0:tiles * P], bank[d][:, 0:tiles * P],
                                   gain[:, d:d + 1]).then_inc(out_a, 1)

                    @block.vector
                    def _(v):
                        v.wait_ge(rooted, 1)
                        nc.vector.reciprocal(stat[:, 16:16 + tiles], stat[:, 8:8 + tiles]).then_inc(chain, 1)
                        v.wait_ge(chain, 1)
                        for t in range(tiles):
                            scaled(True, h[:, t, :], src[:, t, :], stat[:, 16 + t:17 + t]).then_inc(scaled_h, 1)
                        for d in range(0, ND, 2):
                            v.wait_ge(turned, d + 1)
                            scaled(True, dst[:, d, 0:tiles * P], bank[d][:, 0:tiles * P],
                                   gain[:, d:d + 1]).then_inc(out_v, 1)

                    @block.tensor
                    def _(pe):
                        pe.wait_ge(scaled_h, tiles)
                        for d in range(ND):
                            for t in range(tiles):
                                mm = nc.tensor.transpose(bank[d][:, t * P:(t + 1) * P],
                                                         h[:, t, d * P:(d + 1) * P], ident)
                            mm.then_inc(turned, 1)

                    @block.sync
                    def _(sp):
                        load_weights(sp, state["used"])

        def token_stage(name, actT, kt, chunks, evac, engines, tiles=NT):
            n_v = sum(engines[:tiles])
            n_a = tiles - n_v
            slots, n = [], state["used"]
            for wname, width in chunks:
                per = -(-kt // (1024 // width))
                slots.append((n, per, width, wname))
                n += per
            with ExitStack() as sc:
                out_v, out_a = sem(f"{name}_outv", sc), sem(f"{name}_outa", sc)
                with nc.Block() as block:
                    @block.tensor
                    def _(pe):
                        for c, (n0, per, width, wname) in enumerate(slots):
                            base = 4 * (c % 2)
                            if c >= 2:
                                if n_v:
                                    pe.wait_ge(out_v, (c - 1) * n_v)
                                if n_a:
                                    pe.wait_ge(out_a, (c - 1) * n_a)
                            k = 0
                            for s in range(per):
                                slot = tile_for(pe, n0 + s, wname)
                                for kk in range(plan[n0 + s][2]):
                                    for t in range(tiles):
                                        mm = nc.tensor.matmul(bank[base + t][:, 0:width],
                                                              lhsT=actT[:, k, t * P:(t + 1) * P],
                                                              rhs=slot[:, kk, :],
                                                              start=(k == 0), stop=(k == kt - 1))
                                    k += 1
                                mm.then_inc(w_used, 1)
                            assert k == kt

                    def empty(eng, vector):
                        for c, (n0, per, width, _) in enumerate(slots):
                            eng.wait_ge(w_used, n0 + per)
                            for t in range(tiles):
                                if engines[t] == vector:
                                    evac(c, t, bank[4 * (c % 2) + t][:, 0:width], vector)\
                                        .then_inc(out_v if vector else out_a, 1)

                    @block.vector
                    def _(v):
                        empty(v, True)

                    @block.scalar
                    def _(a):
                        if n_a:
                            empty(a, False)

                    @block.sync
                    def _(sp):
                        load_weights(sp, n)
            state["used"] = n

        def feature_stage(name, actT, ncols, tiles, evac, kt=ND):
            n0 = state["used"]
            with ExitStack() as sc:
                out_e = [sem(f"{name}_outv", sc), sem(f"{name}_outa", sc)]
                with nc.Block() as block:
                    @block.tensor
                    def _(pe):
                        for i, wname in enumerate(tiles):
                            if i >= 8:
                                pe.wait_ge(out_e[i % 2], (i - 8) // 2 + 1)
                            slot = tile_for(pe, n0 + i, wname)
                            for k in range(kt):
                                mm = nc.tensor.matmul(bank[i % 8][:, 0:ncols], lhsT=slot[:, k, :],
                                                      rhs=actT[:, k, 0:ncols], start=(k == 0), stop=(k == kt - 1))
                            mm.then_inc(w_used, 1)

                    def empty(eng, parity):
                        for i in range(parity, len(tiles), 2):
                            eng.wait_ge(w_used, n0 + i + 1)
                            evac(i, bank[i % 8][:, 0:ncols], parity == 0).then_inc(out_e[parity], 1)

                    @block.vector
                    def _(v):
                        empty(v, 0)

                    @block.scalar
                    def _(a):
                        empty(a, 1)

                    @block.sync
                    def _(sp):
                        load_weights(sp, n0 + len(tiles))
            state["used"] = n0 + len(tiles)

        def turn_stage(name, blocks):
            with ExitStack() as sc:
                turned = sem(f"{name}_turned", sc)
                out_e = [sem(f"{name}_outv", sc), sem(f"{name}_outa", sc)]
                with nc.Block() as block:
                    @block.tensor
                    def _(pe):
                        for i, (src, _, _) in enumerate(blocks):
                            if i >= 8:
                                pe.wait_ge(out_e[i % 2], (i - 8) // 2 + 1)
                            for t in range(NT):
                                mm = nc.tensor.transpose(bank[i % 8][:, t * P:(t + 1) * P], src(t), ident)
                            mm.then_inc(turned, 1)

                    def empty(eng, parity):
                        for i in range(parity, len(blocks), 2):
                            _, dst, by = blocks[i]
                            eng.wait_ge(turned, i + 1)
                            ins = copy(parity == 0, dst, bank[i % 8][:, :]) if by is None else \
                                scaled(parity == 0, dst, bank[i % 8][:, :], by)
                            ins.then_inc(out_e[parity], 1)

                    @block.vector
                    def _(v):
                        empty(v, 0)

                    @block.scalar
                    def _(a):
                        empty(a, 1)

        def attention_stage(name, units, scratch):
            prob, probT = scratch
            n = len(units)
            with ExitStack() as sc:
                scored, peaked, exped, turned, summed, emptied, chain = (
                    sem(f"{name}_{s}", sc)
                    for s in ("scored", "peaked", "exped", "turned", "summed", "emptied", "chain"))
                copied = [sem(f"{name}_copied{i}", sc) for i in range(2)]
                npeak = [stat[:, 20 + i:21 + i] for i in range(3)]
                total = [stat[:, 24 + i:25 + i] for i in range(4)]

                with nc.Block() as block:
                    @block.tensor
                    def _(pe):
                        for s in range(n + 2):
                            if s < n:
                                if s >= 3:
                                    pe.wait_ge(exped, s - 2)
                                sc_ = units[s]["scores"]
                                for j, (c0, cn, lhsT, rhs) in enumerate(sc_):
                                    mm = nc.tensor.matmul(bank[s % 3][:, c0:c0 + cn], lhsT=lhsT, rhs=rhs,
                                                          start=(j == 0), stop=(j == len(sc_) - 1))
                                mm.then_inc(scored, 1)
                            u = s - 1
                            if 0 <= u < n:
                                pe.wait_ge(exped, u + 1)
                                if u >= 2:
                                    pe.wait_ge(copied[u % 2], u // 2)
                                for j, (c0, _) in enumerate(units[u]["keys"]):
                                    mm = nc.tensor.transpose(bank[3 + u % 2][:, j * P:(j + 1) * P],
                                                             prob[:, u % 3, c0:c0 + P], ident)
                                mm.then_inc(turned, 1)
                            u = s - 2
                            if u >= 0:
                                pe.wait_ge(copied[u % 2], u // 2 + 1)
                                if u >= 2:
                                    pe.wait_ge(emptied, u - 1)
                                keys = units[u]["keys"]
                                for j, (_, val) in enumerate(keys):
                                    mm = nc.tensor.matmul(bank[5 + u % 2][:, 0:val.shape[-1]],
                                                          lhsT=probT[:, u % 2, j * P:(j + 1) * P], rhs=val,
                                                          start=(j == 0), stop=(j == len(keys) - 1))
                                mm.then_inc(summed, 1)

                    def copy_turned(eng, u):
                        eng.wait_ge(turned, u + 1)
                        if u >= 2:
                            eng.wait_ge(summed, u - 1)
                        k = len(units[u]["keys"]) * P
                        copy(u % 2 == 0, probT[:, u % 2, 0:k], bank[3 + u % 2][:, 0:k]).then_inc(copied[u % 2], 1)

                    @block.vector
                    def _(v):
                        link = Chain(v, chain)
                        for s in range(n + 2):
                            if s < n:
                                v.wait_ge(scored, s + 1)
                                if s >= 3:
                                    v.wait_ge(exped, s - 2)
                                nc.vector.tensor_reduce(npeak[s % 3], bank[s % 3][:, 0:units[s]["width"]], AXX,
                                                        ALU.max, negate=True).then_inc(peaked, 1)
                            if 0 <= s - 1 < n and (s - 1) % 2 == 0:
                                copy_turned(v, s - 1)
                            u = s - 2
                            if u >= 0:
                                v.wait_ge(summed, u + 1)
                                units[u]["finish"](link, u, bank[5 + u % 2], total[u % 4]).then_inc(emptied, 1)

                    @block.scalar
                    def _(a):
                        for s in range(n + 1):
                            if s < n:
                                a.wait_ge(peaked, s + 1)
                                if s >= 3:
                                    a.wait_ge(turned, s - 2)
                                if s >= 4:
                                    a.wait_ge(emptied, s - 3)
                                wd = units[s]["width"]
                                nc.scalar.activation(prob[:, s % 3, 0:wd], bank[s % 3][:, 0:wd], ACT.Exp,
                                                     bias=npeak[s % 3], accum_out=total[s % 4]).then_inc(exped, 1)
                            if s >= 1 and (s - 1) % 2 == 1:
                                copy_turned(a, s - 1)

        recip = [stat[:, 30 + i:31 + i] for i in range(2)]
        coef = [stat[:, 32 + i:33 + i] for i in range(2)]

        def finish_plain(dst):
            def f(link, u, ps, total):
                link(nc.vector.reciprocal(recip[u % 2], total))
                return scaled(True, dst, ps[:, 0:dst.shape[-1]], recip[u % 2])
            return f

        def finish_gated(dst, gate):
            def f(link, u, ps, total):
                link(nc.vector.reciprocal(recip[u % 2], total))
                link(nc.vector.tensor_tensor(coef[u % 2], recip[u % 2], gate, ALU.mult))
                return nc.vector.scalar_tensor_tensor(dst, ps[:, 0:HD], coef[u % 2], dst, ALU.mult, ALU.add)
            return f

        def residual_add(c, t, ps, vector):
            dst = x[:, t, c * BANK:(c + 1) * BANK]
            return nc.vector.tensor_tensor(dst, dst, ps, ALU.add)

        load_stage()
        norm_stage("anorm", x, NT, par[:, K_ANORM:], hT)

        mixers = ctx.enter_context(ExitStack())
        yT = sb("yT", [P, 10, S], mixers)
        yt = sb("yt", [P, NT, D], mixers)
        inner = ExitStack()
        tokv = sb("tokv", [P, NT, 896], inner)
        qkT = sb("qkT", [P, 13, S], inner)
        toep = sb("toep", [P, SWA_H, 256], inner)
        rows = sb("rows", [P, 2, S], inner)
        mcol = sb("mcol", [P, 2, NT, ML_H], inner)
        gain_h = sb("gain_h", [P, 256], inner)
        sinks = sb("sinks", [1, SWA_H], inner)

        normed = ExitStack()
        tokqk = sb("tokqk", [P, NT, 1152], normed)
        pieces_a = [[(0, 512, tokqk, 0)], [(0, 256, tokv, 0)], [(0, 256, tokv, 256)], [(0, 256, tokv, 512)],
                    [(0, 512, tokqk, 512)], [(0, 128, tokqk, 1024), (128, 128, tokv, 768)]]

        def evac_pieces(pieces):
            def f(c, t, ps, vector):
                for s0, wd, dst, d0 in pieces[c]:
                    ins = copy(vector, dst[:, t, d0:d0 + wd], ps[:, s0:s0 + wd])
                return ins
            return f

        half = [True, False, True, False]
        token_stage("projA", hT, ND, [('w_in', n) for _, n in TOKEN_CHUNKS_A], evac_pieces(pieces_a), half)

        def qk_norm_stage():
            nh = NT * 18
            flat = tokqk[:, :, :].rearrange("p t (h d) -> p (t h) d", d=HD)
            sqr = yT[:, 0:9, :].rearrange("p a b -> p (a b)").rearrange("p (h d) -> p h d", d=HD)
            with ExitStack() as sc:
                ssum, rooted, chain = sem("qkn_sum", sc), sem("qkn_root", sc), sem("qkn_chain", sc)
                with nc.Block() as block:
                    @block.vector
                    def _(v):
                        link = Chain(v, chain)
                        link(nc.vector.tensor_tensor(sqr, flat, flat, ALU.mult))
                        nc.vector.tensor_reduce(stat[:, 0:nh], sqr, AXX, ALU.add).then_inc(ssum, 1)
                        nc.vector.tensor_scalar(stat[:, 148:149], par[:, K_FQ:K_FQ + 1], HD ** -0.5, None, ALU.mult)
                        nc.vector.tensor_scalar(stat[:, 149:150], par[:, K_SQ:K_SQ + 1], HD ** -0.5, None, ALU.mult)
                        v.wait_ge(rooted, 1)
                        link(nc.vector.reciprocal(stat[:, 0:nh], stat[:, 72:72 + nh]))
                        by = stat[:, 0:nh].unsqueeze(2).to_broadcast([P, nh, HD])
                        nc.vector.tensor_tensor(flat, flat, by, ALU.mult)

                    @block.scalar
                    def _(a):
                        a.wait_ge(ssum, 1)
                        nc.scalar.activation(stat[:, 72:72 + nh], stat[:, 0:nh], ACT.Sqrt, bias=eps,
                                             scale=1.0 / HD).then_inc(rooted, 1)

        qk_norm_stage()

        def tok(tile, c0):
            return lambda t: tile[:, t, c0:c0 + P]

        turn_stage("qkT", [(tok(tokqk, 0), qkT[:, 0, :], stat[:, 148:149]), (tok(tokqk, P), qkT[:, 1, :], stat[:, 148:149]),
                           (tok(tokqk, 256), qkT[:, 2, :], par[:, K_FK:K_FK + 1]),
                           (tok(tokqk, 384), qkT[:, 3, :], par[:, K_FK:K_FK + 1])]
                   + [(tok(tokqk, 512 + i * P), qkT[:, 8 + i, :], stat[:, 149:150]) for i in range(4)]
                   + [(tok(tokqk, 1024), qkT[:, 12, :], par[:, K_SK:K_SK + 1])])
        normed.close()

        conv = ExitStack()
        cx = sb("cx", [P, 6, 514], conv)
        cy = sb("cy", [P, 2, S], conv)
        wsm = sb("wsm", [P, ND, 96], conv)
        rb = sb("rb", [P, 3, S], conv)
        relT = sb("relT", [BUCKETS + 1, SWA_H], conv)
        biasrow = sb("biasrow", [SWA_H, 384], conv)

        def evac_feat(i, ps, vector):
            if i < 2:
                return scaled(vector, qkT[:, 4 + i, :], ps, HD ** -0.5) if vector else \
                    nc.scalar.activation(qkT[:, 4 + i, :], ps, ACT.Copy, scale=HD ** -0.5)
            if i < 4:
                return copy(vector, qkT[:, 4 + i, :], ps)
            return copy(vector, cx[:, i - 4, 2:514], ps)

        feature_stage("projAT", hT, S, ['w_in'] * 10, evac_feat)

        scratch_bias = w['bias_rows']

        def small_stage():
            with ExitStack() as sc:
                names = ("zeroed", "cols_in", "misc", "logits", "logits_in", "absed", "exped", "logged", "bias_mm",
                         "bias_row", "bias_out", "toep_in", "chain", "scanned", "turned", "pool", "achain")
                s = {k: sem(f"small_{k}", sc) for k in names}
                with nc.Block() as block:
                    @block.gpsimd
                    def _(g):
                        nc.gpsimd.memset(wsm[:, :, :], 0.0).then_inc(s["zeroed"], 1)
                        g.wait_ge(s["zeroed"], 1)
                        nc.gpsimd.memset(relT[BUCKETS:BUCKETS + 1, :], 1.0).then_inc(s["zeroed"], 1)

                    @block.sync
                    def _(sp):
                        sp.wait_ge(s["zeroed"], 2)
                        wv = w['w_in'].rearrange("(k p) c -> p k c", p=P)
                        for at, c0 in ((0, FF), (32, MI), (64, MF)):
                            sp.dma_start(wsm[:, :, at:at + 4], wv[:, :, c0:c0 + 4]).then_inc(s["cols_in"], 16)
                        sp.dma_start(relT[0:BUCKETS, :], w['rel_bias']).then_inc(s["misc"], 16)
                        sp.dma_start(gain_h[:, :], w['mlstm_h_gain'].to_broadcast([P, 256])).then_inc(s["misc"], 16)
                        sp.dma_start(sinks[:, :], w['swa_sinks']).then_inc(s["misc"], 16)
                        sp.wait_ge(s["bias_row"], 1)
                        sp.dma_start(scratch_bias, biasrow[:, :]).then_inc(s["bias_out"], 16)
                        sp.wait_ge(s["bias_out"], 16)
                        skew = bass.AP(tensor=scratch_bias.tensor, offset=scratch_bias.offset,
                                       ap=[[1, P], [384, SWA_H], [1, 256]])
                        sp.dma_start(toep[:, :, :], skew).then_inc(s["toep_in"], 16)
                        sp.wait_ge(s["toep_in"], 16)
                        sp.wait_ge(s["misc"], 48)

                    @block.tensor
                    def _(pe):
                        pe.wait_ge(s["cols_in"], 48)
                        for k in range(ND):
                            mm = nc.tensor.matmul(bank[0][0:96, :], lhsT=wsm[:, k, :], rhs=hT[:, k, :],
                                                  start=(k == 0), stop=(k == ND - 1))
                        mm.then_inc(s["logits"], 1)
                        pe.wait_ge(s["misc"], 48)
                        pe.wait_ge(s["zeroed"], 2)
                        nc.tensor.matmul(bank[1][0:SWA_H, 0:384], lhsT=relT[:, :],
                                         rhs=const[0:BUCKETS + 1, C_OH:C_OH + 384],
                                         start=True, stop=True).then_inc(s["bias_mm"], 1)
                        pe.wait_ge(s["scanned"], 1)
                        for i in range(2):
                            for t in range(NT):
                                mm = nc.tensor.transpose(bank[2 + i][:, t * 4:t * 4 + 4],
                                                         rb[32:36, i, t * P:(t + 1) * P],
                                                         const[32:36, C_ID + 32:C_ID + 36])
                        mm.then_inc(s["turned"], 1)

                    @block.scalar
                    def _(a):
                        a.wait_ge(s["logits"], 1)
                        nc.scalar.activation(rb[0:96, 0, :], bank[0][0:96, :], ACT.Identity,
                                             bias=par[0:96, K_BIAS:K_BIAS + 1]).then_inc(s["logits_in"], 1)
                        link = Chain(a, s["achain"])
                        a.wait_ge(s["logits_in"], 1)
                        link(nc.scalar.activation(rb[0:96, 1, :], rb[0:96, 0, :], ACT.Abs))
                        link(nc.scalar.activation(rb[0:96, 1, :], rb[0:96, 1, :], ACT.Exp, scale=-1.0))
                        nc.scalar.activation(rb[0:96, 2, :], rb[0:96, 1, :], ACT.Ln, bias=1.0).then_inc(s["logged"], 1)
                        a.wait_ge(s["bias_mm"], 1)
                        nc.scalar.activation(biasrow[:, :], bank[1][0:SWA_H, 0:384], ACT.Copy).then_inc(s["bias_row"], 1)

                    @block.vector
                    def _(v):
                        link = Chain(v, s["chain"])
                        nc.vector.memset(cx[:, 2:4, 0:2], 0.0)
                        link(nc.vector.tensor_tensor(cx[:, 2:4, 2:514], cx[:, 2:4, 2:514], cx[:, 0:2, 2:514], ALU.mult))
                        for i in range(2):
                            z = cx[:, 2 + i, :]
                            tap = [par[:, K_CONV + 2 * j + i:K_CONV + 2 * j + i + 1] for j in range(3)]
                            link(nc.vector.tensor_scalar(cy[:, i, :], z[:, 2:514], tap[2], None, ALU.mult))
                            link(nc.vector.scalar_tensor_tensor(cy[:, i, :], z[:, 1:513], tap[1], cy[:, i, :], ALU.mult, ALU.add))
                            link(nc.vector.scalar_tensor_tensor(cy[:, i, :], z[:, 0:512], tap[0], cy[:, i, :], ALU.mult, ALU.add))
                            nc.vector.tensor_tensor(yT[:, 2 + i, :], cy[:, i, :], cx[:, 4 + i, 2:514], ALU.mult)
                        v.wait_ge(s["logged"], 1)
                        link(nc.vector.tensor_scalar(rb[0:96, 1, :], rb[0:96, 0, :], 0.0, None, ALU.min))
                        link(nc.vector.tensor_tensor(rb[0:96, 1, :], rb[0:96, 1, :], rb[0:96, 2, :], ALU.subtract))
                        link(nc.vector.tensor_tensor_scan(rb[0:96, 2, :], rb[0:96, 1, :], rb[0:96, 1, :], 0.0,
                                                          ALU.add, ALU.bypass))
                        nc.vector.tensor_scalar(rows[0:4, 0, :], rb[0:4, 2, :], -1.0, None, ALU.mult)
                        link(nc.vector.tensor_copy(rb[32:36, 1, :], rb[64:68, 2, :]))
                        link(nc.vector.tensor_tensor(rb[32:36, 0, :], rb[32:36, 0, :], rb[32:36, 1, :], ALU.subtract))
                        link(nc.vector.tensor_tensor_scan(rb[32:36, 2, :], rb[32:36, 0, :], rb[32:36, 0, :], 0.0,
                                                          ALU.max, ALU.bypass))
                        link(nc.vector.tensor_scalar(rows[32:36, 1, :], rb[32:36, 2, :], -1.0, None, ALU.mult))
                        nc.vector.tensor_tensor(rb[32:36, 1, :], rows[32:36, 1, :], rb[32:36, 1, :],
                                                ALU.subtract).then_inc(s["scanned"], 1)
                        v.wait_ge(s["turned"], 1)
                        for i in range(2):
                            nc.vector.tensor_copy(mcol[:, i, :, :], bank[2 + i][:, 0:16].rearrange("p (t h) -> p t h", h=4))

        small_stage()
        conv.close()

        attn = ExitStack()
        prob = sb("prob", [P, 3, 514], attn)
        probT = sb("probT", [P, 2, S], attn)
        scratch = (prob, probT)

        def part(h):
            return slice(HD * (h % 2), HD * (h % 2) + HD)

        def q_tile(t):
            return slice(t * P, (t + 1) * P)

        fox_units = []
        for t in range(NT):
            for h in range(FOX_H):
                wd = (t + 1) * P
                fox_units.append({
                    "width": wd,
                    "scores": [(0, wd, qkT[part(h), h // 2, q_tile(t)], qkT[part(h), 2 + h // 2, 0:wd]),
                               (0, wd, const[0:4, C_SEL + h * P:C_SEL + (h + 1) * P], rows[0:4, 0, 0:wd]),
                               (t * P, P, ident, mask_q)],
                    "keys": [(j * P, tokv[:, j, h * HD:(h + 1) * HD]) for j in range(t + 1)],
                    "finish": finish_plain(yt[:, t, h * HD:(h + 1) * HD])})
        attention_stage("fox", fox_units, scratch)

        swa_units = []
        for t in range(NT):
            for h in range(SWA_H):
                g, i = h // 4, h % 4
                k0 = max(t - 1, 0)
                nk = (t + 1 - k0) * P
                hp = slice(HD * g, HD * g + HD)
                swa_units.append({
                    "width": nk + 1,
                    "scores": [(0, nk, qkT[hp, 8 + i, q_tile(t)], qkT[hp, 12, k0 * P:k0 * P + nk]),
                               (0, nk, anti, toep[:, h, 256 - nk:256]),
                               (nk, 1, const[0:1, C_ONE:C_ONE + P], sinks[0:1, h:h + 1])],
                    "keys": [(j * P, tokv[:, k0 + j, 768 + g * HD:768 + (g + 1) * HD]) for j in range(nk // P)],
                    "finish": finish_plain(yt[:, t, 512 + h * HD:512 + (h + 1) * HD])})
        attention_stage("swa", swa_units, scratch)

        attn.close()
        ml = ExitStack()
        v1 = sb("v1", [P, NT, ML_H, HD + 1], ml)
        sw = sb("sw", [P, 2, 10 * P], ml)
        sw_at = [0, 4 * P, 7 * P, 9 * P]
        decay = sb("decay", [P, 2, S], ml)

        def mlstm_stage():
            n = ML_H * NT
            ocol = HD + 1
            with ExitStack() as sc:
                ones_in, qk, dec, dexp, weighted, summed, taken = (
                    sem(f"ml_{k}", sc) for k in ("ones", "qk", "dec", "dexp", "weighted", "summed", "taken"))
                with nc.Block() as block:
                    @block.gpsimd
                    def _(g):
                        nc.gpsimd.tensor_copy(v1[:, :, :, 0:HD],
                                              tokv[:, :, 256:512].rearrange("p t (h d) -> p t h d", d=HD)).then_inc(ones_in, 1)
                        g.wait_ge(ones_in, 1)
                        nc.gpsimd.memset(v1[:, :, :, HD:HD + 1], 1.0).then_inc(ones_in, 1)

                    @block.tensor
                    def _(pe):
                        def values(h):
                            pe.wait_ge(weighted, NT * (h + 1))
                            if h >= 2:
                                pe.wait_ge(taken, h - 1)
                            for t in range(NT):
                                for j in range(t + 1):
                                    mm = nc.tensor.matmul(bank[4 + h % 2][:, t * ocol:(t + 1) * ocol],
                                                          lhsT=sw[:, h % 2, sw_at[j] + (t - j) * P:sw_at[j] + (t - j + 1) * P], rhs=v1[:, j, h, :],
                                                          start=(j == 0), stop=(j == t))
                            mm.then_inc(summed, 1)

                        pe.wait_ge(ones_in, 2)
                        for h in range(ML_H):
                            hp = part(h)
                            for j in range(NT):
                                u = h * NT + j
                                if u >= 2:
                                    pe.wait_ge(weighted, u - 1)
                                c0 = j * P
                                nc.tensor.matmul(bank[2 + u % 2][:, c0:S], lhsT=const[32:36, C_SEL + h * P:C_SEL + (h + 1) * P],
                                                 rhs=rows[32:36, 1, c0:S], start=True, stop=False)
                                nc.tensor.matmul(bank[2 + u % 2][:, c0:c0 + P], lhsT=ident, rhs=mask_t,
                                                 start=False, stop=True).then_inc(dec, 1)
                                nc.tensor.matmul(bank[u % 2][:, c0:S], lhsT=qkT[hp, 6 + h // 2, q_tile(j)],
                                                 rhs=qkT[hp, 4 + h // 2, c0:S], start=True, stop=True).then_inc(qk, 1)
                            if h >= 1:
                                values(h - 1)
                        values(ML_H - 1)

                    @block.scalar
                    def _(a):
                        for u in range(n):
                            h, j = u // NT, u % NT
                            a.wait_ge(dec, u + 1)
                            if u >= 2:
                                a.wait_ge(weighted, u - 1)
                            nc.scalar.activation(decay[:, u % 2, j * P:S], bank[2 + u % 2][:, j * P:S], ACT.Exp,
                                                 bias=mcol[:, 0, j, h:h + 1]).then_inc(dexp, 1)

                    @block.vector
                    def _(v):
                        def take(h):
                            v.wait_ge(summed, h + 1)
                            nc.vector.tensor_copy(ho[:, h, :, :],
                                                  bank[4 + h % 2][:, 0:NT * ocol].rearrange("p (t c) -> p t c", c=ocol)).then_inc(taken, 1)

                        for h in range(ML_H):
                            for j in range(NT):
                                u = h * NT + j
                                v.wait_ge(qk, u + 1)
                                v.wait_ge(dexp, u + 1)
                                if h >= 2:
                                    v.wait_ge(summed, h - 1)
                                nc.vector.tensor_tensor(sw[:, h % 2, sw_at[j]:sw_at[j] + S - j * P], bank[u % 2][:, j * P:S],
                                                        decay[:, u % 2, j * P:S], ALU.mult).then_inc(weighted, 1)
                            if h >= 2:
                                take(h - 2)
                        take(ML_H - 2)
                        take(ML_H - 1)

        ho = sb("ho", [P, ML_H, NT, HD + 1], ml)
        hh = sb("hh", [P, ML_H, NT, HD], ml)
        hs = sb("hs", [P, ML_H, NT, HD], ml)
        mlstm_stage()

        def mlstm_out_stage():
            nht = ML_H * NT
            with ExitStack() as sc:
                em, sums, root, sig, chain = (sem(f"mo_{k}", sc) for k in ("em", "sums", "root", "sig", "chain"))
                with nc.Block() as block:
                    @block.scalar
                    def _(a):
                        nc.scalar.activation(stat[:, 0:nht].rearrange("p (h t) -> p h t", t=NT),
                                             mcol[:, 1, :, :].rearrange("p t h -> p h t"), ACT.Exp).then_inc(em, 1)
                        den = ho[:, :, :, HD:HD + 1].rearrange("p h t o -> p (h t o)")
                        nc.scalar.activation(stat[:, 48:48 + nht], den, ACT.Abs).then_inc(em, 1)
                        a.wait_ge(sums, 1)
                        nc.scalar.activation(stat[:, 32:32 + nht], stat[:, 16:16 + nht], ACT.Sqrt, bias=eps,
                                             scale=1.0 / HD).then_inc(root, 1)
                        nc.scalar.activation(tokv[:, :, 512:768], tokv[:, :, 512:768], ACT.Sigmoid).then_inc(sig, 1)

                    @block.vector
                    def _(v):
                        link = Chain(v, chain)
                        v.wait_ge(em, 2)
                        link(nc.vector.tensor_tensor(stat[:, 48:48 + nht], stat[:, 48:48 + nht], stat[:, 0:nht], ALU.max))
                        link(nc.vector.reciprocal(stat[:, 64:64 + nht], stat[:, 48:48 + nht]))
                        num = ho[:, :, :, 0:HD].rearrange("p h t d -> p (h t) d")
                        hv = hh[:, :, :, :].rearrange("p h t d -> p (h t) d")
                        hq = hs[:, :, :, :].rearrange("p h t d -> p (h t) d")
                        link(nc.vector.tensor_tensor(hv, num, stat[:, 64:64 + nht].unsqueeze(2).to_broadcast([P, nht, HD]), ALU.mult))
                        link(nc.vector.tensor_tensor(hq, hv, hv, ALU.mult))
                        nc.vector.tensor_reduce(stat[:, 16:16 + nht], hq, AXX, ALU.add).then_inc(sums, 1)
                        v.wait_ge(root, 1)
                        link(nc.vector.reciprocal(stat[:, 80:80 + nht], stat[:, 32:32 + nht]))
                        link(nc.vector.tensor_tensor(hv, hv, stat[:, 80:80 + nht].unsqueeze(2).to_broadcast([P, nht, HD]), ALU.mult))
                        v.wait_ge(sig, 1)
                        for t in range(NT):
                            link(nc.vector.tensor_tensor(hs[:, :, t, :], hh[:, :, t, :],
                                                         gain_h[:, :].rearrange("p (h d) -> p h d", d=HD), ALU.mult))
                            nc.vector.tensor_tensor(yt[:, t, 256:512].rearrange("p (h d) -> p h d", d=HD), hs[:, :, t, :],
                                                    tokv[:, t, 512:768].rearrange("p (h d) -> p h d", d=HD), ALU.mult)

        mlstm_out_stage()
        ml.close()
        turn_stage("yT", [(tok(yt, c * P), yT[:, (0, 1, 4, 5, 6, 7, 8, 9)[c], :], None) for c in range(8)])
        inner.close()

        merge = ExitStack()
        mT = sb("mT", [P, ND, S], merge)
        gate = sb("gate", [P, 4, S], merge)
        term = sb("term", [P, 2, S], merge)
        branch_tiles = ((0, 1), (2, 3), (4, 5), (6, 7, 8, 9))
        branch_w = ('w_fox_out', 'w_conv_out', 'w_mlstm_out', 'w_swa_out')

        def merge_stage():
            n0 = state["used"]
            n = ND * N_BRANCH
            with ExitStack() as sc:
                sig, merged, chain = sem("mg_sig", sc), sem("mg_merged", sc), sem("mg_chain", sc)

                def gate_tile(d, b):
                    return n0 + 8 * d + b

                def out_tile(d, b):
                    return n0 + 8 * d + 4 + b

                with nc.Block() as block:
                    @block.tensor
                    def _(pe):
                        for d in range(ND):
                            for b in range(N_BRANCH):
                                if d:
                                    pe.wait_ge(sig, (d - 1) * 4 + b + 1)
                                slot = tile_for(pe, gate_tile(d, b), 'w_in')
                                for k in range(ND):
                                    mm = nc.tensor.matmul(bank[b][:, :], lhsT=slot[:, k, :], rhs=hT[:, k, :],
                                                          start=(k == 0), stop=(k == ND - 1))
                                mm.then_inc(w_used, 1)
                            for b in range(N_BRANCH):
                                if d:
                                    pe.wait_ge(merged, (d - 1) * 4 + b + 1)
                                slot = tile_for(pe, out_tile(d, b), branch_w[b])
                                kt = len(branch_tiles[b])
                                for k, y in enumerate(branch_tiles[b]):
                                    mm = nc.tensor.matmul(bank[4 + b][:, :], lhsT=slot[:, k, :], rhs=yT[:, y, :],
                                                          start=(k == 0), stop=(k == kt - 1))
                                mm.then_inc(w_used, 1)

                    @block.scalar
                    def _(a):
                        for u in range(n):
                            d, b = u // 4, u % 4
                            a.wait_ge(w_used, gate_tile(d, b) + 1)
                            if d:
                                a.wait_ge(merged, (d - 1) * 4 + b + 1)
                            nc.scalar.activation(gate[:, b, :], bank[b][:, :], ACT.Sigmoid).then_inc(sig, 1)

                    @block.vector
                    def _(v):
                        link = Chain(v, chain)
                        for u in range(n):
                            d, b = u // 4, u % 4
                            v.wait_ge(sig, u + 1)
                            v.wait_ge(w_used, out_tile(d, b) + 1)
                            if b == 0:
                                nc.vector.tensor_tensor(mT[:, d, :], gate[:, b, :], bank[4 + b][:, :], ALU.mult).then_inc(merged, 1)
                                v.wait_ge(merged, u + 1)
                            else:
                                nc.vector.tensor_tensor(term[:, b % 2, :], gate[:, b, :], bank[4 + b][:, :], ALU.mult).then_inc(merged, 1)
                                v.wait_ge(merged, u + 1)
                                link(nc.vector.tensor_tensor(mT[:, d, :], mT[:, d, :], term[:, b % 2, :], ALU.add))

                    @block.sync
                    def _(sp):
                        load_weights(sp, n0 + 8 * ND)
            state["used"] = n0 + 8 * ND

        merge_stage()
        all_v = [True] * NT
        token_stage("wmerge", mT, ND, [('w_merge_out', BANK)] * 2, residual_add, all_v)
        merge.close()
        mixers.close()

        def ffn_stage(name, gate_w, up_w, actT, taps):
            n0 = state["used"]
            with ExitStack() as sc:
                g = sb(f"{name}_g", [P, 2, S + 2], sc)
                cv = sb(f"{name}_cv", [P, 2, S], sc)
                sl = sb(f"{name}_sl", [P, 2, S], sc)
                silued, acted, copied, convd, chain = (
                    sem(f"{name}_{k}", sc) for k in ("silued", "acted", "copied", "convd", "chain"))
                with nc.Block() as block:
                    @block.tensor
                    def _(pe):
                        for f in range(NF):
                            for i, wname in enumerate((gate_w, up_w)):
                                if f >= 4:
                                    pe.wait_ge(acted, f - 3)
                                slot = tile_for(pe, n0 + 2 * f + i, wname)
                                for k in range(ND):
                                    mm = nc.tensor.matmul(bank[2 * (f % 4) + i][:, :], lhsT=slot[:, k, :],
                                                          rhs=hT[:, k, :], start=(k == 0), stop=(k == ND - 1))
                                mm.then_inc(w_used, 1)

                    @block.scalar
                    def _(a):
                        for f in range(NF):
                            a.wait_ge(w_used, n0 + 2 * f + 1)
                            src = bank[2 * (f % 4)][:, :]
                            if taps is not None:
                                if f >= 2:
                                    a.wait_ge(convd, f - 1)
                                nc.scalar.activation(g[:, f % 2, 2:], src, ACT.Copy).then_inc(copied, 1)
                                a.wait_ge(convd, f + 1)
                                src = cv[:, f % 2, :]
                            if f >= 2:
                                a.wait_ge(acted, f - 1)
                            nc.scalar.activation(sl[:, f % 2, :], src, ACT.Silu).then_inc(silued, 1)

                    @block.vector
                    def _(v):
                        link = Chain(v, chain)
                        if taps is not None:
                            link(nc.vector.memset(g[:, :, 0:2], 0.0))
                        for f in range(NF):
                            if taps is not None:
                                v.wait_ge(copied, f + 1)
                                if f >= 2:
                                    v.wait_ge(silued, f - 1)
                                c = cv[:, f % 2, :]
                                link(nc.vector.tensor_scalar(c, g[:, f % 2, 2:514], taps(2, f), None, ALU.mult))
                                link(nc.vector.scalar_tensor_tensor(c, g[:, f % 2, 1:513], taps(1, f), c, ALU.mult, ALU.add))
                                nc.vector.scalar_tensor_tensor(c, g[:, f % 2, 0:512], taps(0, f), c,
                                                               ALU.mult, ALU.add).then_inc(convd, 1)
                            v.wait_ge(silued, f + 1)
                            v.wait_ge(w_used, n0 + 2 * f + 2)
                            nc.vector.tensor_tensor(actT[:, f, :], sl[:, f % 2, :], bank[2 * (f % 4) + 1][:, :],
                                                    ALU.mult).then_inc(acted, 1)

                    @block.sync
                    def _(sp):
                        load_weights(sp, n0 + 2 * NF)
            state["used"] = n0 + 2 * NF

        def ffn(name, gain, gate_w, up_w, down_w, taps):
            norm_stage(f"{name}n", x, NT, gain, hT)
            with ExitStack() as sc:
                actT = sb(f"{name}_act", [P, NF, S], sc)
                ffn_stage(name, gate_w, up_w, actT, taps)
                token_stage(f"{name}d", actT, NF, [(down_w, BANK)] * 2, residual_add, all_v)

        ffn("ffn1", par[:, K_FNORM:], 'w_gate', 'w_up', 'w_down', None)

        clear_stage()

        norm_stage("mix", x, NT, par[:, K_MIX:], hT)
        nsa = ExitStack()
        ot = sb("ot", [P, NT, D], nsa)
        nq = sb("nq", [P, 8, S], nsa)
        nkT = sb("nkT", [P, 4, S], nsa)
        nv = sb("nv", [P, NT, 560], nsa)
        kcmp = sb("kcmp", [P, NSA_G, 32], nsa)
        vcmp = sb("vcmp", [P, NSA_G, 256], nsa)
        cmp_s = ExitStack()
        kcs = sb("kcs", [P, 2, NSA_G, S], cmp_s)
        hid = sb("hid", [P, 2, 2, NSA_G * CMP_N], cmp_s)
        pebias = sb("pebias", [P, 4], cmp_s)
        w2k = sb("w2k", [P, 2, P], cmp_s)
        w2v = sb("w2v", [P, 2, HD], cmp_s)

        def nsa_q_stage():
            n0 = state["used"]
            with ExitStack() as sc:
                out_v, out_a = sem("nq_outv", sc), sem("nq_outa", sc)
                with nc.Block() as block:
                    @block.tensor
                    def _(pe):
                        for a in range(2):
                            for s in range(4):
                                slot = tile_for(pe, n0 + 4 * a + s, 'nsa_w_in_2')
                                for kk in range(2):
                                    k = 2 * s + kk
                                    for i in range(HPG):
                                        mm = nc.tensor.matmul(bank[4 * a + i][:, :], lhsT=slot[:, kk, i * P:(i + 1) * P], rhs=hT[:, k, :],
                                                              start=(k == 0), stop=(k == ND - 1))
                                mm.then_inc(w_used, 1)

                    @block.vector
                    def _(v):
                        for a in range(2):
                            v.wait_ge(w_used, n0 + 4 * a + 4)
                            for i in (0, 1):
                                scaled(True, nq[:, 4 * a + i, :], bank[4 * a + i][:, :], HD ** -0.5).then_inc(out_v, 1)

                    @block.scalar
                    def _(e):
                        for a in range(2):
                            e.wait_ge(w_used, n0 + 4 * a + 4)
                            for i in (2, 3):
                                nc.scalar.activation(nq[:, 4 * a + i, :], bank[4 * a + i][:, :], ACT.Copy,
                                                     scale=HD ** -0.5).then_inc(out_a, 1)

                    @block.sync
                    def _(sp):
                        load_weights(sp, n0 + 8)
            state["used"] = n0 + 8

        nsa_q_stage()

        def evac_nsa_feat(i, ps, vector):
            if i >= 4:
                return copy(vector, nkT[:, i - 4, :], ps)
            kv, pair = i // 2, i % 2
            for j in range(2):
                g = 2 * pair + j
                src = ps[HD * j:HD * j + HD, :]
                copy(vector, kcs[0:HD, kv, g, :], src)
                ins = copy(vector, kcs[HD:P, kv, g, 0:S - 1], src[:, 1:S])
            return ins

        feature_stage("nsaT", hT, S, ['nsa_w_in_2'] * 8, evac_nsa_feat)

        def evac_nsa_tok(c, t, ps, vector):
            return copy(vector, nv[:, t, c * 256:c * 256 + ps.shape[-1]], ps)

        token_stage("nsaV", hT, ND, [('nsa_w_in_2', 256), ('nsa_w_in_2', 304)], evac_nsa_tok, half)

        def compress_stage():
            n0 = state["used"]
            nb = NSA_G * CMP_N
            with ExitStack() as sc:
                w2_in, first, biased, act, second, chain, zeroed = (
                    sem(f"cmp_{k}", sc) for k in ("w2", "first", "biased", "act", "second", "chain", "zeroed"))
                with nc.Block() as block:
                    @block.sync
                    def _(sp):
                        kw = w['nsa_ck_w2_2'].rearrange("(k p) c -> p k c", p=P)
                        sp.dma_start(w2k[:, :, 0:HD], kw).then_inc(w2_in, 16)
                        sp.dma_start(w2k[:, :, HD:P], kw).then_inc(w2_in, 16)
                        sp.dma_start(w2v[:, :, :], w['nsa_cv_w2_2'].rearrange("(k p) c -> p k c", p=P)).then_inc(w2_in, 16)
                        load_weights(sp, n0 + 8)
                        sp.wait_ge(w2_in, 48)

                    @block.gpsimd
                    def _(g):
                        nc.gpsimd.memset(kcmp[:, :, :], 0.0).then_inc(zeroed, 1)
                        g.wait_ge(zeroed, 1)
                        nc.gpsimd.memset(vcmp[:, :, :], 0.0).then_inc(zeroed, 1)

                    @block.tensor
                    def _(pe):
                        for kv in range(2):
                            pcol = K_PEK if kv == 0 else K_PEV
                            for s in range(4):
                                slot = tile_for(pe, n0 + 4 * kv + s, ('nsa_ck_w1_2', 'nsa_cv_w1_2')[kv])
                                for kk in range(4):
                                    m = 4 * s + kk
                                    blk = kcs[:, kv, :, 2 * m:2 * m + 16 * (CMP_N - 1) + 1:16]
                                    for half_ in range(2):
                                        lhs = slot[:, kk, half_ * P:(half_ + 1) * P]
                                        nc.tensor.matmul(bank[4 * kv + half_][:, 0:nb], lhsT=lhs, rhs=blk,
                                                         start=(m == 0), stop=(m == 15))
                                        mm = nc.tensor.matmul(bank[4 * kv + 2 + half_][:, 0:1], lhsT=lhs,
                                                              rhs=par[:, pcol + m:pcol + m + 1],
                                                              start=(m == 0), stop=(m == 15))
                                mm.then_inc(w_used, 1)
                        pe.wait_ge(w2_in, 48)
                        pe.wait_ge(act, 4)
                        for k in range(2):
                            mm = nc.tensor.matmul(bank[0][:, 0:nb], lhsT=w2k[:, k, :], rhs=hid[:, 0, k, :],
                                                  start=(k == 0), stop=(k == 1))
                        for g in range(NSA_G):
                            for k in range(2):
                                mm = nc.tensor.matmul(bank[1][0:CMP_N, g * HD:(g + 1) * HD],
                                                      lhsT=hid[:, 1, k, g * CMP_N:(g + 1) * CMP_N], rhs=w2v[:, k, :],
                                                      start=(k == 0), stop=(k == 1))
                        mm.then_inc(second, 1)

                    @block.vector
                    def _(v):
                        for kv in range(2):
                            v.wait_ge(w_used, n0 + 4 * kv + 4)
                            for h in range(2):
                                nc.vector.tensor_copy(pebias[:, 2 * kv + h:2 * kv + h + 1],
                                                      bank[4 * kv + 2 + h][:, 0:1]).then_inc(biased, 1)
                        v.wait_ge(second, 1)
                        v.wait_ge(zeroed, 2)
                        nc.vector.tensor_copy(kcmp[:, :, 0:CMP_N], bank[0][:, 0:nb].rearrange("p (g n) -> p g n", n=CMP_N))
                        for i in range(HPG):
                            nc.vector.tensor_copy(vcmp[32 * i:32 * i + CMP_N, :, i * HD:(i + 1) * HD],
                                                  bank[1][0:CMP_N, 0:256].rearrange("p (g d) -> p g d", d=HD))

                    @block.scalar
                    def _(a):
                        for kv in range(2):
                            for h in range(2):
                                a.wait_ge(biased, 2 * kv + h + 1)
                                nc.scalar.activation(hid[:, kv, h, :], bank[4 * kv + h][:, 0:nb], ACT.Gelu_apprx_tanh,
                                                     bias=pebias[:, 2 * kv + h:2 * kv + h + 1]).then_inc(act, 1)
                        nc.scalar.activation(nv[:, :, 512:560], nv[:, :, 512:560], ACT.Sigmoid).then_inc(chain, 1)
            state["used"] = n0 + 8

        compress_stage()
        cmp_s.close()

        attn = ExitStack()
        prob = sb("nprob", [P, 3, 514], attn)
        probT = sb("nprobT", [P, 2, S], attn)
        gates = nv[:, :, 512:560].rearrange("p t (h b) -> p t h b", b=3)

        def cmp_attention_stage():
            with ExitStack() as sc:
                scores = sb("cscores", [P, 2, NSA_H, 32], sc)
                scored, masked, exped, turned, copied, summed, done, chain = (
                    sem(f"ca_{k}", sc) for k in ("scored", "masked", "exped", "turned", "copied", "summed", "done", "chain"))
                with nc.Block() as block:
                    @block.tensor
                    def _(pe):
                        for t in range(NT):
                            if t >= 1:
                                pe.wait_ge(masked, t)
                            for h in range(NSA_H):
                                g, i = h // HPG, h % HPG
                                gp = part(g)
                                at = ((g // 2) * HPG + i) * 32
                                mm = nc.tensor.matmul(bank[4 * (g % 2)][:, at:at + 32],
                                                      lhsT=nq[gp, 4 * (g // 2) + i, q_tile(t)], rhs=kcmp[gp, g, :],
                                                      start=True, stop=True)
                            mm.then_inc(scored, 1)
                            pe.wait_ge(exped, t + 1)
                            if t >= 1:
                                pe.wait_ge(copied, t)
                            for g in range(NSA_G):
                                mm = nc.tensor.transpose(bank[1][:, g * P:(g + 1) * P],
                                                         scores[:, t % 2, 4 * g:4 * g + 4, :].rearrange("p h n -> p (h n)"),
                                                         ident)
                            mm.then_inc(turned, 1)
                            pe.wait_ge(copied, t + 1)
                            if t >= 1:
                                pe.wait_ge(done, t)
                            for g in range(NSA_G):
                                mm = nc.tensor.matmul(bank[2 + g // 2][:, (g % 2) * 256:(g % 2) * 256 + 256],
                                                      lhsT=probT[:, t % 2, g * P:(g + 1) * P], rhs=vcmp[:, g, :],
                                                      start=True, stop=True)
                            mm.then_inc(summed, 1)

                    @block.scalar
                    def _(a):
                        for t in range(NT):
                            a.wait_ge(masked, t + 1)
                            nc.scalar.activation(scores[:, t % 2, :, :], scores[:, t % 2, :, :], ACT.Exp).then_inc(exped, 1)
                            a.wait_ge(turned, t + 1)
                            nc.scalar.activation(probT[:, t % 2, :], bank[1][:, :], ACT.Copy).then_inc(copied, 1)

                    @block.vector
                    def _(v):
                        link = Chain(v, chain)
                        for t in range(NT):
                            sv_ = scores[:, t % 2, :, :]
                            v.wait_ge(scored, t + 1)
                            mask = const[:, C_CMP + 32 * t:C_CMP + 32 * t + 32].unsqueeze(1).to_broadcast([P, HPG, 32])
                            by_group = sv_.rearrange("p (g i) n -> p g i n", i=HPG)
                            for g in range(NSA_G):
                                src = bank[4 * (g % 2)][:, (g // 2) * P:(g // 2 + 1) * P]
                                link(nc.vector.tensor_tensor(by_group[:, g, :, :], src.rearrange("p (i n) -> p i n", n=32),
                                                             mask, ALU.add))
                            link(nc.vector.tensor_reduce(stat[:, 40:56], sv_, AXX, ALU.max))
                            nc.vector.tensor_tensor(sv_, sv_, stat[:, 40:56].unsqueeze(2).to_broadcast([P, NSA_H, 32]),
                                                    ALU.subtract).then_inc(masked, 1)
                            v.wait_ge(exped, t + 1)
                            link(nc.vector.tensor_reduce(stat[:, 60:76], sv_, AXX, ALU.add))
                            link(nc.vector.reciprocal(stat[:, 80:96], stat[:, 60:76]))
                            link(nc.vector.tensor_scalar(stat[:, 80:96], stat[:, 80:96],
                                                         const[:, C_VALID + t:C_VALID + t + 1], None, ALU.mult))
                            link(nc.vector.tensor_tensor(stat[:, 100:116], stat[:, 80:96], gates[:, t, :, 0], ALU.mult))
                            v.wait_ge(summed, t + 1)
                            for b in range(2):
                                ins = nc.vector.tensor_tensor(
                                    ot[:, t, b * BANK:(b + 1) * BANK].rearrange("p (h d) -> p h d", d=HD),
                                    bank[2 + b][:, :].rearrange("p (h d) -> p h d", d=HD),
                                    stat[:, 100 + 8 * b:108 + 8 * b].unsqueeze(2).to_broadcast([P, 8, HD]), ALU.mult)
                            ins.then_inc(done, 1)

        cmp_attention_stage()

        nsa_units = []
        for t in range(NT):
            for h in range(NSA_H):
                g, i = h // HPG, h % HPG
                gp = part(g)
                for b in range(2):
                    wd = (t + 1) * P
                    nsa_units.append({
                        "width": wd,
                        "scores": [(0, wd, nq[gp, 4 * (g // 2) + i, q_tile(t)], nkT[gp, 2 * b + g // 2, 0:wd]),
                                   (t * P, P, ident, mask_q)],
                        "keys": [(j * P, nv[:, j, 256 * b + g * HD:256 * b + (g + 1) * HD]) for j in range(t + 1)],
                        "finish": finish_gated(ot[:, t, h * HD:(h + 1) * HD], gates[:, t, h, 1 + b:2 + b])})
        attention_stage("nsa", nsa_units, (prob, probT))
        attn.close()

        turn_stage("oT", [(tok(ot, c * P), hT[:, c, :], None) for c in range(8)])
        token_stage("nsaO", hT, ND, [('nsa_w_out_2', BANK)] * 2, residual_add, all_v)
        nsa.close()

        cross = ExitStack()
        cq = sb("cq", [P, ND, S], cross)
        ckT = sb("ckT", [P, ND, MEM], cross)
        cv_ = sb("cv", [P, 2, D], cross)
        co = sb("co", [P, NT, D], cross)
        memx = ExitStack()
        mem = sb("mem", [P, 2, D], memx)
        memT = sb("memT", [P, ND, MEM], memx)

        def mem_stage():
            with nc.Block() as block, ExitStack() as sc:
                in_ = sem("mem_in", sc)

                @block.sync
                def _(sp):
                    sp.dma_start(mem[:, :, :], w['mem_2'].rearrange("o (t p) d -> p (o t) d", p=P)).then_inc(in_, 16)
                    sp.wait_ge(in_, 16)

        mem_stage()
        norm_stage("memn", mem, 2, par[:, K_MEM:], memT)
        feature_stage("ckT", memT, MEM, ['ca_wkv_2'] * 8, lambda i, ps, vec: copy(vec, ckT[:, i, :], ps))
        token_stage("cv", memT, ND, [('ca_wkv_2', BANK)] * 2,
                    lambda c, t, ps, vec: copy(vec, cv_[:, t, c * BANK:(c + 1) * BANK], ps), half, tiles=2)
        memx.close()
        norm_stage("cross", x, NT, par[:, K_CROSS:], hT)
        feature_stage("cqT", hT, S, ['ca_wq_2'] * 8,
                      lambda i, ps, vec: scaled(vec, cq[:, i, :], ps, CA_D ** -0.5) if vec else
                      nc.scalar.activation(cq[:, i, :], ps, ACT.Copy, scale=CA_D ** -0.5))
        attn = ExitStack()
        prob = sb("cprob", [P, 3, 514], attn)
        probT = sb("cprobT", [P, 2, S], attn)
        ca_units = []
        for t in range(NT):
            for h in range(CA_H):
                ca_units.append({
                    "width": MEM,
                    "scores": [(0, MEM, cq[:, 2 * h + k, q_tile(t)], ckT[:, 2 * h + k, :]) for k in range(2)],
                    "keys": [(j * P, cv_[:, j, h * CA_D:(h + 1) * CA_D]) for j in range(2)],
                    "finish": finish_plain(co[:, t, h * CA_D:(h + 1) * CA_D])})
        attention_stage("xattn", ca_units, (prob, probT))
        attn.close()
        turn_stage("coT", [(tok(co, c * P), hT[:, c, :], None) for c in range(8)])
        token_stage("cao", hT, ND, [('ca_wo_2', BANK)] * 2, residual_add, all_v)
        cross.close()

        ffn("ffn2", par[:, K_FFN2:], 'ffn_w_up_2', 'ffn_w_up_2', 'ffn_w_down_2',
            lambda j, f: par[:, K_CONV2 + 22 * j + f:K_CONV2 + 22 * j + f + 1])
        assert state["used"] == len(plan)

        def final_stage():
            with ExitStack() as sc:
                gain = sb("fgain", [P, D], sc)
                sq = sb("fsq", [P, D], sc)
                gain_in, squared, rooted, chain, ready = (
                    sem(f"fin_{k}", sc) for k in ("gain", "sq", "root", "chain", "ready"))
                with nc.Block() as block:
                    @block.sync
                    def _(sp):
                        sp.dma_start(gain[:, :], w['final_norm_w_2'].unsqueeze(0).to_broadcast([P, D])).then_inc(gain_in, 16)
                        ov = out.rearrange("o (t p) d -> p (o t) d", p=P)
                        for t in range(NT):
                            sp.wait_ge(ready, t + 1)
                            sp.dma_start(ov[:, t, :], x[:, t, :]).then_inc(stored, 16)
                        sp.wait_ge(stored, 16 * NT)

                    @block.scalar
                    def _(a):
                        link = Chain(a, squared)
                        for t in range(NT):
                            link(nc.scalar.activation(sq[:, :], x[:, t, :], ACT.Square, accum_out=stat[:, t:t + 1]))
                        nc.scalar.activation(stat[:, 8:8 + NT], stat[:, 0:NT], ACT.Sqrt, bias=eps,
                                             scale=1.0 / D).then_inc(rooted, 1)

                    @block.vector
                    def _(v):
                        link = Chain(v, chain)
                        v.wait_ge(rooted, 1)
                        link(nc.vector.reciprocal(stat[:, 16:16 + NT], stat[:, 8:8 + NT]))
                        v.wait_ge(gain_in, 16)
                        for t in range(NT):
                            nc.vector.scalar_tensor_tensor(x[:, t, :], x[:, t, :], stat[:, 16 + t:17 + t], gain[:, :],
                                                           ALU.mult, ALU.mult).then_inc(ready, 1)

        final_stage()


_WEIGHTS = ['w_in', 'w_fox_out', 'w_conv_out', 'w_mlstm_out', 'w_swa_out', 'w_merge_out', 'w_gate', 'w_up', 'w_down',
            'nsa_w_in_2', 'nsa_ck_w1_2', 'nsa_ck_w2_2', 'nsa_cv_w1_2', 'nsa_cv_w2_2', 'nsa_w_out_2', 'ca_wq_2',
            'ca_wkv_2', 'ca_wo_2', 'ffn_w_up_2', 'ffn_w_down_2']
_OTHERS = ['x', 'mem_2', 'rel_bias', 'mlstm_h_gain', 'swa_sinks', 'final_norm_w_2']


def kernel(**inputs):
    import concourse.bacc as bacc
    from concourse.bass_utils import run_bass_kernel_spmd

    nc = bacc.Bacc("TRN2", target_bir_lowering=False, num_devices=1)
    a = {k: np.asarray(v) for k, v in inputs.items()}
    send = {k: np.ascontiguousarray(a[k][0]) for k in _WEIGHTS}
    send.update({k: np.ascontiguousarray(a[k]) for k in _OTHERS})
    send['w_in'] = pair_heads(send['w_in'], SQ, 1, SWA_H // 2)
    send['nsa_w_in_2'] = pair_heads(send['nsa_w_in_2'], NQ, 2, HPG)
    send['const'] = shape_constants()
    send['par'] = pack_params(a)
    arrays, w = {}, {}
    for name, v in send.items():
        arrays[f"in_{name}"] = v
        w[name] = nc.dram_tensor(f"in_{name}", v.shape, F32, kind="ExternalInput").ap()
    w['bias_rows'] = nc.dram_tensor("bias_rows", [SWA_H, 384], F32, kind="Internal").ap()
    out = nc.dram_tensor("out", [1, S, D], F32, kind="ExternalOutput").ap()
    build(nc, w, out)
    r = run_bass_kernel_spmd(nc, [arrays], core_ids=[0])
    return np.asarray(r.results[0]["out"]).reshape(1, S, D)
```

```python
from contextlib import ExitStack

import numpy as np

import concourse.bass as bass
from concourse import mybir

F32 = mybir.dt.float32
F32R = mybir.dt.float32r
ALU = mybir.AluOpType
ACT = mybir.ActivationFunctionType
AXX = mybir.AxisListType.X

P = 128
S = 512
D = 1024
NT = S // P
ND = D // P
BANK = 512
EPS = 1e-6
NEG = -1e30
HD = 64

FQ, FK, FV, FF = 0, 256, 512, 768
CU, CB, CC = 772, 1028, 1284
MQ, MK, MV, MI, MF, MO = 1540, 1796, 2052, 2308, 2312, 2316
SQ, SK, SV, GATES = 2572, 3084, 3212, 3340
FOX_H, ML_H, SWA_H = 4, 4, 8
N_BRANCH = 4
DFF = 2816
NF = DFF // P
FG = NF // 2
BUCKETS = 32

NQ, NKC, NVC, NKS, NVS, NKW, NVW, NGL = 0, 1024, 1280, 1536, 1792, 2048, 2304, 2560
NSA_H, NSA_G, HPG = 16, 4, 4
CMP_N = 31
CMP_HID = 256
MEM = 256
CA_H, CA_D = 4, 256

RING = 6
SPLIT = 3

C_ID, C_ANTI, C_MQ, C_MT = 0, P, 2 * P, 3 * P
C_CMP = 4 * P
C_VALID = C_CMP + NT * 32
C_SEL = C_VALID + NT
C_OH = C_SEL + 4 * P
C_ONE = C_OH + 384
C_END = C_ONE + P

(K_ANORM, K_FNORM, K_MIX, K_CROSS, K_FFN2, K_MEM) = (8 * i for i in range(6))
K_FQ, K_FK, K_SQ, K_SK = 48, 49, 50, 51
K_CONV = 52
K_BIAS = 58
K_CONV2 = 60
K_PEK = K_CONV2 + 66
K_PEV = K_PEK + 16
K_END = K_PEV + 18


def shape_constants():
    c = np.zeros((P, C_END), np.float32)
    i = np.arange(P)
    c[:, C_ID:C_ID + P] = np.eye(P)
    c[:, C_ANTI:C_ANTI + P] = np.eye(P)[::-1]
    c[:, C_MQ:C_MQ + P] = np.where(i[None, :] <= i[:, None], 0, NEG)
    c[:, C_MT:C_MT + P] = np.where(i[:, None] <= i[None, :], 0, NEG)
    n = np.arange(32)
    for t in range(NT):
        tok = t * P + i
        seen = (16 * n[None, :] + 31 <= tok[:, None]) & (n[None, :] < CMP_N)
        c[:, C_CMP + 32 * t:C_CMP + 32 * t + 32] = np.where(seen, 0, NEG)
        c[:, C_VALID + t] = tok >= 31
    for h in range(4):
        c[h, C_SEL + h * P:C_SEL + (h + 1) * P] = 1
        c[32 + h, C_SEL + h * P:C_SEL + (h + 1) * P] = 1
    dist = 255 - np.arange(384)
    n1 = np.maximum(dist, 1).astype(np.float32)
    large = 16 + (np.log(n1 / np.float32(16)) / np.float32(np.log(8.0)) * np.float32(16)).astype(np.int32)
    bucket = np.where(dist < 16, dist, np.minimum(large, BUCKETS - 1))
    for u in range(384):
        if 0 <= dist[u] < 128:
            c[bucket[u], C_OH + u] = 1
        else:
            c[BUCKETS, C_OH + u] = NEG
    c[:, C_ONE:C_ONE + P] = 1
    return c


def pack_params(a):
    k = np.zeros((P, K_END), np.float32)

    def tiles(v):
        return np.asarray(v).reshape(-1, P).T

    for at, name in ((K_ANORM, 'attn_norm'), (K_FNORM, 'ffn_norm'), (K_MIX, 'norm_mix_w_2'),
                     (K_CROSS, 'norm_cross_w_2'), (K_FFN2, 'norm_ffn_w_2'), (K_MEM, 'mem_norm_w_2')):
        k[:, at:at + 8] = tiles(a[name])
    for at, name in ((K_FQ, 'fox_q_gain'), (K_FK, 'fox_k_gain'), (K_SQ, 'swa_q_gain'), (K_SK, 'swa_k_gain')):
        k[0:HD, at] = a[name][0]
        k[HD:P, at] = a[name][0]
    k[:, K_CONV:K_CONV + 6] = tiles(a['conv_w'])
    k[0:4, K_BIAS] = a['fox_f_bias'][0]
    k[32:36, K_BIAS] = a['mlstm_i_bias'][0]
    k[64:68, K_BIAS] = a['mlstm_f_bias'][0]
    k[:, K_CONV2:K_CONV2 + 66] = tiles(a['ffn_conv_w_2'])
    k[:, K_PEK:K_PEK + 16] = tiles(a['nsa_pe_k_2'])
    k[:, K_PEV:K_PEV + 16] = tiles(a['nsa_pe_v_2'])
    return k


def pair_heads(weight, at, blocks, per):
    m = weight.copy()
    n = blocks * 2 * per * HD
    q = m[:, at:at + n].reshape(-1, blocks, 2, per, HD)
    m[:, at:at + n] = q.transpose(0, 1, 3, 2, 4).reshape(-1, n)
    return m


class Chain:

    def __init__(self, eng, sem):
        self.eng, self.sem, self.n = eng, sem, 0

    def __call__(self, ins):
        self.n += 1
        ins.then_inc(self.sem, 1)
        self.eng.wait_ge(self.sem, self.n)


def build(nc, w, out):
    ctx = ExitStack()
    with ctx:
        def sb(name, shape, scope=ctx, dt=F32):
            return scope.enter_context(nc.sbuf_tensor(name, list(shape), dt))

        stage_sems = []

        def sem(name, scope=ctx):
            if scope is ctx:
                return ctx.enter_context(nc.semaphore(name))
            stage_sems.append(nc.alloc_semaphore(name))
            return stage_sems[-1]

        def clear_stage():
            with nc.Block() as block:
                @block.gpsimd
                def _(g):
                    nc.clear_and_free_semaphores(list(stage_sems))
            stage_sems.clear()

        bank = [ctx.enter_context(nc.psum_tensor(f"bank{i}", [P, BANK], F32)) for i in range(8)]
        const = sb("const", [P, C_END])
        par = sb("par", [P, K_END])
        x = sb("x", [P, NT, D])
        hT = sb("hT", [P, ND, S], dt=F32R)
        hL = sb("hL", [P, ND, S], dt=F32R)
        ring = sb("ring", [P, RING, 1024])
        w_high = sb("w_high", [P, SPLIT, 1024], dt=F32R)
        w_low = sb("w_low", [P, SPLIT, 1024], dt=F32R)
        stat = sb("stat", [P, 160])

        ident = const[:, C_ID:C_ID + P]
        anti = const[:, C_ANTI:C_ANTI + P]
        mask_q = const[:, C_MQ:C_MQ + P]
        mask_t = const[:, C_MT:C_MT + P]
        eps = stat[:, 150:151]

        w_ready = [sem(f"w_ready{i}") for i in range(RING)]
        w_hi = sem("w_hi")
        w_lo = sem("w_lo")
        w_used = sem("w_used")
        stored = sem("stored")
        plan = []

        def cols(name, c0, n=P, first=0, kt=None):
            m = w[name]
            per = 1024 // n
            end = m.shape[0] // P if kt is None else first + kt
            for k0 in range(first, end, per):
                k = min(per, end - k0)
                src = m[k0 * P:(k0 + k) * P, c0:c0 + n].rearrange("(k p) c -> p k c", p=P)
                plan.append((name, src, k, n))

        def weight_plan():
            for c0, n in TOKEN_CHUNKS_A:
                cols('w_in', c0, n)
            for c0 in FEATURE_TILES_A:
                cols('w_in', c0)
            for d in range(ND):
                for b in range(N_BRANCH):
                    cols('w_in', GATES + b * D + d * P)
                for b in range(N_BRANCH):
                    cols(('w_fox_out', 'w_conv_out', 'w_mlstm_out', 'w_swa_out')[b], d * P)
            for half in range(2):
                cols('w_merge_out', half * BANK, BANK)
            for f0 in range(0, NF, FG):
                for f in range(f0, f0 + FG):
                    cols('w_gate', f * P)
                    cols('w_up', f * P)
                for half in range(2):
                    cols('w_down', half * BANK, BANK, f0, FG)
            for half in range(2):
                cols('nsa_w_in_2', half * BANK, BANK)
            for c0 in FEATURE_TILES_N:
                cols('nsa_w_in_2', c0)
            for c0, n in TOKEN_CHUNKS_N:
                cols('nsa_w_in_2', c0, n)
            cols('nsa_ck_w1_2', 0, CMP_HID)
            cols('nsa_cv_w1_2', 0, CMP_HID)
            for half in range(2):
                cols('nsa_w_out_2', half * BANK, BANK)
            for d in range(ND):
                cols('ca_wkv_2', d * P)
            for half in range(2):
                cols('ca_wkv_2', D + half * BANK, BANK)
            for d in range(ND):
                cols('ca_wq_2', d * P)
            for half in range(2):
                cols('ca_wo_2', half * BANK, BANK)
            for f0 in range(0, NF, FG):
                for f in range(f0, f0 + FG):
                    cols('ffn_w_up_2', f * P)
                    cols('ffn_w_up_2', DFF + f * P)
                for half in range(2):
                    cols('ffn_w_down_2', half * BANK, BANK, f0, FG)

        TOKEN_CHUNKS_A = [(FQ, 512), (FV, 256), (MV, 256), (MO, 256), (SQ, 512), (SK, 256)]
        FEATURE_TILES_A = [c + P * i for c in (MQ, MK, CU, CC, CB) for i in range(2)]
        FEATURE_TILES_N = [c + P * i for c in (NKC, NVC, NKS, NKW) for i in range(2)]
        TOKEN_CHUNKS_N = [(NVS, 256), (NVW, 304)]
        weight_plan()
        state = {"issued": 0, "used": 0, "high": 0, "low": 0}

        def tile_view(buf, n, depth):
            _, _, k, width = plan[n]
            return buf[:, n % depth, 0:k * width].rearrange("p (k c) -> p k c", c=width)

        def load_weights(sp, split):
            while state["issued"] < min(split + RING, len(plan)):
                n = state["issued"]
                if n >= RING:
                    sp.wait_ge(w_lo, n - RING + 1)
                sp.dma_start(tile_view(ring, n, RING), plan[n][1]).then_inc(w_ready[n % RING], 16)
                state["issued"] += 1

        def split_high(a, end):
            while state["high"] < min(end, len(plan)):
                n = state["high"]
                a.wait_ge(w_ready[n % RING], 16 * (n // RING + 1))
                if n >= SPLIT:
                    a.wait_ge(w_used, n - SPLIT + 1)
                nc.scalar.activation(tile_view(w_high, n, SPLIT), tile_view(ring, n, RING), ACT.Copy).then_inc(w_hi, 1)
                state["high"] += 1

        def split_low(g, end):
            while state["low"] < min(end, len(plan)):
                n = state["low"]
                g.wait_ge(w_hi, n + 1)
                nc.gpsimd.tensor_tensor(tile_view(w_low, n, SPLIT), tile_view(ring, n, RING),
                                        tile_view(w_high, n, SPLIT), ALU.subtract).then_inc(w_lo, 1)
                state["low"] += 1

        def tile_for(pe, n, name):
            assert plan[n][0] == name, (plan[n][0], name, n)
            pe.wait_ge(w_lo, n + 1)
            return tile_view(w_high, n, SPLIT), tile_view(w_low, n, SPLIT)

        def product(ps, stationary, moving, first, last):
            (sh, sl), (mh, ml_) = stationary, moving
            nc.tensor.matmul(ps, lhsT=sh, rhs=mh, start=first, stop=False)
            nc.tensor.matmul(ps, lhsT=sh, rhs=ml_, start=False, stop=False)
            return nc.tensor.matmul(ps, lhsT=sl, rhs=mh, start=False, stop=last)

        def copy(vector, dst, src):
            if vector:
                return nc.vector.tensor_copy(dst, src)
            return nc.scalar.activation(dst, src, ACT.Copy)

        def scaled(vector, dst, src, by):
            if vector:
                return nc.vector.tensor_scalar(dst, src, by, None, ALU.mult)
            return nc.scalar.activation(dst, src, ACT.Copy, scale=by)

        def load_stage():
            with nc.Block() as block, ExitStack() as sc:
                loaded = sem("loaded", sc)

                @block.sync
                def _(sp):
                    sp.dma_start(x[:, :, :], w['x'].rearrange("o (t p) d -> p (o t) d", p=P)).then_inc(loaded, 16)
                    sp.dma_start(const[:, :], w['const']).then_inc(loaded, 16)
                    sp.dma_start(par[:, :], w['par']).then_inc(loaded, 16)
                    load_weights(sp, 0)
                    sp.wait_ge(loaded, 48)

                @block.vector
                def _(v):
                    nc.vector.memset(eps, EPS)

        def norm_stage(name, src, tiles, gain, dst, scope_bytes=None):
            with ExitStack() as sc:
                h = sb(f"{name}_h", [P, tiles, D], sc)
                sq = sb(f"{name}_sq", [P, D], sc)
                squared, rooted, scaled_h = (sem(f"{name}_{s}", sc) for s in ("squared", "rooted", "scaled"))
                turned, out_v, out_a, chain = (sem(f"{name}_{s}", sc) for s in ("turned", "outv", "outa", "chain"))
                with nc.Block() as block:
                    @block.scalar
                    def _(a):
                        link = Chain(a, squared)
                        for t in range(tiles):
                            link(nc.scalar.activation(sq[:, :], src[:, t, :], ACT.Square, accum_out=stat[:, t:t + 1]))
                        nc.scalar.activation(stat[:, 8:8 + tiles], stat[:, 0:tiles], ACT.Sqrt, bias=eps,
                                             scale=1.0 / D).then_inc(rooted, 1)
                        for d in range(ND):
                            a.wait_ge(turned, d + 1)
                            scaled(False, dst[0][:, d, 0:tiles * P], bank[d][:, 0:tiles * P],
                                   gain[:, d:d + 1]).then_inc(out_a, 1)
                        split_high(a, state["used"] + SPLIT)

                    @block.vector
                    def _(v):
                        v.wait_ge(rooted, 1)
                        nc.vector.reciprocal(stat[:, 16:16 + tiles], stat[:, 8:8 + tiles]).then_inc(chain, 1)
                        v.wait_ge(chain, 1)
                        for t in range(tiles):
                            scaled(True, h[:, t, :], src[:, t, :], stat[:, 16 + t:17 + t]).then_inc(scaled_h, 1)
                        for d in range(ND):
                            v.wait_ge(out_a, d + 1)
                            nc.vector.scalar_tensor_tensor(dst[1][:, d, 0:tiles * P], bank[d][:, 0:tiles * P],
                                                           gain[:, d:d + 1], dst[0][:, d, 0:tiles * P],
                                                           ALU.mult, ALU.subtract).then_inc(out_v, 1)

                    @block.tensor
                    def _(pe):
                        pe.wait_ge(scaled_h, tiles)
                        for d in range(ND):
                            for t in range(tiles):
                                mm = nc.tensor.transpose(bank[d][:, t * P:(t + 1) * P],
                                                         h[:, t, d * P:(d + 1) * P], ident)
                            mm.then_inc(turned, 1)

                    @block.gpsimd
                    def _(g):
                        split_low(g, state["used"] + SPLIT)

                    @block.sync
                    def _(sp):
                        load_weights(sp, state["used"] + SPLIT)

        def token_stage(name, actT, kt, chunks, evac, engines, tiles=NT):
            n_v = sum(engines[:tiles])
            n_a = tiles - n_v
            slots, n = [], state["used"]
            for wname, width in chunks:
                per = -(-kt // (1024 // width))
                slots.append((n, per, width, wname))
                n += per
            with ExitStack() as sc:
                out_v, out_a = sem(f"{name}_outv", sc), sem(f"{name}_outa", sc)
                with nc.Block() as block:
                    @block.tensor
                    def _(pe):
                        for c, (n0, per, width, wname) in enumerate(slots):
                            base = 4 * (c % 2)
                            if c >= 2:
                                if n_v:
                                    pe.wait_ge(out_v, (c - 1) * n_v)
                                if n_a:
                                    pe.wait_ge(out_a, (c - 1) * n_a)
                            k = 0
                            for s in range(per):
                                wh, wl = tile_for(pe, n0 + s, wname)
                                for kk in range(plan[n0 + s][2]):
                                    for t in range(tiles):
                                        tok_ = slice(t * P, (t + 1) * P)
                                        mm = product(bank[base + t][:, 0:width],
                                                     (actT[0][:, k, tok_], actT[1][:, k, tok_]),
                                                     (wh[:, kk, :], wl[:, kk, :]), k == 0, k == kt - 1)
                                    k += 1
                                mm.then_inc(w_used, 1)
                            assert k == kt

                    def empty(eng, vector):
                        for c, (n0, per, width, _) in enumerate(slots):
                            if not vector:
                                split_high(eng, n0 + per + SPLIT - 1)
                            eng.wait_ge(w_used, n0 + per)
                            for t in range(tiles):
                                if engines[t] == vector:
                                    evac(c, t, bank[4 * (c % 2) + t][:, 0:width], vector)\
                                        .then_inc(out_v if vector else out_a, 1)

                    @block.vector
                    def _(v):
                        empty(v, True)

                    @block.scalar
                    def _(a):
                        if n_a:
                            empty(a, False)
                        split_high(a, n + SPLIT)

                    @block.gpsimd
                    def _(g):
                        split_low(g, n + SPLIT)

                    @block.sync
                    def _(sp):
                        load_weights(sp, n + SPLIT)
            state["used"] = n

        def feature_stage(name, actT, ncols, tiles, evac, kt=ND):
            n0 = state["used"]
            with ExitStack() as sc:
                out_e = [sem(f"{name}_outv", sc), sem(f"{name}_outa", sc)]
                with nc.Block() as block:
                    @block.tensor
                    def _(pe):
                        for i, wname in enumerate(tiles):
                            if i >= 8:
                                pe.wait_ge(out_e[i % 2], (i - 8) // 2 + 1)
                            wh, wl = tile_for(pe, n0 + i, wname)
                            for k in range(kt):
                                mm = product(bank[i % 8][:, 0:ncols], (wh[:, k, :], wl[:, k, :]),
                                             (actT[0][:, k, 0:ncols], actT[1][:, k, 0:ncols]), k == 0, k == kt - 1)
                            mm.then_inc(w_used, 1)

                    def empty(eng, parity):
                        for i in range(parity, len(tiles), 2):
                            if parity == 1:
                                split_high(eng, n0 + i + SPLIT)
                            eng.wait_ge(w_used, n0 + i + 1)
                            evac(i, bank[i % 8][:, 0:ncols], parity == 0).then_inc(out_e[parity], 1)

                    @block.vector
                    def _(v):
                        empty(v, 0)

                    @block.scalar
                    def _(a):
                        empty(a, 1)
                        split_high(a, n0 + len(tiles) + SPLIT)

                    @block.gpsimd
                    def _(g):
                        split_low(g, n0 + len(tiles) + SPLIT)

                    @block.sync
                    def _(sp):
                        load_weights(sp, n0 + len(tiles) + SPLIT)
            state["used"] = n0 + len(tiles)

        def turn_stage(name, blocks):
            with ExitStack() as sc:
                turned = sem(f"{name}_turned", sc)
                out_e = [sem(f"{name}_outv", sc), sem(f"{name}_outa", sc)]
                with nc.Block() as block:
                    @block.tensor
                    def _(pe):
                        for i, (src, _, _) in enumerate(blocks):
                            if i >= 8:
                                pe.wait_ge(out_e[i % 2], (i - 8) // 2 + 1)
                            for t in range(NT):
                                mm = nc.tensor.transpose(bank[i % 8][:, t * P:(t + 1) * P], src(t), ident)
                            mm.then_inc(turned, 1)

                    def empty(eng, parity):
                        for i in range(parity, len(blocks), 2):
                            _, dst, by = blocks[i]
                            eng.wait_ge(turned, i + 1)
                            scaled(parity == 0, dst, bank[i % 8][:, :], by).then_inc(out_e[parity], 1)

                    @block.vector
                    def _(v):
                        empty(v, 0)

                    @block.scalar
                    def _(a):
                        empty(a, 1)

        def turn_split_stage(name, blocks, extra=()):
            with ExitStack() as sc:
                turned, high = sem(f"{name}_turned", sc), sem(f"{name}_high", sc)
                sources = [(bank[i][:, :], dst) for i, (_, dst) in enumerate(blocks)] + list(extra)
                with nc.Block() as block:
                    @block.tensor
                    def _(pe):
                        for i, (src, _) in enumerate(blocks):
                            for t in range(NT):
                                mm = nc.tensor.transpose(bank[i][:, t * P:(t + 1) * P], src(t), ident)
                            mm.then_inc(turned, 1)

                    @block.scalar
                    def _(a):
                        for i, (src, dst) in enumerate(sources):
                            if i < len(blocks):
                                a.wait_ge(turned, i + 1)
                            copy(False, dst[0], src).then_inc(high, 1)

                    @block.vector
                    def _(v):
                        for i, (src, dst) in enumerate(sources):
                            v.wait_ge(high, i + 1)
                            nc.vector.tensor_tensor(dst[1], src, dst[0], ALU.subtract)

        def attention_stage(name, units, scratch):
            prob, probT = scratch
            n = len(units)
            with ExitStack() as sc:
                scored, peaked, exped, turned, summed, emptied, chain = (
                    sem(f"{name}_{s}", sc)
                    for s in ("scored", "peaked", "exped", "turned", "summed", "emptied", "chain"))
                copied = [sem(f"{name}_copied{i}", sc) for i in range(2)]
                npeak = [stat[:, 20 + i:21 + i] for i in range(3)]
                total = [stat[:, 24 + i:25 + i] for i in range(4)]

                with nc.Block() as block:
                    @block.tensor
                    def _(pe):
                        for s in range(n + 2):
                            if s < n:
                                if s >= 3:
                                    pe.wait_ge(exped, s - 2)
                                sc_ = units[s]["scores"]
                                for j, (c0, cn, lhsT, rhs) in enumerate(sc_):
                                    mm = nc.tensor.matmul(bank[s % 3][:, c0:c0 + cn], lhsT=lhsT, rhs=rhs,
                                                          start=(j == 0), stop=(j == len(sc_) - 1))
                                mm.then_inc(scored, 1)
                            u = s - 1
                            if 0 <= u < n:
                                pe.wait_ge(exped, u + 1)
                                if u >= 2:
                                    pe.wait_ge(copied[u % 2], u // 2)
                                for j, (c0, _) in enumerate(units[u]["keys"]):
                                    mm = nc.tensor.transpose(bank[3 + u % 2][:, j * P:(j + 1) * P],
                                                             prob[:, u % 3, c0:c0 + P], ident)
                                mm.then_inc(turned, 1)
                            u = s - 2
                            if u >= 0:
                                pe.wait_ge(copied[u % 2], u // 2 + 1)
                                if u >= 2:
                                    pe.wait_ge(emptied, u - 1)
                                keys = units[u]["keys"]
                                for j, (_, val) in enumerate(keys):
                                    mm = nc.tensor.matmul(bank[5 + u % 2][:, 0:val.shape[-1]],
                                                          lhsT=probT[:, u % 2, j * P:(j + 1) * P], rhs=val,
                                                          start=(j == 0), stop=(j == len(keys) - 1))
                                mm.then_inc(summed, 1)

                    def copy_turned(eng, u):
                        eng.wait_ge(turned, u + 1)
                        if u >= 2:
                            eng.wait_ge(summed, u - 1)
                        k = len(units[u]["keys"]) * P
                        copy(u % 2 == 0, probT[:, u % 2, 0:k], bank[3 + u % 2][:, 0:k]).then_inc(copied[u % 2], 1)

                    @block.vector
                    def _(v):
                        link = Chain(v, chain)
                        for s in range(n + 2):
                            if s < n:
                                v.wait_ge(scored, s + 1)
                                if s >= 3:
                                    v.wait_ge(exped, s - 2)
                                nc.vector.tensor_reduce(npeak[s % 3], bank[s % 3][:, 0:units[s]["width"]], AXX,
                                                        ALU.max, negate=True).then_inc(peaked, 1)
                            if 0 <= s - 1 < n and (s - 1) % 2 == 0:
                                copy_turned(v, s - 1)
                            u = s - 2
                            if u >= 0:
                                v.wait_ge(summed, u + 1)
                                units[u]["finish"](link, u, bank[5 + u % 2], total[u % 4]).then_inc(emptied, 1)

                    @block.scalar
                    def _(a):
                        for s in range(n + 1):
                            if s < n:
                                a.wait_ge(peaked, s + 1)
                                if s >= 3:
                                    a.wait_ge(turned, s - 2)
                                if s >= 4:
                                    a.wait_ge(emptied, s - 3)
                                wd = units[s]["width"]
                                nc.scalar.activation(prob[:, s % 3, 0:wd], bank[s % 3][:, 0:wd], ACT.Exp,
                                                     bias=npeak[s % 3], accum_out=total[s % 4]).then_inc(exped, 1)
                            if s >= 1 and (s - 1) % 2 == 1:
                                copy_turned(a, s - 1)

        recip = [stat[:, 30 + i:31 + i] for i in range(2)]
        coef = [stat[:, 32 + i:33 + i] for i in range(2)]

        def finish_plain(dst):
            def f(link, u, ps, total):
                link(nc.vector.reciprocal(recip[u % 2], total))
                return scaled(True, dst, ps[:, 0:dst.shape[-1]], recip[u % 2])
            return f

        def finish_gated(dst, gate):
            def f(link, u, ps, total):
                link(nc.vector.reciprocal(recip[u % 2], total))
                link(nc.vector.tensor_tensor(coef[u % 2], recip[u % 2], gate, ALU.mult))
                return nc.vector.scalar_tensor_tensor(dst, ps[:, 0:HD], coef[u % 2], dst, ALU.mult, ALU.add)
            return f

        def residual_add(c, t, ps, vector):
            dst = x[:, t, c * BANK:(c + 1) * BANK]
            return nc.vector.tensor_tensor(dst, dst, ps, ALU.add)

        load_stage()
        norm_stage("anorm", x, NT, par[:, K_ANORM:], (hT, hL))

        mixers = ctx.enter_context(ExitStack())
        convT = sb("convT", [P, 2, S], mixers)
        yt = sb("yt", [P, NT, D], mixers)
        inner = ExitStack()
        tokv = sb("tokv", [P, NT, 896], inner)
        qkT = sb("qkT", [P, 13, S], inner)
        toep = sb("toep", [P, SWA_H, 256], inner)
        rows = sb("rows", [P, 2, S], inner)
        mcol = sb("mcol", [P, 2, NT, ML_H], inner)
        gain_h = sb("gain_h", [P, 256], inner)
        sinks = sb("sinks", [1, SWA_H], inner)

        normed = ExitStack()
        tokqk = sb("tokqk", [P, NT, 1152], normed)
        pieces_a = [[(0, 512, tokqk, 0)], [(0, 256, tokv, 0)], [(0, 256, tokv, 256)], [(0, 256, tokv, 512)],
                    [(0, 512, tokqk, 512)], [(0, 128, tokqk, 1024), (128, 128, tokv, 768)]]

        def evac_pieces(pieces):
            def f(c, t, ps, vector):
                for s0, wd, dst, d0 in pieces[c]:
                    ins = copy(vector, dst[:, t, d0:d0 + wd], ps[:, s0:s0 + wd])
                return ins
            return f

        half = [True, False, True, False]
        token_stage("projA", (hT, hL), ND, [('w_in', n) for _, n in TOKEN_CHUNKS_A], evac_pieces(pieces_a), half)

        def qk_norm_stage():
            nh = NT * 18
            flat = tokqk[:, :, :].rearrange("p t (h d) -> p (t h) d", d=HD)
            sqr = yt[:, :, :].rearrange("p a b -> p (a b)")[:, 0:3 * 1152].rearrange("p (h d) -> p h d", d=HD)
            with ExitStack() as sc:
                ssum, rooted, chain = sem("qkn_sum", sc), sem("qkn_root", sc), sem("qkn_chain", sc)
                with nc.Block() as block:
                    @block.vector
                    def _(v):
                        link = Chain(v, chain)
                        for h0, hn in ((0, 54), (54, 18)):
                            part_ = flat[:, h0:h0 + hn, :]
                            link(nc.vector.tensor_tensor(sqr[:, 0:hn, :], part_, part_, ALU.mult))
                            link(nc.vector.tensor_reduce(stat[:, h0:h0 + hn], sqr[:, 0:hn, :], AXX, ALU.add))
                        nc.vector.tensor_copy(stat[:, 146:147], stat[:, nh - 1:nh]).then_inc(ssum, 1)
                        nc.vector.tensor_scalar(stat[:, 148:149], par[:, K_FQ:K_FQ + 1], HD ** -0.5, None, ALU.mult)
                        nc.vector.tensor_scalar(stat[:, 149:150], par[:, K_SQ:K_SQ + 1], HD ** -0.5, None, ALU.mult)
                        v.wait_ge(rooted, 1)
                        link(nc.vector.reciprocal(stat[:, 0:nh], stat[:, 72:72 + nh]))
                        by = stat[:, 0:nh].unsqueeze(2).to_broadcast([P, nh, HD])
                        nc.vector.tensor_tensor(flat, flat, by, ALU.mult)

                    @block.scalar
                    def _(a):
                        a.wait_ge(ssum, 1)
                        nc.scalar.activation(stat[:, 72:72 + nh], stat[:, 0:nh], ACT.Sqrt, bias=eps,
                                             scale=1.0 / HD).then_inc(rooted, 1)

        qk_norm_stage()

        def tok(tile, c0):
            return lambda t: tile[:, t, c0:c0 + P]

        turn_stage("qkT", [(tok(tokqk, 0), qkT[:, 0, :], stat[:, 148:149]), (tok(tokqk, P), qkT[:, 1, :], stat[:, 148:149]),
                           (tok(tokqk, 256), qkT[:, 2, :], par[:, K_FK:K_FK + 1]),
                           (tok(tokqk, 384), qkT[:, 3, :], par[:, K_FK:K_FK + 1])]
                   + [(tok(tokqk, 512 + i * P), qkT[:, 8 + i, :], stat[:, 149:150]) for i in range(4)]
                   + [(tok(tokqk, 1024), qkT[:, 12, :], par[:, K_SK:K_SK + 1])])
        normed.close()

        conv = ExitStack()
        cx = sb("cx", [P, 6, 514], conv)
        wsm = sb("wsm", [P, ND, 96], conv)
        wsh = sb("wsh", [P, ND, 96], conv, F32R)
        wsl = sb("wsl", [P, ND, 96], conv, F32R)
        rb = sb("rb", [P, 3, S], conv)
        relT = sb("relT", [BUCKETS + 1, SWA_H], conv)
        biasrow = sb("biasrow", [SWA_H, 384], conv)

        def evac_feat(i, ps, vector):
            if i < 2:
                return scaled(vector, qkT[:, 4 + i, :], ps, HD ** -0.5) if vector else \
                    nc.scalar.activation(qkT[:, 4 + i, :], ps, ACT.Copy, scale=HD ** -0.5)
            if i < 4:
                return copy(vector, qkT[:, 4 + i, :], ps)
            return copy(vector, cx[:, i - 4, 2:514], ps)

        feature_stage("projAT", (hT, hL), S, ['w_in'] * 10, evac_feat)

        scratch_bias = w['bias_rows']

        def small_stage():
            with ExitStack() as sc:
                names = ("zeroed", "cols_in", "misc", "logits", "logits_in", "absed", "exped", "logged", "bias_mm",
                         "bias_row", "bias_out", "toep_in", "chain", "scanned", "turned", "achain", "ws_split")
                s = {k: sem(f"small_{k}", sc) for k in names}
                with nc.Block() as block:
                    @block.gpsimd
                    def _(g):
                        nc.gpsimd.memset(wsm[:, :, :], 0.0).then_inc(s["zeroed"], 1)
                        g.wait_ge(s["zeroed"], 1)
                        nc.gpsimd.memset(relT[BUCKETS:BUCKETS + 1, :], 1.0).then_inc(s["zeroed"], 1)

                    @block.sync
                    def _(sp):
                        sp.wait_ge(s["zeroed"], 2)
                        wv = w['w_in'].rearrange("(k p) c -> p k c", p=P)
                        for at, c0 in ((0, FF), (32, MI), (64, MF)):
                            sp.dma_start(wsm[:, :, at:at + 4], wv[:, :, c0:c0 + 4]).then_inc(s["cols_in"], 16)
                        sp.dma_start(relT[0:BUCKETS, :], w['rel_bias']).then_inc(s["misc"], 16)
                        sp.dma_start(gain_h[:, :], w['mlstm_h_gain'].to_broadcast([P, 256])).then_inc(s["misc"], 16)
                        sp.dma_start(sinks[:, :], w['swa_sinks']).then_inc(s["misc"], 16)
                        sp.wait_ge(s["bias_row"], 1)
                        sp.dma_start(scratch_bias, biasrow[:, :]).then_inc(s["bias_out"], 16)
                        sp.wait_ge(s["bias_out"], 16)
                        skew = bass.AP(tensor=scratch_bias.tensor, offset=scratch_bias.offset,
                                       ap=[[1, P], [384, SWA_H], [1, 256]])
                        sp.dma_start(toep[:, :, :], skew).then_inc(s["toep_in"], 16)
                        sp.wait_ge(s["toep_in"], 16)
                        sp.wait_ge(s["misc"], 48)

                    @block.tensor
                    def _(pe):
                        pe.wait_ge(s["ws_split"], 2)
                        for k in range(ND):
                            mm = product(bank[0][0:96, :], (wsh[:, k, :], wsl[:, k, :]), (hT[:, k, :], hL[:, k, :]),
                                         k == 0, k == ND - 1)
                        mm.then_inc(s["logits"], 1)
                        pe.wait_ge(s["misc"], 48)
                        pe.wait_ge(s["zeroed"], 2)
                        nc.tensor.matmul(bank[1][0:SWA_H, 0:384], lhsT=relT[:, :],
                                         rhs=const[0:BUCKETS + 1, C_OH:C_OH + 384],
                                         start=True, stop=True).then_inc(s["bias_mm"], 1)
                        pe.wait_ge(s["scanned"], 1)
                        for i in range(2):
                            for t in range(NT):
                                mm = nc.tensor.transpose(bank[2 + i][:, t * 4:t * 4 + 4],
                                                         rb[32:36, i, t * P:(t + 1) * P],
                                                         const[32:36, C_ID + 32:C_ID + 36])
                        mm.then_inc(s["turned"], 1)

                    @block.scalar
                    def _(a):
                        a.wait_ge(s["logits"], 1)
                        nc.scalar.activation(rb[0:96, 0, :], bank[0][0:96, :], ACT.Identity,
                                             bias=par[0:96, K_BIAS:K_BIAS + 1]).then_inc(s["logits_in"], 1)
                        link = Chain(a, s["achain"])
                        a.wait_ge(s["logits_in"], 1)
                        link(nc.scalar.activation(rb[0:96, 1, :], rb[0:96, 0, :], ACT.Abs))
                        link(nc.scalar.activation(rb[0:96, 1, :], rb[0:96, 1, :], ACT.Exp, scale=-1.0))
                        nc.scalar.activation(rb[0:96, 2, :], rb[0:96, 1, :], ACT.Ln, bias=1.0).then_inc(s["logged"], 1)
                        a.wait_ge(s["bias_mm"], 1)
                        nc.scalar.activation(biasrow[:, :], bank[1][0:SWA_H, 0:384], ACT.Copy).then_inc(s["bias_row"], 1)

                    @block.vector
                    def _(v):
                        link = Chain(v, s["chain"])
                        v.wait_ge(s["cols_in"], 48)
                        nc.vector.tensor_copy(wsh[:, :, :], wsm[:, :, :]).then_inc(s["ws_split"], 1)
                        v.wait_ge(s["ws_split"], 1)
                        nc.vector.tensor_tensor(wsl[:, :, :], wsm[:, :, :], wsh[:, :, :], ALU.subtract).then_inc(s["ws_split"], 1)
                        nc.vector.memset(cx[:, 2:4, 0:2], 0.0)
                        link(nc.vector.tensor_tensor(cx[:, 2:4, 2:514], cx[:, 2:4, 2:514], cx[:, 0:2, 2:514], ALU.mult))
                        for i in range(2):
                            z = cx[:, 2 + i, :]
                            tap = [par[:, K_CONV + 2 * j + i:K_CONV + 2 * j + i + 1] for j in range(3)]
                            link(nc.vector.tensor_scalar(convT[:, i, :], z[:, 2:514], tap[2], None, ALU.mult))
                            link(nc.vector.scalar_tensor_tensor(convT[:, i, :], z[:, 1:513], tap[1], convT[:, i, :], ALU.mult, ALU.add))
                            link(nc.vector.scalar_tensor_tensor(convT[:, i, :], z[:, 0:512], tap[0], convT[:, i, :], ALU.mult, ALU.add))
                            nc.vector.tensor_tensor(convT[:, i, :], convT[:, i, :], cx[:, 4 + i, 2:514], ALU.mult)
                        v.wait_ge(s["logged"], 1)
                        link(nc.vector.tensor_scalar(rb[0:96, 1, :], rb[0:96, 0, :], 0.0, None, ALU.min))
                        link(nc.vector.tensor_tensor(rb[0:96, 1, :], rb[0:96, 1, :], rb[0:96, 2, :], ALU.subtract))
                        link(nc.vector.tensor_tensor_scan(rb[0:96, 2, :], rb[0:96, 1, :], rb[0:96, 1, :], 0.0,
                                                          ALU.add, ALU.bypass))
                        nc.vector.tensor_scalar(rows[0:4, 0, :], rb[0:4, 2, :], -1.0, None, ALU.mult)
                        link(nc.vector.tensor_copy(rb[32:36, 1, :], rb[64:68, 2, :]))
                        link(nc.vector.tensor_tensor(rb[32:36, 0, :], rb[32:36, 0, :], rb[32:36, 1, :], ALU.subtract))
                        link(nc.vector.tensor_tensor_scan(rb[32:36, 2, :], rb[32:36, 0, :], rb[32:36, 0, :], 0.0,
                                                          ALU.max, ALU.bypass))
                        link(nc.vector.tensor_scalar(rows[32:36, 1, :], rb[32:36, 2, :], -1.0, None, ALU.mult))
                        nc.vector.tensor_tensor(rb[32:36, 1, :], rows[32:36, 1, :], rb[32:36, 1, :],
                                                ALU.subtract).then_inc(s["scanned"], 1)
                        v.wait_ge(s["turned"], 1)
                        for i in range(2):
                            nc.vector.tensor_copy(mcol[:, i, :, :], bank[2 + i][:, 0:16].rearrange("p (t h) -> p t h", h=4))

        small_stage()
        conv.close()

        attn = ExitStack()
        prob = sb("prob", [P, 3, 514], attn)
        probT = sb("probT", [P, 2, S], attn)
        scratch = (prob, probT)

        def part(h):
            return slice(HD * (h % 2), HD * (h % 2) + HD)

        def q_tile(t):
            return slice(t * P, (t + 1) * P)

        fox_units = []
        for t in range(NT):
            for h in range(FOX_H):
                wd = (t + 1) * P
                fox_units.append({
                    "width": wd,
                    "scores": [(0, wd, qkT[part(h), h // 2, q_tile(t)], qkT[part(h), 2 + h // 2, 0:wd]),
                               (0, wd, const[0:4, C_SEL + h * P:C_SEL + (h + 1) * P], rows[0:4, 0, 0:wd]),
                               (t * P, P, ident, mask_q)],
                    "keys": [(j * P, tokv[:, j, h * HD:(h + 1) * HD]) for j in range(t + 1)],
                    "finish": finish_plain(yt[:, t, h * HD:(h + 1) * HD])})
        attention_stage("fox", fox_units, scratch)

        swa_units = []
        for t in range(NT):
            for h in range(SWA_H):
                g, i = h // 4, h % 4
                k0 = max(t - 1, 0)
                nk = (t + 1 - k0) * P
                hp = slice(HD * g, HD * g + HD)
                swa_units.append({
                    "width": nk + 1,
                    "scores": [(0, nk, qkT[hp, 8 + i, q_tile(t)], qkT[hp, 12, k0 * P:k0 * P + nk]),
                               (0, nk, anti, toep[:, h, 256 - nk:256]),
                               (nk, 1, const[0:1, C_ONE:C_ONE + P], sinks[0:1, h:h + 1])],
                    "keys": [(j * P, tokv[:, k0 + j, 768 + g * HD:768 + (g + 1) * HD]) for j in range(nk // P)],
                    "finish": finish_plain(yt[:, t, 512 + h * HD:512 + (h + 1) * HD])})
        attention_stage("swa", swa_units, scratch)

        attn.close()
        ml = ExitStack()
        v1 = sb("v1", [P, NT, ML_H, HD + 1], ml)
        sw = sb("sw", [P, 2, 10 * P], ml)
        sw_at = [0, 4 * P, 7 * P, 9 * P]
        decay = sb("decay", [P, 2, S], ml)

        def mlstm_stage():
            n = ML_H * NT
            ocol = HD + 1
            with ExitStack() as sc:
                ones_in, qk, dec, dexp, weighted, summed, taken = (
                    sem(f"ml_{k}", sc) for k in ("ones", "qk", "dec", "dexp", "weighted", "summed", "taken"))
                with nc.Block() as block:
                    @block.gpsimd
                    def _(g):
                        nc.gpsimd.tensor_copy(v1[:, :, :, 0:HD],
                                              tokv[:, :, 256:512].rearrange("p t (h d) -> p t h d", d=HD)).then_inc(ones_in, 1)
                        g.wait_ge(ones_in, 1)
                        nc.gpsimd.memset(v1[:, :, :, HD:HD + 1], 1.0).then_inc(ones_in, 1)

                    @block.tensor
                    def _(pe):
                        def values(h):
                            pe.wait_ge(weighted, NT * (h + 1))
                            if h >= 2:
                                pe.wait_ge(taken, h - 1)
                            for t in range(NT):
                                for j in range(t + 1):
                                    mm = nc.tensor.matmul(bank[4 + h % 2][:, t * ocol:(t + 1) * ocol],
                                                          lhsT=sw[:, h % 2, sw_at[j] + (t - j) * P:sw_at[j] + (t - j + 1) * P], rhs=v1[:, j, h, :],
                                                          start=(j == 0), stop=(j == t))
                            mm.then_inc(summed, 1)

                        pe.wait_ge(ones_in, 2)
                        for h in range(ML_H):
                            hp = part(h)
                            for j in range(NT):
                                u = h * NT + j
                                if u >= 2:
                                    pe.wait_ge(weighted, u - 1)
                                c0 = j * P
                                nc.tensor.matmul(bank[2 + u % 2][:, c0:S], lhsT=const[32:36, C_SEL + h * P:C_SEL + (h + 1) * P],
                                                 rhs=rows[32:36, 1, c0:S], start=True, stop=False)
                                nc.tensor.matmul(bank[2 + u % 2][:, c0:c0 + P], lhsT=ident, rhs=mask_t,
                                                 start=False, stop=True).then_inc(dec, 1)
                                nc.tensor.matmul(bank[u % 2][:, c0:S], lhsT=qkT[hp, 6 + h // 2, q_tile(j)],
                                                 rhs=qkT[hp, 4 + h // 2, c0:S], start=True, stop=True).then_inc(qk, 1)
                            if h >= 1:
                                values(h - 1)
                        values(ML_H - 1)

                    @block.scalar
                    def _(a):
                        for u in range(n):
                            h, j = u // NT, u % NT
                            a.wait_ge(dec, u + 1)
                            if u >= 2:
                                a.wait_ge(weighted, u - 1)
                            nc.scalar.activation(decay[:, u % 2, j * P:S], bank[2 + u % 2][:, j * P:S], ACT.Exp,
                                                 bias=mcol[:, 0, j, h:h + 1]).then_inc(dexp, 1)

                    @block.vector
                    def _(v):
                        def take(h):
                            v.wait_ge(summed, h + 1)
                            nc.vector.tensor_copy(ho[:, h, :, :],
                                                  bank[4 + h % 2][:, 0:NT * ocol].rearrange("p (t c) -> p t c", c=ocol)).then_inc(taken, 1)

                        for h in range(ML_H):
                            for j in range(NT):
                                u = h * NT + j
                                v.wait_ge(qk, u + 1)
                                v.wait_ge(dexp, u + 1)
                                if h >= 2:
                                    v.wait_ge(summed, h - 1)
                                nc.vector.tensor_tensor(sw[:, h % 2, sw_at[j]:sw_at[j] + S - j * P], bank[u % 2][:, j * P:S],
                                                        decay[:, u % 2, j * P:S], ALU.mult).then_inc(weighted, 1)
                            if h >= 2:
                                take(h - 2)
                        take(ML_H - 2)
                        take(ML_H - 1)

        ho = sb("ho", [P, ML_H, NT, HD + 1], ml)
        hh = sb("hh", [P, ML_H, NT, HD], ml)
        hs = sb("hs", [P, ML_H, NT, HD], ml)
        mlstm_stage()

        def mlstm_out_stage():
            nht = ML_H * NT
            with ExitStack() as sc:
                em, sums, root, sig, chain = (sem(f"mo_{k}", sc) for k in ("em", "sums", "root", "sig", "chain"))
                with nc.Block() as block:
                    @block.scalar
                    def _(a):
                        nc.scalar.activation(stat[:, 0:nht].rearrange("p (h t) -> p h t", t=NT),
                                             mcol[:, 1, :, :].rearrange("p t h -> p h t"), ACT.Exp).then_inc(em, 1)
                        den = ho[:, :, :, HD:HD + 1].rearrange("p h t o -> p (h t o)")
                        nc.scalar.activation(stat[:, 48:48 + nht], den, ACT.Abs).then_inc(em, 1)
                        a.wait_ge(sums, 1)
                        nc.scalar.activation(stat[:, 32:32 + nht], stat[:, 16:16 + nht], ACT.Sqrt, bias=eps,
                                             scale=1.0 / HD).then_inc(root, 1)
                        nc.scalar.activation(tokv[:, :, 512:768], tokv[:, :, 512:768], ACT.Sigmoid).then_inc(sig, 1)

                    @block.vector
                    def _(v):
                        link = Chain(v, chain)
                        v.wait_ge(em, 2)
                        link(nc.vector.tensor_tensor(stat[:, 48:48 + nht], stat[:, 48:48 + nht], stat[:, 0:nht], ALU.max))
                        link(nc.vector.reciprocal(stat[:, 64:64 + nht], stat[:, 48:48 + nht]))
                        num = ho[:, :, :, 0:HD].rearrange("p h t d -> p (h t) d")
                        hv = hh[:, :, :, :].rearrange("p h t d -> p (h t) d")
                        hq = hs[:, :, :, :].rearrange("p h t d -> p (h t) d")
                        link(nc.vector.tensor_tensor(hv, num, stat[:, 64:64 + nht].unsqueeze(2).to_broadcast([P, nht, HD]), ALU.mult))
                        link(nc.vector.tensor_tensor(hq, hv, hv, ALU.mult))
                        nc.vector.tensor_reduce(stat[:, 16:16 + nht], hq, AXX, ALU.add).then_inc(sums, 1)
                        v.wait_ge(root, 1)
                        link(nc.vector.reciprocal(stat[:, 80:80 + nht], stat[:, 32:32 + nht]))
                        link(nc.vector.tensor_tensor(hv, hv, stat[:, 80:80 + nht].unsqueeze(2).to_broadcast([P, nht, HD]), ALU.mult))
                        v.wait_ge(sig, 1)
                        for t in range(NT):
                            link(nc.vector.tensor_tensor(hs[:, :, t, :], hh[:, :, t, :],
                                                         gain_h[:, :].rearrange("p (h d) -> p h d", d=HD), ALU.mult))
                            nc.vector.tensor_tensor(yt[:, t, 256:512].rearrange("p (h d) -> p h d", d=HD), hs[:, :, t, :],
                                                    tokv[:, t, 512:768].rearrange("p (h d) -> p h d", d=HD), ALU.mult)

        mlstm_out_stage()
        ml.close()
        inner.close()

        merge = ExitStack()
        yT = sb("yT", [P, 10, S], merge, F32R)
        yL = sb("yL", [P, 10, S], merge, F32R)
        turn_split_stage("yT", [(tok(yt, c * P), (yT[:, y, :], yL[:, y, :]))
                                for c, y in enumerate((0, 1, 4, 5, 6, 7, 8, 9))],
                         [(convT[:, i, :], (yT[:, 2 + i, :], yL[:, 2 + i, :])) for i in range(2)])
        mT = sb("mT", [P, ND, S], merge, F32R)
        mL = sb("mL", [P, ND, S], merge, F32R)
        gate = sb("gate", [P, 4, S], merge)
        branch_tiles = ((0, 1), (2, 3), (4, 5), (6, 7, 8, 9))
        branch_w = ('w_fox_out', 'w_conv_out', 'w_mlstm_out', 'w_swa_out')

        def merge_stage():
            n0 = state["used"]
            n = ND * N_BRANCH
            with ExitStack() as sc:
                sig, merged, total, high, low, chain = (
                    sem(f"mg_{k}", sc) for k in ("sig", "merged", "total", "high", "low", "chain"))

                def gate_tile(d, b):
                    return n0 + 8 * d + b

                def out_tile(d, b):
                    return n0 + 8 * d + 4 + b

                with nc.Block() as block:
                    @block.tensor
                    def _(pe):
                        for d in range(ND):
                            for b in range(N_BRANCH):
                                if d:
                                    pe.wait_ge(sig, (d - 1) * 4 + b + 1)
                                wh, wl = tile_for(pe, gate_tile(d, b), 'w_in')
                                for k in range(ND):
                                    mm = product(bank[b][:, :], (wh[:, k, :], wl[:, k, :]), (hT[:, k, :], hL[:, k, :]),
                                                 k == 0, k == ND - 1)
                                mm.then_inc(w_used, 1)
                            for b in range(N_BRANCH):
                                if d:
                                    pe.wait_ge(merged, (d - 1) * 4 + b + 1)
                                wh, wl = tile_for(pe, out_tile(d, b), branch_w[b])
                                kt = len(branch_tiles[b])
                                for k, y in enumerate(branch_tiles[b]):
                                    mm = product(bank[4 + b][:, :], (wh[:, k, :], wl[:, k, :]), (yT[:, y, :], yL[:, y, :]),
                                                 k == 0, k == kt - 1)
                                mm.then_inc(w_used, 1)

                    @block.scalar
                    def _(a):
                        def high_part(d):
                            a.wait_ge(total, d + 1)
                            copy(False, mT[:, d, :], gate[:, 0, :]).then_inc(high, 1)

                        for u in range(n):
                            d, b = u // 4, u % 4
                            if b == 0 and d:
                                split_high(a, out_tile(d - 1, 3) + SPLIT)
                                high_part(d - 1)
                                a.wait_ge(low, d)
                            split_high(a, gate_tile(d, b) + SPLIT)
                            a.wait_ge(w_used, gate_tile(d, b) + 1)
                            nc.scalar.activation(gate[:, b, :], bank[b][:, :], ACT.Sigmoid).then_inc(sig, 1)
                        split_high(a, out_tile(ND - 1, 3) + SPLIT)
                        high_part(ND - 1)
                        split_high(a, n0 + 8 * ND + SPLIT)

                    @block.gpsimd
                    def _(g):
                        split_low(g, n0 + 8 * ND + SPLIT)

                    @block.vector
                    def _(v):
                        link = Chain(v, chain)
                        for u in range(n):
                            d, b = u // 4, u % 4
                            v.wait_ge(sig, u + 1)
                            v.wait_ge(w_used, out_tile(d, b) + 1)
                            nc.vector.tensor_tensor(gate[:, b, :], gate[:, b, :], bank[4 + b][:, :], ALU.mult).then_inc(merged, 1)
                            v.wait_ge(merged, u + 1)
                            if b in (1, 2):
                                link(nc.vector.tensor_tensor(gate[:, 0, :], gate[:, 0, :], gate[:, b, :], ALU.add))
                            if b == 3:
                                nc.vector.tensor_tensor(gate[:, 0, :], gate[:, 0, :], gate[:, 3, :], ALU.add).then_inc(total, 1)
                                v.wait_ge(high, d + 1)
                                nc.vector.tensor_tensor(mL[:, d, :], gate[:, 0, :], mT[:, d, :], ALU.subtract).then_inc(low, 1)

                    @block.sync
                    def _(sp):
                        load_weights(sp, n0 + 8 * ND + SPLIT)
            state["used"] = n0 + 8 * ND

        merge_stage()
        all_v = [True] * NT
        token_stage("wmerge", (mT, mL), ND, [('w_merge_out', BANK)] * 2, residual_add, all_v)
        merge.close()
        mixers.close()

        def ffn_stage(name, gate_w, up_w, actT, taps, f0):
            n0 = state["used"]
            with ExitStack() as sc:
                g = sb(f"{name}_g", [P, 2, S + 2], sc)
                cv = sb(f"{name}_cv", [P, 2, S], sc)
                sl = sb(f"{name}_sl", [P, 2, S], sc)
                ac = sb(f"{name}_ac", [P, 2, S], sc)
                silued, acted, copied, convd, high, low, chain = (
                    sem(f"{name}_{k}", sc) for k in ("silued", "acted", "copied", "convd", "high", "low", "chain"))
                with nc.Block() as block:
                    @block.tensor
                    def _(pe):
                        for f in range(FG):
                            for i, wname in enumerate((gate_w, up_w)):
                                if f >= 4:
                                    pe.wait_ge(acted, f - 3)
                                wh, wl = tile_for(pe, n0 + 2 * f + i, wname)
                                for k in range(ND):
                                    mm = product(bank[2 * (f % 4) + i][:, :], (wh[:, k, :], wl[:, k, :]),
                                                 (hT[:, k, :], hL[:, k, :]), k == 0, k == ND - 1)
                                mm.then_inc(w_used, 1)

                    @block.scalar
                    def _(a):
                        def high_part(f):
                            a.wait_ge(acted, f + 1)
                            copy(False, actT[0][:, f, :], ac[:, f % 2, :]).then_inc(high, 1)

                        for f in range(FG):
                            split_high(a, n0 + 2 * f + SPLIT)
                            a.wait_ge(w_used, n0 + 2 * f + 1)
                            src = bank[2 * (f % 4)][:, :]
                            if taps is not None:
                                if f >= 2:
                                    a.wait_ge(convd, f - 1)
                                nc.scalar.activation(g[:, f % 2, 2:], src, ACT.Copy).then_inc(copied, 1)
                                a.wait_ge(convd, f + 1)
                                src = cv[:, f % 2, :]
                            if f >= 2:
                                a.wait_ge(acted, f - 1)
                            nc.scalar.activation(sl[:, f % 2, :], src, ACT.Silu).then_inc(silued, 1)
                            split_high(a, n0 + 2 * f + 1 + SPLIT)
                            if f >= 1:
                                high_part(f - 1)
                        high_part(FG - 1)
                        split_high(a, n0 + 2 * FG + SPLIT)

                    @block.vector
                    def _(v):
                        link = Chain(v, chain)
                        if taps is not None:
                            link(nc.vector.memset(g[:, :, 0:2], 0.0))

                        def low_part(f):
                            v.wait_ge(high, f + 1)
                            nc.vector.tensor_tensor(actT[1][:, f, :], ac[:, f % 2, :], actT[0][:, f, :],
                                                    ALU.subtract).then_inc(low, 1)

                        for f in range(FG):
                            if taps is not None:
                                v.wait_ge(copied, f + 1)
                                if f >= 2:
                                    v.wait_ge(silued, f - 1)
                                c = cv[:, f % 2, :]
                                link(nc.vector.tensor_scalar(c, g[:, f % 2, 2:514], taps(2, f0 + f), None, ALU.mult))
                                link(nc.vector.scalar_tensor_tensor(c, g[:, f % 2, 1:513], taps(1, f0 + f), c, ALU.mult, ALU.add))
                                nc.vector.scalar_tensor_tensor(c, g[:, f % 2, 0:512], taps(0, f0 + f), c,
                                                               ALU.mult, ALU.add).then_inc(convd, 1)
                            v.wait_ge(silued, f + 1)
                            v.wait_ge(w_used, n0 + 2 * f + 2)
                            if f >= 2:
                                v.wait_ge(low, f - 1)
                            nc.vector.tensor_tensor(ac[:, f % 2, :], sl[:, f % 2, :], bank[2 * (f % 4) + 1][:, :],
                                                    ALU.mult).then_inc(acted, 1)
                            if f >= 1:
                                low_part(f - 1)
                        low_part(FG - 1)

                    @block.gpsimd
                    def _(g_):
                        split_low(g_, n0 + 2 * FG + SPLIT)

                    @block.sync
                    def _(sp):
                        load_weights(sp, n0 + 2 * FG + SPLIT)
            state["used"] = n0 + 2 * FG

        def ffn(name, gain, gate_w, up_w, down_w, taps):
            norm_stage(f"{name}n", x, NT, gain, (hT, hL))
            with ExitStack() as sc:
                actT = tuple(sb(f"{name}_act{i}", [P, FG, S], sc, F32R) for i in range(2))
                for f0 in range(0, NF, FG):
                    ffn_stage(f"{name}u{f0}", gate_w, up_w, actT, taps, f0)
                    token_stage(f"{name}d{f0}", actT, FG, [(down_w, BANK)] * 2, residual_add, all_v)

        ffn("ffn1", par[:, K_FNORM:], 'w_gate', 'w_up', 'w_down', None)

        clear_stage()

        norm_stage("mix", x, NT, par[:, K_MIX:], (hT, hL))
        nsa = ExitStack()
        ot = sb("ot", [P, NT, D], nsa)
        nq = sb("nq", [P, 8, S], nsa)
        nkT = sb("nkT", [P, 4, S], nsa)
        nv = sb("nv", [P, NT, 560], nsa)
        kcmp = sb("kcmp", [P, NSA_G, 32], nsa)
        vcmp = sb("vcmp", [P, NSA_G, 256], nsa)
        cmp_s = ExitStack()
        kcp = sb("kcp", [P, 2, 8, 132], cmp_s)
        blkh = sb("blkh", [P, 8, P], cmp_s, F32R)
        blkl = sb("blkl", [P, 8, P], cmp_s, F32R)
        hid = sb("hid", [P, 2, CMP_HID], cmp_s)
        hidT = sb("hidT", [P, 4, P], cmp_s)
        w2k = sb("w2k", [P, 2, P], cmp_s)
        w2v = sb("w2v", [P, 2, HD], cmp_s)

        def nsa_q_stage():
            n0 = state["used"]
            with ExitStack() as sc:
                out_v, out_a = sem("nq_outv", sc), sem("nq_outa", sc)
                with nc.Block() as block:
                    @block.tensor
                    def _(pe):
                        for a in range(2):
                            for s in range(4):
                                wh, wl = tile_for(pe, n0 + 4 * a + s, 'nsa_w_in_2')
                                for kk in range(2):
                                    k = 2 * s + kk
                                    for i in range(HPG):
                                        mm = product(bank[4 * a + i][:, :],
                                                     (wh[:, kk, i * P:(i + 1) * P], wl[:, kk, i * P:(i + 1) * P]),
                                                     (hT[:, k, :], hL[:, k, :]), k == 0, k == ND - 1)
                                mm.then_inc(w_used, 1)

                    @block.vector
                    def _(v):
                        for a in range(2):
                            v.wait_ge(w_used, n0 + 4 * a + 4)
                            for i in (0, 1):
                                scaled(True, nq[:, 4 * a + i, :], bank[4 * a + i][:, :], HD ** -0.5).then_inc(out_v, 1)

                    @block.scalar
                    def _(e):
                        for a in range(2):
                            split_high(e, n0 + 4 * a + 3 + SPLIT)
                            e.wait_ge(w_used, n0 + 4 * a + 4)
                            for i in (2, 3):
                                nc.scalar.activation(nq[:, 4 * a + i, :], bank[4 * a + i][:, :], ACT.Copy,
                                                     scale=HD ** -0.5).then_inc(out_a, 1)

                        split_high(e, n0 + 8 + SPLIT)

                    @block.gpsimd
                    def _(g):
                        split_low(g, n0 + 8 + SPLIT)

                    @block.sync
                    def _(sp):
                        load_weights(sp, n0 + 8 + SPLIT)
            state["used"] = n0 + 8

        nsa_q_stage()

        def evac_kc(i, ps, vector):
            kv, pair = i // 2, i % 2
            for j in range(2):
                g = 2 * pair + j
                src = ps[HD * j:HD * j + HD, :].rearrange("p (n q e) -> p e q n", q=8, e=2)
                for e in range(2):
                    ins = copy(vector, kcp[HD * e:HD * e + HD, kv, :, g * 32:(g + 1) * 32], src[:, e, :, :])
            return ins

        feature_stage("nsaC", (hT, hL), S, ['nsa_w_in_2'] * 4, evac_kc)
        feature_stage("nsaT", (hT, hL), S, ['nsa_w_in_2'] * 4, lambda i, ps, vec: copy(vec, nkT[:, i, :], ps))

        def evac_nsa_tok(c, t, ps, vector):
            return copy(vector, nv[:, t, c * 256:c * 256 + ps.shape[-1]], ps)

        token_stage("nsaV", (hT, hL), ND, [('nsa_w_in_2', 256), ('nsa_w_in_2', 304)], evac_nsa_tok, half)

        def compress_stage():
            n0 = state["used"]
            units = 32
            with ExitStack() as sc:
                w2_in, high, low, act, turned, taken, second, zeroed, gated = (
                    sem(f"cmp_{k}", sc) for k in ("w2", "high", "low", "act", "turned", "taken", "second", "zeroed", "gated"))

                def block_of(u):
                    kv, m = u // 16, u % 16
                    return kcp[:, kv, m % 8, m // 8:m // 8 + P], par[:, K_PEK + u:K_PEK + u + 1]

                with nc.Block() as block:
                    @block.sync
                    def _(sp):
                        kw = w['nsa_ck_w2_2'].rearrange("(k p) c -> p k c", p=P)
                        sp.dma_start(w2k[:, :, 0:HD], kw).then_inc(w2_in, 16)
                        sp.dma_start(w2k[:, :, HD:P], kw).then_inc(w2_in, 16)
                        sp.dma_start(w2v[:, :, :], w['nsa_cv_w2_2'].rearrange("(k p) c -> p k c", p=P)).then_inc(w2_in, 16)
                        load_weights(sp, n0 + 8 + SPLIT)
                        sp.wait_ge(w2_in, 48)

                    @block.gpsimd
                    def _(g):
                        nc.gpsimd.memset(kcp[:, :, :, P:P + 1], 0.0).then_inc(zeroed, 1)
                        g.wait_ge(zeroed, 1)
                        nc.gpsimd.memset(vcmp[:, :, :], 0.0).then_inc(zeroed, 1)
                        g.wait_ge(zeroed, 2)
                        split_low(g, n0 + 8 + SPLIT)

                    @block.tensor
                    def _(pe):
                        for u in range(units):
                            kv, s, kk = u // 16, u // 4, u % 4
                            if kk == 0:
                                wh, wl = tile_for(pe, n0 + s, ('nsa_ck_w1_2', 'nsa_cv_w1_2')[kv])
                            pe.wait_ge(low, u + 1)
                            mm = product(bank[kv][:, 0:CMP_HID], (blkh[:, u % 8, :], blkl[:, u % 8, :]),
                                         (wh[:, kk, :], wl[:, kk, :]), u % 16 == 0, u % 16 == 15)
                            if kk == 3:
                                mm.then_inc(w_used, 1)
                        for kv in range(2):
                            pe.wait_ge(act, kv + 1)
                            for h in range(2):
                                mm = nc.tensor.transpose(bank[2][:, (2 * kv + h) * P:(2 * kv + h + 1) * P],
                                                         hid[:, kv, h * P:(h + 1) * P], ident)
                        mm.then_inc(turned, 1)
                        pe.wait_ge(w2_in, 48)
                        pe.wait_ge(taken, 1)
                        for k in range(2):
                            nc.tensor.matmul(bank[3][:, 0:P], lhsT=w2k[:, k, :], rhs=hidT[:, k, :],
                                             start=(k == 0), stop=(k == 1))
                        for g in range(NSA_G):
                            for k in range(2):
                                mm = nc.tensor.matmul(bank[4][0:32, g * HD:(g + 1) * HD],
                                                      lhsT=hidT[:, 2 + k, g * 32:(g + 1) * 32], rhs=w2v[:, k, :],
                                                      start=(k == 0), stop=(k == 1))
                        mm.then_inc(second, 1)

                    @block.vector
                    def _(v):
                        for u in range(units):
                            v.wait_ge(high, u + 1)
                            blk, pos = block_of(u)
                            nc.vector.scalar_tensor_tensor(blkl[:, u % 8, :], blk, pos, blkh[:, u % 8, :],
                                                           ALU.add, ALU.subtract).then_inc(low, 1)
                        v.wait_ge(turned, 1)
                        nc.vector.tensor_copy(hidT[:, :, :], bank[2][:, :].rearrange("p (k c) -> p k c", c=P)).then_inc(taken, 1)
                        v.wait_ge(second, 1)
                        v.wait_ge(zeroed, 2)
                        nc.vector.tensor_copy(kcmp[:, :, :], bank[3][:, 0:P].rearrange("p (g n) -> p g n", n=32))
                        for i in range(HPG):
                            nc.vector.tensor_copy(vcmp[32 * i:32 * i + 32, :, i * HD:(i + 1) * HD],
                                                  bank[4][0:32, 0:256].rearrange("p (g d) -> p g d", d=HD))

                    @block.scalar
                    def _(a):
                        def hidden(kv):
                            a.wait_ge(w_used, n0 + 4 * kv + 4)
                            nc.scalar.activation(hid[:, kv, :], bank[kv][:, 0:CMP_HID], ACT.Gelu_apprx_tanh).then_inc(act, 1)

                        a.wait_ge(zeroed, 1)
                        for s in range(8):
                            if s >= 2:
                                a.wait_ge(w_used, n0 + s - 1)
                            for u in range(4 * s, 4 * s + 4):
                                blk, pos = block_of(u)
                                nc.scalar.activation(blkh[:, u % 8, :], blk, ACT.Identity, bias=pos).then_inc(high, 1)
                            split_high(a, n0 + s + SPLIT)
                        for kv in range(2):
                            hidden(kv)
                        nc.scalar.activation(nv[:, :, 512:560], nv[:, :, 512:560], ACT.Sigmoid).then_inc(gated, 1)
                        split_high(a, n0 + 8 + SPLIT)
            state["used"] = n0 + 8

        compress_stage()
        cmp_s.close()

        attn = ExitStack()
        prob = sb("nprob", [P, 3, 514], attn)
        probT = sb("nprobT", [P, 2, S], attn)
        gates = nv[:, :, 512:560].rearrange("p t (h b) -> p t h b", b=3)

        def cmp_attention_stage():
            with ExitStack() as sc:
                scores = sb("cscores", [P, 2, NSA_H, 32], sc)
                scored, masked, exped, turned, copied, summed, done, chain = (
                    sem(f"ca_{k}", sc) for k in ("scored", "masked", "exped", "turned", "copied", "summed", "done", "chain"))
                with nc.Block() as block:
                    @block.tensor
                    def _(pe):
                        for t in range(NT):
                            if t >= 1:
                                pe.wait_ge(masked, t)
                            for h in range(NSA_H):
                                g, i = h // HPG, h % HPG
                                gp = part(g)
                                at = ((g // 2) * HPG + i) * 32
                                mm = nc.tensor.matmul(bank[4 * (g % 2)][:, at:at + 32],
                                                      lhsT=nq[gp, 4 * (g // 2) + i, q_tile(t)], rhs=kcmp[gp, g, :],
                                                      start=True, stop=True)
                            mm.then_inc(scored, 1)
                            pe.wait_ge(exped, t + 1)
                            if t >= 1:
                                pe.wait_ge(copied, t)
                            for g in range(NSA_G):
                                mm = nc.tensor.transpose(bank[1][:, g * P:(g + 1) * P],
                                                         scores[:, t % 2, 4 * g:4 * g + 4, :].rearrange("p h n -> p (h n)"),
                                                         ident)
                            mm.then_inc(turned, 1)
                            pe.wait_ge(copied, t + 1)
                            if t >= 1:
                                pe.wait_ge(done, t)
                            for g in range(NSA_G):
                                mm = nc.tensor.matmul(bank[2 + g // 2][:, (g % 2) * 256:(g % 2) * 256 + 256],
                                                      lhsT=probT[:, t % 2, g * P:(g + 1) * P], rhs=vcmp[:, g, :],
                                                      start=True, stop=True)
                            mm.then_inc(summed, 1)

                    @block.scalar
                    def _(a):
                        for t in range(NT):
                            a.wait_ge(masked, t + 1)
                            nc.scalar.activation(scores[:, t % 2, :, :], scores[:, t % 2, :, :], ACT.Exp).then_inc(exped, 1)
                            a.wait_ge(turned, t + 1)
                            nc.scalar.activation(probT[:, t % 2, :], bank[1][:, :], ACT.Copy).then_inc(copied, 1)

                    @block.vector
                    def _(v):
                        link = Chain(v, chain)
                        for t in range(NT):
                            sv_ = scores[:, t % 2, :, :]
                            v.wait_ge(scored, t + 1)
                            mask = const[:, C_CMP + 32 * t:C_CMP + 32 * t + 32].unsqueeze(1).to_broadcast([P, HPG, 32])
                            by_group = sv_.rearrange("p (g i) n -> p g i n", i=HPG)
                            for g in range(NSA_G):
                                src = bank[4 * (g % 2)][:, (g // 2) * P:(g // 2 + 1) * P]
                                link(nc.vector.tensor_tensor(by_group[:, g, :, :], src.rearrange("p (i n) -> p i n", n=32),
                                                             mask, ALU.add))
                            link(nc.vector.tensor_reduce(stat[:, 40:56], sv_, AXX, ALU.max))
                            nc.vector.tensor_tensor(sv_, sv_, stat[:, 40:56].unsqueeze(2).to_broadcast([P, NSA_H, 32]),
                                                    ALU.subtract).then_inc(masked, 1)
                            v.wait_ge(exped, t + 1)
                            link(nc.vector.tensor_reduce(stat[:, 60:76], sv_, AXX, ALU.add))
                            link(nc.vector.reciprocal(stat[:, 80:96], stat[:, 60:76]))
                            link(nc.vector.tensor_scalar(stat[:, 80:96], stat[:, 80:96],
                                                         const[:, C_VALID + t:C_VALID + t + 1], None, ALU.mult))
                            link(nc.vector.tensor_tensor(stat[:, 100:116], stat[:, 80:96], gates[:, t, :, 0], ALU.mult))
                            v.wait_ge(summed, t + 1)
                            for b in range(2):
                                ins = nc.vector.tensor_tensor(
                                    ot[:, t, b * BANK:(b + 1) * BANK].rearrange("p (h d) -> p h d", d=HD),
                                    bank[2 + b][:, :].rearrange("p (h d) -> p h d", d=HD),
                                    stat[:, 100 + 8 * b:108 + 8 * b].unsqueeze(2).to_broadcast([P, 8, HD]), ALU.mult)
                            ins.then_inc(done, 1)

        cmp_attention_stage()

        nsa_units = []
        for t in range(NT):
            for h in range(NSA_H):
                g, i = h // HPG, h % HPG
                gp = part(g)
                for b in range(2):
                    wd = (t + 1) * P
                    nsa_units.append({
                        "width": wd,
                        "scores": [(0, wd, nq[gp, 4 * (g // 2) + i, q_tile(t)], nkT[gp, 2 * b + g // 2, 0:wd]),
                                   (t * P, P, ident, mask_q)],
                        "keys": [(j * P, nv[:, j, 256 * b + g * HD:256 * b + (g + 1) * HD]) for j in range(t + 1)],
                        "finish": finish_gated(ot[:, t, h * HD:(h + 1) * HD], gates[:, t, h, 1 + b:2 + b])})
        attention_stage("nsa", nsa_units, (prob, probT))
        attn.close()

        turn_split_stage("oT", [(tok(ot, c * P), (hT[:, c, :], hL[:, c, :])) for c in range(8)])
        token_stage("nsaO", (hT, hL), ND, [('nsa_w_out_2', BANK)] * 2, residual_add, all_v)
        nsa.close()

        cross = ExitStack()
        cq = sb("cq", [P, ND, S], cross)
        ckT = sb("ckT", [P, ND, MEM], cross)
        cv_ = sb("cv", [P, 2, D], cross)
        co = sb("co", [P, NT, D], cross)
        memx = ExitStack()
        mem = sb("mem", [P, 2, D], memx)
        memT = sb("memT", [P, ND, MEM], memx, F32R)
        memL = sb("memL", [P, ND, MEM], memx, F32R)

        def mem_stage():
            with nc.Block() as block, ExitStack() as sc:
                in_ = sem("mem_in", sc)

                @block.sync
                def _(sp):
                    sp.dma_start(mem[:, :, :], w['mem_2'].rearrange("o (t p) d -> p (o t) d", p=P)).then_inc(in_, 16)
                    sp.wait_ge(in_, 16)

        mem_stage()
        norm_stage("memn", mem, 2, par[:, K_MEM:], (memT, memL))
        feature_stage("ckT", (memT, memL), MEM, ['ca_wkv_2'] * 8, lambda i, ps, vec: copy(vec, ckT[:, i, :], ps))
        token_stage("cv", (memT, memL), ND, [('ca_wkv_2', BANK)] * 2,
                    lambda c, t, ps, vec: copy(vec, cv_[:, t, c * BANK:(c + 1) * BANK], ps), half, tiles=2)
        memx.close()
        norm_stage("cross", x, NT, par[:, K_CROSS:], (hT, hL))
        feature_stage("cqT", (hT, hL), S, ['ca_wq_2'] * 8,
                      lambda i, ps, vec: scaled(vec, cq[:, i, :], ps, CA_D ** -0.5) if vec else
                      nc.scalar.activation(cq[:, i, :], ps, ACT.Copy, scale=CA_D ** -0.5))
        attn = ExitStack()
        prob = sb("cprob", [P, 3, 514], attn)
        probT = sb("cprobT", [P, 2, S], attn)
        ca_units = []
        for t in range(NT):
            for h in range(CA_H):
                ca_units.append({
                    "width": MEM,
                    "scores": [(0, MEM, cq[:, 2 * h + k, q_tile(t)], ckT[:, 2 * h + k, :]) for k in range(2)],
                    "keys": [(j * P, cv_[:, j, h * CA_D:(h + 1) * CA_D]) for j in range(2)],
                    "finish": finish_plain(co[:, t, h * CA_D:(h + 1) * CA_D])})
        attention_stage("xattn", ca_units, (prob, probT))
        attn.close()
        turn_split_stage("coT", [(tok(co, c * P), (hT[:, c, :], hL[:, c, :])) for c in range(8)])
        token_stage("cao", (hT, hL), ND, [('ca_wo_2', BANK)] * 2, residual_add, all_v)
        cross.close()

        ffn("ffn2", par[:, K_FFN2:], 'ffn_w_up_2', 'ffn_w_up_2', 'ffn_w_down_2',
            lambda j, f: par[:, K_CONV2 + 22 * j + f:K_CONV2 + 22 * j + f + 1])
        assert state["used"] == len(plan)

        def final_stage():
            with ExitStack() as sc:
                gain = sb("fgain", [P, D], sc)
                sq = sb("fsq", [P, D], sc)
                gain_in, squared, rooted, chain, ready = (
                    sem(f"fin_{k}", sc) for k in ("gain", "sq", "root", "chain", "ready"))
                with nc.Block() as block:
                    @block.sync
                    def _(sp):
                        sp.dma_start(gain[:, :], w['final_norm_w_2'].unsqueeze(0).to_broadcast([P, D])).then_inc(gain_in, 16)
                        ov = out.rearrange("o (t p) d -> p (o t) d", p=P)
                        for t in range(NT):
                            sp.wait_ge(ready, t + 1)
                            sp.dma_start(ov[:, t, :], x[:, t, :]).then_inc(stored, 16)
                        sp.wait_ge(stored, 16 * NT)

                    @block.scalar
                    def _(a):
                        link = Chain(a, squared)
                        for t in range(NT):
                            link(nc.scalar.activation(sq[:, :], x[:, t, :], ACT.Square, accum_out=stat[:, t:t + 1]))
                        nc.scalar.activation(stat[:, 8:8 + NT], stat[:, 0:NT], ACT.Sqrt, bias=eps,
                                             scale=1.0 / D).then_inc(rooted, 1)

                    @block.vector
                    def _(v):
                        link = Chain(v, chain)
                        v.wait_ge(rooted, 1)
                        link(nc.vector.reciprocal(stat[:, 16:16 + NT], stat[:, 8:8 + NT]))
                        v.wait_ge(gain_in, 16)
                        for t in range(NT):
                            nc.vector.scalar_tensor_tensor(x[:, t, :], x[:, t, :], stat[:, 16 + t:17 + t], gain[:, :],
                                                           ALU.mult, ALU.mult).then_inc(ready, 1)

        final_stage()


_WEIGHTS = ['w_in', 'w_fox_out', 'w_conv_out', 'w_mlstm_out', 'w_swa_out', 'w_merge_out', 'w_gate', 'w_up', 'w_down',
            'nsa_w_in_2', 'nsa_ck_w1_2', 'nsa_ck_w2_2', 'nsa_cv_w1_2', 'nsa_cv_w2_2', 'nsa_w_out_2', 'ca_wq_2',
            'ca_wkv_2', 'ca_wo_2', 'ffn_w_up_2', 'ffn_w_down_2']
_OTHERS = ['x', 'mem_2', 'rel_bias', 'mlstm_h_gain', 'swa_sinks', 'final_norm_w_2']


def kernel(**inputs):
    import concourse.bacc as bacc
    from concourse.bass_utils import run_bass_kernel_spmd

    nc = bacc.Bacc("TRN2", target_bir_lowering=False, num_devices=1)
    a = {k: np.asarray(v) for k, v in inputs.items()}
    send = {k: np.ascontiguousarray(a[k][0]) for k in _WEIGHTS}
    send.update({k: np.ascontiguousarray(a[k]) for k in _OTHERS})
    send['w_in'] = pair_heads(send['w_in'], SQ, 1, SWA_H // 2)
    send['nsa_w_in_2'] = pair_heads(send['nsa_w_in_2'], NQ, 2, HPG)
    send['const'] = shape_constants()
    send['par'] = pack_params(a)
    arrays, w = {}, {}
    for name, v in send.items():
        arrays[f"in_{name}"] = v
        w[name] = nc.dram_tensor(f"in_{name}", v.shape, F32, kind="ExternalInput").ap()
    w['bias_rows'] = nc.dram_tensor("bias_rows", [SWA_H, 384], F32, kind="Internal").ap()
    out = nc.dram_tensor("out", [1, S, D], F32, kind="ExternalOutput").ap()
    build(nc, w, out)
    r = run_bass_kernel_spmd(nc, [arrays], core_ids=[0])
    return np.asarray(r.results[0]["out"]).reshape(1, S, D)
```

```python
from contextlib import ExitStack

import numpy as np

import concourse.bass as bass
from concourse import mybir

F32 = mybir.dt.float32
F32R = mybir.dt.float32r
ALU = mybir.AluOpType
ACT = mybir.ActivationFunctionType
AXX = mybir.AxisListType.X

P = 128
S = 512
D = 1024
NT = S // P
ND = D // P
BANK = 512
EPS = 1e-6
NEG = -1e30
HD = 64

FQ, FK, FV, FF = 0, 256, 512, 768
CU, CB, CC = 772, 1028, 1284
MQ, MK, MV, MI, MF, MO = 1540, 1796, 2052, 2308, 2312, 2316
SQ, SK, SV, GATES = 2572, 3084, 3212, 3340
FOX_H, ML_H, SWA_H = 4, 4, 8
N_BRANCH = 4
DFF = 2816
NF = DFF // P
FG = NF // 2
BUCKETS = 32

NQ, NKC, NVC, NKS, NVS, NKW, NVW, NGL = 0, 1024, 1280, 1536, 1792, 2048, 2304, 2560
NSA_H, NSA_G, HPG = 16, 4, 4
CMP_N = 31
CMP_HID = 256
MEM = 256
CA_H, CA_D = 4, 256

RING = 6
SPLIT = 3

C_ID, C_ANTI, C_MQ, C_MT = 0, P, 2 * P, 3 * P
C_CMP = 4 * P
C_VALID = C_CMP + NT * 32
C_SEL = C_VALID + NT
C_OH = C_SEL + 4 * P
C_ONE = C_OH + 384
C_END = C_ONE + P

K_FQ, K_FK, K_SQ, K_SK = 0, 1, 2, 3
K_CONV = 4
K_BIAS = 10
K_CONV2 = 12
K_PEK = K_CONV2 + 66
K_PEV = K_PEK + 16
K_END = K_PEV + 18


def shape_constants():
    c = np.zeros((P, C_END), np.float32)
    i = np.arange(P)
    c[:, C_ID:C_ID + P] = np.eye(P)
    c[:, C_ANTI:C_ANTI + P] = np.eye(P)[::-1]
    c[:, C_MQ:C_MQ + P] = np.where(i[None, :] <= i[:, None], 0, NEG)
    c[:, C_MT:C_MT + P] = np.where(i[:, None] <= i[None, :], 0, NEG)
    n = np.arange(32)
    for t in range(NT):
        tok = t * P + i
        seen = (16 * n[None, :] + 31 <= tok[:, None]) & (n[None, :] < CMP_N)
        c[:, C_CMP + 32 * t:C_CMP + 32 * t + 32] = np.where(seen, 0, NEG)
        c[:, C_VALID + t] = tok >= 31
    for h in range(4):
        c[h, C_SEL + h * P:C_SEL + (h + 1) * P] = 1
        c[32 + h, C_SEL + h * P:C_SEL + (h + 1) * P] = 1
    dist = 255 - np.arange(384)
    n1 = np.maximum(dist, 1).astype(np.float32)
    large = 16 + (np.log(n1 / np.float32(16)) / np.float32(np.log(8.0)) * np.float32(16)).astype(np.int32)
    bucket = np.where(dist < 16, dist, np.minimum(large, BUCKETS - 1))
    for u in range(384):
        if 0 <= dist[u] < 128:
            c[bucket[u], C_OH + u] = 1
        else:
            c[BUCKETS, C_OH + u] = NEG
    c[:, C_ONE:C_ONE + P] = 1
    return c


def pack_params(a):
    k = np.zeros((P, K_END), np.float32)

    def tiles(v):
        return np.asarray(v).reshape(-1, P).T

    for at, name in ((K_FQ, 'fox_q_gain'), (K_FK, 'fox_k_gain'), (K_SQ, 'swa_q_gain'), (K_SK, 'swa_k_gain')):
        k[0:HD, at] = a[name][0]
        k[HD:P, at] = a[name][0]
    k[:, K_CONV:K_CONV + 6] = tiles(a['conv_w'])
    k[0:4, K_BIAS] = a['fox_f_bias'][0]
    k[32:36, K_BIAS] = a['mlstm_i_bias'][0]
    k[64:68, K_BIAS] = a['mlstm_f_bias'][0]
    k[:, K_CONV2:K_CONV2 + 66] = tiles(a['ffn_conv_w_2'])
    k[:, K_PEK:K_PEK + 16] = tiles(a['nsa_pe_k_2'])
    k[:, K_PEV:K_PEV + 16] = tiles(a['nsa_pe_v_2'])
    return k


def pair_heads(weight, at, blocks, per):
    m = weight.copy()
    n = blocks * 2 * per * HD
    q = m[:, at:at + n].reshape(-1, blocks, 2, per, HD)
    m[:, at:at + n] = q.transpose(0, 1, 3, 2, 4).reshape(-1, n)
    return m


class Chain:

    def __init__(self, eng, sem):
        self.eng, self.sem, self.n = eng, sem, 0

    def __call__(self, ins):
        self.n += 1
        ins.then_inc(self.sem, 1)
        self.eng.wait_ge(self.sem, self.n)


def build(nc, w, out):
    ctx = ExitStack()
    with ctx:
        def sb(name, shape, scope=ctx, dt=F32):
            return scope.enter_context(nc.sbuf_tensor(name, list(shape), dt))

        stage_sems = []

        def sem(name, scope=ctx):
            if scope is ctx:
                return ctx.enter_context(nc.semaphore(name))
            stage_sems.append(nc.alloc_semaphore(name))
            return stage_sems[-1]

        def clear_stage():
            with nc.Block() as block:
                @block.gpsimd
                def _(g):
                    nc.clear_and_free_semaphores(list(stage_sems))
            stage_sems.clear()

        psum = ctx.enter_context(nc.psum_tensor("psum", [P, 8, BANK], F32))
        bank = [psum[:, i, :] for i in range(8)]
        const = sb("const", [P, C_END])
        par = sb("par", [P, K_END])
        x = sb("x", [P, NT, D])
        hT = sb("hT", [P, ND, S], dt=F32R)
        hL = sb("hL", [P, ND, S], dt=F32R)
        ring = sb("ring", [P, RING, 1024])
        w_high = sb("w_high", [P, SPLIT, 1024], dt=F32R)
        w_low = sb("w_low", [P, SPLIT, 1024], dt=F32R)
        stat = sb("stat", [P, 160])

        ident = const[:, C_ID:C_ID + P]
        anti = const[:, C_ANTI:C_ANTI + P]
        mask_q = const[:, C_MQ:C_MQ + P]
        mask_t = const[:, C_MT:C_MT + P]
        eps = stat[:, 150:151]
        const_r = sb("const_r", [P, 3 * P], dt=F32R)
        ident_r, anti_r, mask_r = (const_r[:, c:c + P] for c in (C_ID, C_ANTI, C_MQ))

        w_ready = [sem(f"w_ready{i}") for i in range(RING)]
        w_hi = sem("w_hi")
        w_lo = sem("w_lo")
        w_used = sem("w_used")
        stored = sem("stored")
        plan = []

        def cols(name, c0, n=P, first=0, kt=None):
            m = w[name]
            per = 1024 // n
            end = m.shape[0] // P if kt is None else first + kt
            for k0 in range(first, end, per):
                k = min(per, end - k0)
                src = m[k0 * P:(k0 + k) * P, c0:c0 + n].rearrange("(k p) c -> p k c", p=P)
                plan.append((name, src, k, n))

        def weight_plan():
            for c0, n in TOKEN_CHUNKS_A:
                cols('w_in', c0, n)
            for c0 in FEATURE_TILES_A:
                cols('w_in', c0)
            for d in range(ND):
                for b in range(N_BRANCH):
                    cols('w_in', GATES + b * D + d * P)
                for b in range(N_BRANCH):
                    cols(('w_fox_out', 'w_conv_out', 'w_mlstm_out', 'w_swa_out')[b], d * P)
            for half in range(2):
                cols('w_merge_out', half * BANK, BANK)
            for f0 in range(0, NF, FG):
                for f in range(f0, f0 + FG):
                    cols('w_gate', f * P)
                    cols('w_up', f * P)
                for half in range(2):
                    cols('w_down', half * BANK, BANK, f0, FG)
            for half in range(2):
                cols('nsa_w_in_2', half * BANK, BANK)
            for c0 in FEATURE_TILES_N:
                cols('nsa_w_in_2', c0)
            for c0, n in TOKEN_CHUNKS_N:
                cols('nsa_w_in_2', c0, n)
            for c0 in KEY_TILES_N:
                cols('nsa_w_in_2', c0)
            cols('nsa_ck_w1_2', 0, CMP_HID)
            cols('nsa_cv_w1_2', 0, CMP_HID)
            for half in range(2):
                cols('nsa_w_out_2', half * BANK, BANK)
            for d in range(ND):
                cols('ca_wkv_2', d * P)
            for half in range(2):
                cols('ca_wkv_2', D + half * BANK, BANK)
            for d in range(ND):
                cols('ca_wq_2', d * P)
            for half in range(2):
                cols('ca_wo_2', half * BANK, BANK)
            for f0 in range(0, NF, FG):
                for f in range(f0, f0 + FG):
                    cols('ffn_w_up_2', f * P)
                    cols('ffn_w_up_2', DFF + f * P)
                for half in range(2):
                    cols('ffn_w_down_2', half * BANK, BANK, f0, FG)

        TOKEN_CHUNKS_A = [(FQ, 512), (FV, 256), (MV, 256), (MO, 256), (SQ, 512), (SK, 256)]
        FEATURE_TILES_A = [c + P * i for c in (MQ, MK, CU, CC, CB) for i in range(2)]
        FEATURE_TILES_N = [c + P * i for c in (NKC, NVC) for i in range(2)]
        KEY_TILES_N = [c + P * i for c in (NKS, NKW) for i in range(2)]
        TOKEN_CHUNKS_N = [(NVS, 256), (NVW, 304)]
        weight_plan()
        state = {"issued": 0, "used": 0, "high": 0, "low": 0}

        def tile_view(buf, n, depth):
            _, _, k, width = plan[n]
            return buf[:, n % depth, 0:k * width].rearrange("p (k c) -> p k c", c=width)

        def load_weights(sp, split):
            while state["issued"] < min(split + RING, len(plan)):
                n = state["issued"]
                if n >= RING:
                    sp.wait_ge(w_lo, n - RING + 1)
                sp.dma_start(tile_view(ring, n, RING), plan[n][1]).then_inc(w_ready[n % RING], 16)
                state["issued"] += 1

        def split_high(a, end):
            while state["high"] < min(end, len(plan)):
                n = state["high"]
                a.wait_ge(w_ready[n % RING], 16 * (n // RING + 1))
                if n >= SPLIT:
                    a.wait_ge(w_used, n - SPLIT + 1)
                nc.scalar.activation(tile_view(w_high, n, SPLIT), tile_view(ring, n, RING), ACT.Copy).then_inc(w_hi, 1)
                state["high"] += 1

        def split_low(g, end):
            while state["low"] < min(end, len(plan)):
                n = state["low"]
                g.wait_ge(w_hi, n + 1)
                nc.gpsimd.tensor_tensor(tile_view(w_low, n, SPLIT), tile_view(ring, n, RING),
                                        tile_view(w_high, n, SPLIT), ALU.subtract).then_inc(w_lo, 1)
                state["low"] += 1

        def tile_for(pe, n, name):
            assert plan[n][0] == name, (plan[n][0], name, n)
            pe.wait_ge(w_lo, n + 1)
            return tile_view(w_high, n, SPLIT), tile_view(w_low, n, SPLIT)

        def product(ps, stationary, moving, first, last):
            (sh, sl), (mh, ml_) = stationary, moving
            nc.tensor.matmul(ps, lhsT=sh, rhs=mh, start=first, stop=False)
            nc.tensor.matmul(ps, lhsT=sh, rhs=ml_, start=False, stop=False)
            return nc.tensor.matmul(ps, lhsT=sl, rhs=mh, start=False, stop=last)

        def copy(vector, dst, src):
            if vector:
                return nc.vector.tensor_copy(dst, src)
            return nc.scalar.activation(dst, src, ACT.Copy)

        def scaled(vector, dst, src, by):
            if vector:
                return nc.vector.tensor_scalar(dst, src, by, None, ALU.mult)
            return nc.scalar.activation(dst, src, ACT.Copy, scale=by)

        x_in = [sem(f"x_in{t}") for t in range(NT)]

        def load_stage():
            with nc.Block() as block, ExitStack() as sc:
                loaded = sem("loaded", sc)

                @block.sync
                def _(sp):
                    for t in range(NT):
                        sp.dma_start(x[:, t, :], w['x'][0, t * P:(t + 1) * P, :]).then_inc(x_in[t], 16)
                    sp.dma_start(const[:, :], w['const']).then_inc(loaded, 16)
                    sp.dma_start(par[:, :], w['par']).then_inc(loaded, 16)
                    sp.wait_ge(loaded, 32)

                @block.vector
                def _(v):
                    nc.vector.memset(eps, EPS)
                    v.wait_ge(loaded, 32)
                    nc.vector.tensor_copy(const_r[:, :], const[:, 0:3 * P])

        class NormTiles:
            def __init__(self, name, sc, src, gain, dst, halves):
                self.src, self.weight, self.dst, self.halves = src, gain, dst, halves
                self.h = sb(f"{name}_h", [P, 2, D], sc)
                self.gain = sb(f"{name}_gain", [P, D], sc)
                (self.gain_in, self.squared, self.biased, self.rooted, self.scaled, self.turned, self.high, self.low,
                 self.chain) = (sem(f"{name}_{s}", sc) for s in
                                ("gain_in", "squared", "biased", "rooted", "scaled", "turned", "high", "low", "chain"))
                self.squares = 0

            def load(self, sp):
                sp.dma_start(self.gain[:, :], self.weight.to_broadcast([P, D])).then_inc(self.gain_in, 16)

            def square(self, a, t, c0, n):
                if t >= 2 and self.dst is not None and c0 + n == D:
                    a.wait_ge(self.turned, 2 * t - 2)
                part = 0 if c0 == 0 and self.halves else 4
                nc.scalar.activation(self.h[:, t % 2, c0:c0 + n], self.src[:, t, c0:c0 + n], ACT.Square,
                                     accum_out=stat[:, part + t:part + t + 1]).then_inc(self.squared, 1)
                self.squares += 1
                a.wait_ge(self.squared, self.squares)

            def bias(self, v, tiles):
                v.wait_ge(self.squared, tiles)
                nc.vector.tensor_scalar(stat[:, 12:12 + tiles], stat[:, 0:tiles], 1.0 / D, EPS,
                                        ALU.mult, ALU.add).then_inc(self.biased, 1)

            def root(self, a, t):
                bias = eps
                if self.halves:
                    a.wait_ge(self.biased, 1)
                    bias = stat[:, 12 + t:13 + t]
                nc.scalar.activation(stat[:, 8 + t:9 + t], stat[:, 4 + t:5 + t], ACT.Sqrt, bias=bias,
                                     scale=1.0 / D).then_inc(self.rooted, 1)

            def scale(self, v, t):
                if t == 0:
                    v.wait_ge(self.gain_in, 16)
                v.wait_ge(self.rooted, t + 1)
                nc.vector.reciprocal(stat[:, 16 + t:17 + t], stat[:, 8 + t:9 + t]).then_inc(self.chain, 1)
                v.wait_ge(self.chain, t + 1)
                for c in range(2):
                    cut = slice(c * BANK, (c + 1) * BANK)
                    to = self.src[:, t, cut] if self.dst is None else self.h[:, t % 2, cut]
                    nc.vector.scalar_tensor_tensor(to, self.src[:, t, cut], stat[:, 16 + t:17 + t], self.gain[:, cut],
                                                   ALU.mult, ALU.mult).then_inc(self.scaled, 1)

            def turn(self, pe, t):
                for c in range(2):
                    pe.wait_ge(self.scaled, 2 * t + c + 1)
                    if t >= 2:
                        pe.wait_ge(self.low, 2 * (t - 2) + c + 1)
                    for i in range(4):
                        d = 4 * c + i
                        mm = nc.tensor.transpose(bank[2 * (t % 2) + c][:, i * P:(i + 1) * P],
                                                 self.h[:, t % 2, d * P:(d + 1) * P], ident)
                    mm.then_inc(self.turned, 1)

            def _parts(self, t, c):
                cut, four = slice(t * P, (t + 1) * P), slice(4 * c, 4 * c + 4)
                return (bank[2 * (t % 2) + c].rearrange("p (d s) -> p d s", s=P),
                        self.dst[0][:, four, cut], self.dst[1][:, four, cut])

            def high_part(self, a, t):
                for c in range(2):
                    src, high, _ = self._parts(t, c)
                    a.wait_ge(self.turned, 2 * t + c + 1)
                    nc.scalar.activation(high, src, ACT.Copy).then_inc(self.high, 1)

            def low_part(self, v, t):
                for c in range(2):
                    src, high, low = self._parts(t, c)
                    v.wait_ge(self.high, 2 * t + c + 1)
                    nc.vector.tensor_tensor(low, src, high, ALU.subtract).then_inc(self.low, 1)

        def norm_stage(name, src, tiles, gain, dst, source=None, src_in=None):
            with ExitStack() as sc:
                norm = NormTiles(name, sc, src, gain, dst, False)
                src_in = src_in or [sem(f"{name}_in{t}", sc) for t in range(tiles)]
                with nc.Block() as block:
                    @block.sync
                    def _(sp):
                        norm.load(sp)
                        for t in range(tiles if source is not None else 0):
                            sp.dma_start(src[:, t, :], source[0, t * P:(t + 1) * P, :]).then_inc(src_in[t], 16)
                        load_weights(sp, state["used"] + SPLIT)

                    @block.scalar
                    def _(a):
                        for t in range(tiles + 1):
                            if t < tiles:
                                a.wait_ge(src_in[t], 16)
                                norm.square(a, t, 0, D)
                                norm.root(a, t)
                            else:
                                split_high(a, state["used"] + 1)
                            if t >= 1:
                                norm.high_part(a, t - 1)
                        split_high(a, state["used"] + SPLIT)

                    @block.vector
                    def _(v):
                        for t in range(tiles + 1):
                            if t < tiles:
                                norm.scale(v, t)
                            if t >= 1:
                                norm.low_part(v, t - 1)

                    @block.tensor
                    def _(pe):
                        for t in range(tiles):
                            norm.turn(pe, t)

                    @block.gpsimd
                    def _(g):
                        split_low(g, state["used"] + SPLIT)

        def token_stage(name, actT, kt, chunks, evac, engines, tiles=NT, norm_gain=None, norm_dst=None):
            n_v = [sum(engines(c)[:tiles]) for c in range(len(chunks))]
            slots, n = [], state["used"]
            for wname, width in chunks:
                per = -(-kt // (1024 // width))
                slots.append((n, per, width, wname))
                n += per
            with ExitStack() as sc:
                out_v, out_a, chain, tile_done = (sem(f"{name}_{k}", sc) for k in ("outv", "outa", "chain", "tile"))
                norm = NormTiles(f"{name}n", sc, x, norm_gain, norm_dst, True) if norm_gain is not None else None
                store = norm is not None and norm_dst is None
                with nc.Block() as block:
                    @block.tensor
                    def _(pe):
                        for c, (n0, per, width, wname) in enumerate(slots):
                            base = 4 * (c % 2)
                            if c >= 2:
                                by_v = sum(n_v[:c - 1])
                                by_a = tiles * (c - 1) - by_v
                                if by_v:
                                    pe.wait_ge(out_v, by_v)
                                if by_a:
                                    pe.wait_ge(out_a, by_a)

                            def products(s, kk, wh, wl, t):
                                k = s * (1024 // width) + kk
                                tok_ = slice(t * P, (t + 1) * P)
                                return product(bank[base + t][:, 0:width], (actT[0][:, k, tok_], actT[1][:, k, tok_]),
                                               (wh[:, kk, :], wl[:, kk, :]), k == 0, k == kt - 1)

                            held = min(SPLIT, per) if norm is not None and c == len(slots) - 1 else 0
                            for s in range(per - held):
                                wh, wl = tile_for(pe, n0 + s, wname)
                                for kk in range(plan[n0 + s][2]):
                                    for t in range(tiles):
                                        mm = products(s, kk, wh, wl, t)
                                mm.then_inc(w_used, 1)
                            for t in range(tiles if held else 0):
                                for s in range(per - held, per):
                                    wh, wl = tile_for(pe, n0 + s, wname)
                                    for kk in range(plan[n0 + s][2]):
                                        mm = products(s, kk, wh, wl, t)
                                    if t == tiles - 1:
                                        mm.then_inc(w_used, 1)
                                if t < tiles - 1:
                                    mm.then_inc(tile_done, 1)
                                if t >= 1 and not store:
                                    if t == 1:
                                        pe.wait_ge(out_v, tiles)
                                    norm.turn(pe, t - 1)
                            if held and not store:
                                norm.turn(pe, tiles - 1)

                    def empty(eng, vector):
                        link = Chain(eng, chain) if vector else None
                        for c, (n0, per, width, _) in enumerate(slots):
                            last = norm is not None and c == len(slots) - 1
                            if not vector:
                                split_high(eng, n0 + per + SPLIT - 1)
                            if not last:
                                eng.wait_ge(w_used, n0 + per)
                            for t in range(tiles):
                                if last and t < tiles - 1:
                                    eng.wait_ge(tile_done, t + 1)
                                elif last:
                                    eng.wait_ge(w_used, n0 + per)
                                if engines(c)[t] == vector:
                                    evac(c, t, bank[4 * (c % 2) + t][:, 0:width], link)\
                                        .then_inc(out_v if vector else out_a, 1)
                                if last:
                                    norm.scale(eng, t)
                                    if t >= 1 and not store:
                                        norm.low_part(eng, t - 1)
                            if norm is not None and c == 0:
                                norm.bias(eng, tiles)
                        if norm is not None and not store:
                            norm.low_part(eng, tiles - 1)

                    @block.vector
                    def _(v):
                        empty(v, True)

                    @block.scalar
                    def _(a):
                        if sum(n_v) < tiles * len(chunks):
                            empty(a, False)
                        if norm is not None:
                            (n0, per, width, _) = slots[-1]
                            split_high(a, n0 + SPLIT)
                            for t in range(tiles):
                                a.wait_ge(out_v, t + 1)
                                norm.square(a, t, 0, BANK)
                            split_high(a, n0 + per)
                            for t in range(tiles):
                                a.wait_ge(out_v, tiles + t + 1)
                                norm.square(a, t, BANK, BANK)
                                norm.root(a, t)
                                if t >= 1 and not store:
                                    norm.high_part(a, t - 1)
                                if t == tiles - 2:
                                    split_high(a, n0 + per - min(SPLIT, per) + SPLIT + 1)
                            split_high(a, n0 + per - min(SPLIT, per) + SPLIT + 2)
                            if not store:
                                norm.high_part(a, tiles - 1)
                        split_high(a, n + SPLIT)

                    @block.gpsimd
                    def _(g):
                        split_low(g, n + SPLIT)

                    @block.sync
                    def _(sp):
                        if norm is not None:
                            norm.load(sp)
                        load_weights(sp, n + SPLIT)
                        if store:
                            ov = out.rearrange("o (t p) d -> p (o t) d", p=P)
                            for t in range(tiles):
                                sp.wait_ge(norm.scaled, 2 * t + 2)
                                sp.dma_start(ov[:, t, :], x[:, t, :]).then_inc(stored, 16)
                            sp.wait_ge(stored, 16 * tiles)
            state["used"] = n

        def feature_stage(name, actT, ncols, tiles, evac, kt=ND):
            n0 = state["used"]
            with ExitStack() as sc:
                out_e = [sem(f"{name}_outv", sc), sem(f"{name}_outa", sc)]
                with nc.Block() as block:
                    @block.tensor
                    def _(pe):
                        for i, wname in enumerate(tiles):
                            if i >= 8:
                                pe.wait_ge(out_e[i % 2], (i - 8) // 2 + 1)
                            wh, wl = tile_for(pe, n0 + i, wname)
                            for k in range(kt):
                                mm = product(bank[i % 8][:, 0:ncols], (wh[:, k, :], wl[:, k, :]),
                                             (actT[0][:, k, 0:ncols], actT[1][:, k, 0:ncols]), k == 0, k == kt - 1)
                            mm.then_inc(w_used, 1)

                    def empty(eng, parity):
                        for i in range(parity, len(tiles), 2):
                            if parity == 1:
                                split_high(eng, n0 + i + SPLIT)
                            eng.wait_ge(w_used, n0 + i + 1)
                            evac(i, bank[i % 8][:, 0:ncols], parity == 0).then_inc(out_e[parity], 1)

                    @block.vector
                    def _(v):
                        empty(v, 0)

                    @block.scalar
                    def _(a):
                        empty(a, 1)
                        split_high(a, n0 + len(tiles) + SPLIT)

                    @block.gpsimd
                    def _(g):
                        split_low(g, n0 + len(tiles) + SPLIT)

                    @block.sync
                    def _(sp):
                        load_weights(sp, n0 + len(tiles) + SPLIT)
            state["used"] = n0 + len(tiles)

        def turn_stage(name, blocks):
            with ExitStack() as sc:
                turned = sem(f"{name}_turned", sc)
                out_e = [sem(f"{name}_outv", sc), sem(f"{name}_outa", sc)]
                with nc.Block() as block:
                    @block.tensor
                    def _(pe):
                        for i, (src, _, _) in enumerate(blocks):
                            if i >= 8:
                                pe.wait_ge(out_e[i % 2], (i - 8) // 2 + 1)
                            for t in range(NT):
                                mm = nc.tensor.transpose(bank[i % 8][:, t * P:(t + 1) * P], src(t), ident)
                            mm.then_inc(turned, 1)

                    def empty(eng, parity):
                        for i in range(parity, len(blocks), 2):
                            _, dst, by = blocks[i]
                            eng.wait_ge(turned, i + 1)
                            scaled(parity == 0, dst, bank[i % 8][:, :], by).then_inc(out_e[parity], 1)

                    @block.vector
                    def _(v):
                        empty(v, 0)

                    @block.scalar
                    def _(a):
                        empty(a, 1)

        def turn_split_stage(name, blocks, extra=()):
            with ExitStack() as sc:
                turned, high = sem(f"{name}_turned", sc), sem(f"{name}_high", sc)
                sources = [(bank[i][:, :], dst) for i, (_, dst) in enumerate(blocks)] + list(extra)
                with nc.Block() as block:
                    @block.tensor
                    def _(pe):
                        for i, (src, _) in enumerate(blocks):
                            for t in range(NT):
                                mm = nc.tensor.transpose(bank[i][:, t * P:(t + 1) * P], src(t), ident)
                            mm.then_inc(turned, 1)

                    @block.scalar
                    def _(a):
                        for i, (src, dst) in enumerate(sources):
                            if i < len(blocks):
                                a.wait_ge(turned, i + 1)
                            copy(False, dst[0], src).then_inc(high, 1)

                    @block.vector
                    def _(v):
                        for i, (src, dst) in enumerate(sources):
                            v.wait_ge(high, i + 1)
                            nc.vector.tensor_tensor(dst[1], src, dst[0], ALU.subtract)

        def attention_stage(name, units, scratch):
            prob, probT = scratch[0], scratch[1]
            probL = scratch[2] if len(scratch) == 3 else None
            n = len(units)
            with ExitStack() as sc:
                scored, peaked, exped, turned, summed, emptied, chain = (
                    sem(f"{name}_{s}", sc)
                    for s in ("scored", "peaked", "exped", "turned", "summed", "emptied", "chain"))
                copied = [sem(f"{name}_copied{i}", sc) for i in range(2)]
                npeak = [stat[:, 20 + i:21 + i] for i in range(3)]
                total = [stat[:, 24 + i:25 + i] for i in range(6)]

                with nc.Block() as block:
                    @block.tensor
                    def _(pe):
                        for s in range(n + 4):
                            if s < n:
                                if s >= 3:
                                    pe.wait_ge(exped, s - 2)
                                sc_ = units[s]["scores"]
                                for j, (c0, cn, lhsT, rhs) in enumerate(sc_):
                                    mm = nc.tensor.matmul(bank[s % 3][:, c0:c0 + cn], lhsT=lhsT, rhs=rhs,
                                                          start=(j == 0), stop=(j == len(sc_) - 1))
                                mm.then_inc(scored, 1)
                            u = s - 2
                            if 0 <= u < n:
                                pe.wait_ge(exped, u + 1)
                                if u >= 2 and probL is not None:
                                    pe.wait_ge(copied[1], u - 1)
                                elif u >= 2:
                                    pe.wait_ge(copied[u % 2], u // 2)
                                for j, (c0, _) in enumerate(units[u]["keys"]):
                                    mm = nc.tensor.transpose(bank[3 + u % 2][:, j * P:(j + 1) * P],
                                                             prob[:, u % 3, c0:c0 + P], ident)
                                mm.then_inc(turned, 1)
                            u = s - 4
                            if u >= 0:
                                if probL is not None:
                                    pe.wait_ge(copied[1], u + 1)
                                else:
                                    pe.wait_ge(copied[u % 2], u // 2 + 1)
                                if u >= 3:
                                    pe.wait_ge(emptied, u - 2)
                                keys = units[u]["keys"]
                                for j, (_, val) in enumerate(keys if probL is not None else ()):
                                    cut = slice(j * P, (j + 1) * P)
                                    nc.tensor.matmul(bank[5 + u % 3][:, 0:2 * HD], lhsT=probT[:, u % 3, cut], rhs=val,
                                                     start=(j == 0), stop=False)
                                    mm = nc.tensor.matmul(bank[5 + u % 3][:, 0:HD], lhsT=probL[:, u % 2, cut],
                                                          rhs=val[:, 0:HD], start=False, stop=(j == len(keys) - 1))
                                for j, (_, val) in enumerate(keys if probL is None else ()):
                                    mm = nc.tensor.matmul(bank[5 + u % 3][:, 0:val.shape[-1]],
                                                          lhsT=probT[:, u % 3, j * P:(j + 1) * P], rhs=val,
                                                          start=(j == 0), stop=(j == len(keys) - 1))
                                mm.then_inc(summed, 1)

                    def copy_turned(eng, u):
                        eng.wait_ge(turned, u + 1)
                        if u >= 3:
                            eng.wait_ge(summed, u - 2)
                        k = len(units[u]["keys"]) * P
                        copy(u % 2 == 0, probT[:, u % 3, 0:k], bank[3 + u % 2][:, 0:k]).then_inc(copied[u % 2], 1)

                    def split_turned(v, u):
                        v.wait_ge(copied[0], u + 1)
                        if u >= 2:
                            v.wait_ge(summed, u - 1)
                        k = len(units[u]["keys"]) * P
                        nc.vector.tensor_tensor(probL[:, u % 2, 0:k], bank[3 + u % 2][:, 0:k], probT[:, u % 3, 0:k],
                                                ALU.subtract).then_inc(copied[1], 1)

                    def high_turned(a, u):
                        a.wait_ge(turned, u + 1)
                        if u >= 3:
                            a.wait_ge(summed, u - 2)
                        k = len(units[u]["keys"]) * P
                        copy(False, probT[:, u % 3, 0:k], bank[3 + u % 2][:, 0:k]).then_inc(copied[0], 1)

                    @block.vector
                    def _(v):
                        link = Chain(v, chain)
                        for s in range(n + 5):
                            if s < n:
                                v.wait_ge(scored, s + 1)
                                if s >= 3:
                                    v.wait_ge(exped, s - 2)
                                nc.vector.tensor_reduce(npeak[s % 3], bank[s % 3][:, 0:units[s]["width"]], AXX,
                                                        ALU.max, negate=True).then_inc(peaked, 1)
                            if 0 <= s - 3 < n and probL is not None:
                                split_turned(v, s - 3)
                            elif 0 <= s - 3 < n and (s - 3) % 2 == 0:
                                copy_turned(v, s - 3)
                            u = s - 5
                            if u >= 0:
                                v.wait_ge(summed, u + 1)
                                units[u]["finish"](link, u, bank[5 + u % 3], total[u % 6]).then_inc(emptied, 1)

                    @block.scalar
                    def _(a):
                        for s in range(n + 2):
                            if s < n:
                                a.wait_ge(peaked, s + 1)
                                if s >= 3:
                                    a.wait_ge(turned, s - 2)
                                if s >= 6:
                                    a.wait_ge(emptied, s - 5)
                                wd = units[s]["width"]
                                nc.scalar.activation(prob[:, s % 3, 0:wd], bank[s % 3][:, 0:wd], ACT.Exp,
                                                     bias=npeak[s % 3], accum_out=total[s % 6]).then_inc(exped, 1)
                            if s >= 2 and probL is not None:
                                high_turned(a, s - 2)
                            elif s >= 2 and s % 2 == 1:
                                copy_turned(a, s - 2)

        def pair_attention_stage(name, pairs, scratch):
            prob, probT, probL, put = scratch
            nprob, nT, nL, nput = (t.shape[1] for t in scratch)
            n = len(pairs)
            with ExitStack() as sc:
                scored, peaked, exped, turned, high, low, summed, divided, collected, chain, chain_g = (
                    sem(f"{name}_{s}", sc)
                    for s in ("scored", "peaked", "exped", "turned", "high", "low", "summed", "divided", "collected",
                              "chain", "chain_g"))
                npeak = [stat[:, 20 + 2 * i:22 + 2 * i] for i in range(2)]
                total = [stat[:, 24 + 2 * i:26 + 2 * i] for i in range(4)]
                by = [stat[:, 32 + 2 * i:34 + 2 * i] for i in range(2)]

                with nc.Block() as block:
                    @block.tensor
                    def _(pe):
                        def scores(p):
                            if p >= 2:
                                pe.wait_ge(exped, 2 * p - 2)
                            for b, unit in enumerate(pairs[p]["units"]):
                                sc_ = unit["scores"]
                                for j, (c0, cn, lhsT, rhs) in enumerate(sc_):
                                    mm = nc.tensor.matmul(bank[2 * (p % 2) + b][:, c0:c0 + cn], lhsT=lhsT, rhs=rhs,
                                                          start=(j == 0), stop=(j == len(sc_) - 1))
                            mm.then_inc(scored, 1)

                        def turn(p):
                            for b, unit in enumerate(pairs[p]["units"]):
                                v_ = 2 * p + b
                                pe.wait_ge(exped, v_ + 1)
                                if p >= 1:
                                    pe.wait_ge(low, v_ - 1)
                                for j, (c0, _) in enumerate(unit["keys"]):
                                    mm = nc.tensor.transpose(bank[4 + b][:, j * P:(j + 1) * P],
                                                             prob[:, v_ % nprob, c0:c0 + P], ident)
                                mm.then_inc(turned, 1)

                        def values(p):
                            if p >= 2:
                                pe.wait_ge(divided, p - 1)
                            for b, unit in enumerate(pairs[p]["units"]):
                                v_ = 2 * p + b
                                pe.wait_ge(low, v_ + 1)
                                to, keys = bank[6 + p % 2][:, b * P:(b + 1) * P], unit["keys"]
                                for j, (_, val) in enumerate(keys):
                                    cut = slice(j * P, (j + 1) * P)
                                    nc.tensor.matmul(to, lhsT=probT[:, v_ % nT, cut], rhs=val, start=(j == 0), stop=False)
                                    mm = nc.tensor.matmul(to[:, 0:HD], lhsT=probL[:, v_ % nL, cut], rhs=val[:, 0:HD],
                                                          start=False, stop=(j == len(keys) - 1))
                                mm.then_inc(summed, 1)

                        scores(0)
                        for s in range(n + 2):
                            if 1 <= s <= n:
                                turn(s - 1)
                            if s >= 2:
                                values(s - 2)
                            if s + 1 < n:
                                scores(s + 1)

                    @block.scalar
                    def _(a):
                        for s in range(n + 1):
                            for v_ in ((2 * s - 2, 2 * s - 1) if s >= 1 else ()):
                                a.wait_ge(turned, v_ + 1)
                                if v_ >= nT:
                                    a.wait_ge(summed, v_ - nT + 1)
                                k = len(pairs[v_ // 2]["units"][v_ % 2]["keys"]) * P
                                nc.scalar.activation(probT[:, v_ % nT, 0:k], bank[4 + v_ % 2][:, 0:k], ACT.Copy).then_inc(high, 1)
                            for b in range(2 if s < n else 0):
                                v_, wd = 2 * s + b, pairs[s]["units"][b]["width"]
                                if b == 0:
                                    a.wait_ge(peaked, s + 1)
                                if b == 0 and s >= 4:
                                    a.wait_ge(divided, s - 3)
                                if v_ >= nprob:
                                    a.wait_ge(turned, v_ - nprob + 1)
                                nc.scalar.activation(prob[:, v_ % nprob, 0:wd], bank[2 * (s % 2) + b][:, 0:wd], ACT.Exp,
                                                     bias=npeak[s % 2][:, b:b + 1],
                                                     accum_out=total[s % 4][:, b:b + 1]).then_inc(exped, 1)

                    @block.vector
                    def _(v):
                        link = Chain(v, chain)
                        for s in range(n + 3):
                            if s < n:
                                wd = pairs[s]["units"][0]["width"]
                                v.wait_ge(scored, s + 1)
                                if s >= 2:
                                    v.wait_ge(exped, 2 * s - 2)
                                nc.vector.tensor_reduce(npeak[s % 2], psum[:, 2 * (s % 2):2 * (s % 2) + 2, 0:wd], AXX,
                                                        ALU.max, negate=True).then_inc(peaked, 1)
                            for v_ in ((2 * s - 2, 2 * s - 1) if 1 <= s <= n else ()):
                                v.wait_ge(high, v_ + 1)
                                if v_ >= nL:
                                    v.wait_ge(summed, v_ - nL + 1)
                                k = len(pairs[v_ // 2]["units"][v_ % 2]["keys"]) * P
                                nc.vector.tensor_tensor(probL[:, v_ % nL, 0:k], bank[4 + v_ % 2][:, 0:k],
                                                        probT[:, v_ % nT, 0:k], ALU.subtract).then_inc(low, 1)
                            p = s - 3
                            if p >= 0:
                                v.wait_ge(exped, 2 * p + 2)
                                link(nc.vector.reciprocal(by[p % 2], total[p % 4]))
                                if pairs[p]["gates"] is not None:
                                    link(nc.vector.tensor_tensor(by[p % 2], by[p % 2], pairs[p]["gates"], ALU.mult))
                                v.wait_ge(summed, 2 * p + 2)
                                if p >= nput:
                                    v.wait_ge(collected, p - nput + 1)
                                nc.vector.tensor_tensor(put[:, p % nput, :, :],
                                                        bank[6 + p % 2][:, 0:2 * P].rearrange("p (b c) -> p b c", c=P),
                                                        by[p % 2].unsqueeze(2).to_broadcast([P, 2, P]),
                                                        ALU.mult).then_inc(divided, 1)

                    @block.gpsimd
                    def _(g):
                        link = Chain(g, chain_g)
                        for p in range(n):
                            g.wait_ge(divided, p + 1)
                            pairs[p]["collect"](link, put[:, p % nput, :, :]).then_inc(collected, 1)

        def collect_heads(dst):
            def f(link, put):
                return nc.gpsimd.tensor_tensor(dst, put[:, :, 0:HD], put[:, :, HD:P], ALU.add)
            return f

        def collect_branches(dst):
            def f(link, put):
                link(nc.gpsimd.tensor_tensor(put[:, 0, :], put[:, 0, :], put[:, 1, :], ALU.add))
                link(nc.gpsimd.tensor_tensor(put[:, 0, 0:HD], put[:, 0, 0:HD], put[:, 0, HD:P], ALU.add))
                return nc.gpsimd.tensor_tensor(dst, dst, put[:, 0, 0:HD], ALU.add)
            return f

        recip = [stat[:, 30 + i:31 + i] for i in range(2)]

        def finish_plain(dst):
            def f(link, u, ps, total):
                link(nc.vector.reciprocal(recip[u % 2], total))
                return scaled(True, dst, ps[:, 0:dst.shape[-1]], recip[u % 2])
            return f

        def finish_parts(dst):
            def f(link, u, ps, total):
                link(nc.vector.reciprocal(recip[u % 2], total))
                link(scaled(True, dst, ps[:, 0:HD], recip[u % 2]))
                return nc.vector.scalar_tensor_tensor(dst, ps[:, HD:2 * HD], recip[u % 2], dst, ALU.mult, ALU.add)
            return f

        def split_values(link, high, low, src):
            link(nc.vector.tensor_copy(high, src))
            return nc.vector.tensor_tensor(low, src, high, ALU.subtract)

        def residual_add(c, t, ps, link):
            dst = x[:, t, c * BANK:(c + 1) * BANK]
            return nc.vector.tensor_tensor(dst, dst, ps, ALU.add)

        load_stage()
        norm_stage("anorm", x, NT, w['attn_norm'], (hT, hL), src_in=x_in)

        mixers = ctx.enter_context(ExitStack())
        convT = sb("convT", [P, 2, S], mixers)
        yt = sb("yt", [P, NT, D], mixers)
        inner = ExitStack()
        tokv = sb("tokv", [P, NT, 512], inner)
        mqkT = sb("mqkT", [P, 4, S], inner)
        rows = sb("rows", [P, 2, S], inner)
        mcol = sb("mcol", [P, 2, NT, ML_H], inner)
        softmaxed = ExitStack()
        qkT = sb("qkT", [P, 9, S], softmaxed)
        vfox = sb("vfox", [P, NT, FOX_H, P], softmaxed, F32R)
        vswa = sb("vswa", [P, NT, 2, P], softmaxed, F32R)

        normed = ExitStack()
        tokqk = sb("tokqk", [P, NT, 1152], normed)
        def evac_a(c, t, ps, link):
            if c in (1, 5):
                v = (vfox, vswa)[c // 5]
                src = ps[:, 128 * (c // 5):256].rearrange("p (h d) -> p h d", d=HD)
                ins = split_values(link, v[:, t, :, 0:HD], v[:, t, :, HD:P], src)
                return ins if c == 1 else copy(True, tokqk[:, t, 1024:1152], ps[:, 0:128])
            dst, d0 = ((tokqk, 0), None, (tokv, 0), (tokv, 256), (tokqk, 512))[c]
            return copy(link is not None, dst[:, t, d0:d0 + ps.shape[-1]], ps)

        def half(c):
            return [True, False, True, False]

        def half_but_values(c):
            return [True] * NT if c in (1, 5) else half(c)
        token_stage("projA", (hT, hL), ND, [('w_in', n) for _, n in TOKEN_CHUNKS_A], evac_a, half_but_values)

        def qk_norm_stage():
            nh = NT * 18
            flat = tokqk[:, :, :].rearrange("p t (h d) -> p (t h) d", d=HD)
            sqr = yt[:, :, :].rearrange("p a b -> p (a b)")[:, 0:3 * 1152].rearrange("p (h d) -> p h d", d=HD)
            with ExitStack() as sc:
                ssum, rooted, chain = sem("qkn_sum", sc), sem("qkn_root", sc), sem("qkn_chain", sc)
                squared, recip_done = sem("qkn_squared", sc), sem("qkn_recip", sc)
                cut = NT * 12
                with nc.Block() as block:
                    @block.vector
                    def _(v):
                        link = Chain(v, chain)
                        mid, end = 18, 54
                        link(nc.vector.tensor_tensor(sqr[:, 0:mid, :], flat[:, 0:mid, :], flat[:, 0:mid, :], ALU.mult))
                        link(nc.vector.tensor_reduce(stat[:, 0:mid], sqr[:, 0:mid, :], AXX, ALU.add))
                        link(nc.vector.tensor_tensor(sqr[:, 0:mid, :], flat[:, end:nh, :], flat[:, end:nh, :], ALU.mult))
                        link(nc.vector.tensor_reduce(stat[:, end:nh], sqr[:, 0:mid, :], AXX, ALU.add))
                        v.wait_ge(squared, 1)
                        nc.vector.tensor_reduce(stat[:, mid:end], sqr[:, mid:end, :], AXX, ALU.add).then_inc(ssum, 1)
                        nc.vector.tensor_scalar(stat[:, 148:149], par[:, K_FQ:K_FQ + 1], HD ** -0.5, None, ALU.mult)
                        nc.vector.tensor_scalar(stat[:, 149:150], par[:, K_SQ:K_SQ + 1], HD ** -0.5, None, ALU.mult)
                        v.wait_ge(rooted, 1)
                        nc.vector.reciprocal(stat[:, 0:nh], stat[:, 72:72 + nh]).then_inc(recip_done, 1)
                        v.wait_ge(recip_done, 1)
                        by = stat[:, 0:cut].unsqueeze(2).to_broadcast([P, cut, HD])
                        nc.vector.tensor_tensor(flat[:, 0:cut, :], flat[:, 0:cut, :], by, ALU.mult)

                    @block.gpsimd
                    def _(g):
                        g.wait_ge(recip_done, 1)
                        by = stat[:, cut:nh].unsqueeze(2).to_broadcast([P, nh - cut, HD])
                        nc.gpsimd.tensor_tensor(flat[:, cut:nh, :], flat[:, cut:nh, :], by, ALU.mult)

                    @block.scalar
                    def _(a):
                        nc.scalar.activation(sqr[:, 18:54, :], flat[:, 18:54, :], ACT.Square).then_inc(squared, 1)
                        a.wait_ge(ssum, 1)
                        nc.scalar.activation(stat[:, 72:72 + nh], stat[:, 0:nh], ACT.Sqrt, bias=eps,
                                             scale=1.0 / HD).then_inc(rooted, 1)

        qk_norm_stage()

        def tok(tile, c0):
            return lambda t: tile[:, t, c0:c0 + P]

        turn_stage("qkT", [(tok(tokqk, 0), qkT[:, 0, :], stat[:, 148:149]), (tok(tokqk, P), qkT[:, 1, :], stat[:, 148:149]),
                           (tok(tokqk, 256), qkT[:, 2, :], par[:, K_FK:K_FK + 1]),
                           (tok(tokqk, 384), qkT[:, 3, :], par[:, K_FK:K_FK + 1])]
                   + [(tok(tokqk, 512 + i * P), qkT[:, 4 + i, :], stat[:, 149:150]) for i in range(4)]
                   + [(tok(tokqk, 1024), qkT[:, 8, :], par[:, K_SK:K_SK + 1])])
        normed.close()

        conv = ExitStack()
        cx = sb("cx", [P, 6, 514], conv)
        wsm = sb("wsm", [P, ND, 96], conv)
        wsh = sb("wsh", [P, ND, 96], conv, F32R)
        wsl = sb("wsl", [P, ND, 96], conv, F32R)
        rb = sb("rb", [P, 3, S], conv)
        relT = sb("relT", [BUCKETS + 1, SWA_H], conv)
        biasrow = sb("biasrow", [SWA_H, 384], conv)

        def evac_feat(i, ps, vector):
            if i < 2:
                return scaled(vector, mqkT[:, i, :], ps, HD ** -0.5) if vector else \
                    nc.scalar.activation(mqkT[:, i, :], ps, ACT.Copy, scale=HD ** -0.5)
            if i < 4:
                return copy(vector, mqkT[:, i, :], ps)
            return copy(vector, cx[:, i - 4, 2:514], ps)

        feature_stage("projAT", (hT, hL), S, ['w_in'] * 10, evac_feat)

        scratch_bias = w['bias_rows']

        def small_stage():
            with ExitStack() as sc:
                names = ("zeroed", "cols_in", "misc", "logits", "logits_in", "absed", "exped", "logged", "bias_mm",
                         "bias_row", "bias_out", "chain", "scanned", "turned", "achain", "ws_split")
                s = {k: sem(f"small_{k}", sc) for k in names}
                with nc.Block() as block:
                    @block.gpsimd
                    def _(g):
                        nc.gpsimd.memset(wsm[:, :, :], 0.0).then_inc(s["zeroed"], 1)
                        g.wait_ge(s["zeroed"], 1)
                        nc.gpsimd.memset(relT[BUCKETS:BUCKETS + 1, :], 1.0).then_inc(s["zeroed"], 1)

                    @block.sync
                    def _(sp):
                        sp.wait_ge(s["zeroed"], 2)
                        wv = w['w_in'].rearrange("(k p) c -> p k c", p=P)
                        for at, c0 in ((0, FF), (32, MI), (64, MF)):
                            sp.dma_start(wsm[:, :, at:at + 4], wv[:, :, c0:c0 + 4]).then_inc(s["cols_in"], 16)
                        sp.dma_start(relT[0:BUCKETS, :], w['rel_bias']).then_inc(s["misc"], 16)
                        sp.wait_ge(s["bias_row"], 1)
                        sp.dma_start(scratch_bias, biasrow[:, :]).then_inc(s["bias_out"], 16)
                        sp.wait_ge(s["bias_out"], 16)
                        sp.wait_ge(s["misc"], 16)

                    @block.tensor
                    def _(pe):
                        pe.wait_ge(s["ws_split"], 2)
                        for k in range(ND):
                            mm = product(bank[0][0:96, :], (wsh[:, k, :], wsl[:, k, :]), (hT[:, k, :], hL[:, k, :]),
                                         k == 0, k == ND - 1)
                        mm.then_inc(s["logits"], 1)
                        pe.wait_ge(s["misc"], 16)
                        pe.wait_ge(s["zeroed"], 2)
                        nc.tensor.matmul(bank[1][0:SWA_H, 0:384], lhsT=relT[:, :],
                                         rhs=const[0:BUCKETS + 1, C_OH:C_OH + 384],
                                         start=True, stop=True).then_inc(s["bias_mm"], 1)
                        pe.wait_ge(s["scanned"], 1)
                        for i in range(2):
                            for t in range(NT):
                                mm = nc.tensor.transpose(bank[2 + i][:, t * 4:t * 4 + 4],
                                                         rb[32:36, i, t * P:(t + 1) * P],
                                                         const[32:36, C_ID + 32:C_ID + 36])
                        mm.then_inc(s["turned"], 1)

                    @block.scalar
                    def _(a):
                        a.wait_ge(s["logits"], 1)
                        nc.scalar.activation(rb[0:96, 0, :], bank[0][0:96, :], ACT.Identity,
                                             bias=par[0:96, K_BIAS:K_BIAS + 1]).then_inc(s["logits_in"], 1)
                        link = Chain(a, s["achain"])
                        a.wait_ge(s["logits_in"], 1)
                        link(nc.scalar.activation(rb[0:96, 1, :], rb[0:96, 0, :], ACT.Abs))
                        link(nc.scalar.activation(rb[0:96, 1, :], rb[0:96, 1, :], ACT.Exp, scale=-1.0))
                        nc.scalar.activation(rb[0:96, 2, :], rb[0:96, 1, :], ACT.Ln, bias=1.0).then_inc(s["logged"], 1)
                        a.wait_ge(s["bias_mm"], 1)
                        nc.scalar.activation(biasrow[:, :], bank[1][0:SWA_H, 0:384], ACT.Copy).then_inc(s["bias_row"], 1)

                    @block.vector
                    def _(v):
                        link = Chain(v, s["chain"])
                        v.wait_ge(s["cols_in"], 48)
                        nc.vector.tensor_copy(wsh[:, :, :], wsm[:, :, :]).then_inc(s["ws_split"], 1)
                        v.wait_ge(s["ws_split"], 1)
                        nc.vector.tensor_tensor(wsl[:, :, :], wsm[:, :, :], wsh[:, :, :], ALU.subtract).then_inc(s["ws_split"], 1)
                        nc.vector.memset(cx[:, 2:4, 0:2], 0.0)
                        link(nc.vector.tensor_tensor(cx[:, 2:4, 2:514], cx[:, 2:4, 2:514], cx[:, 0:2, 2:514], ALU.mult))
                        for i in range(2):
                            z = cx[:, 2 + i, :]
                            tap = [par[:, K_CONV + 2 * j + i:K_CONV + 2 * j + i + 1] for j in range(3)]
                            link(nc.vector.tensor_scalar(convT[:, i, :], z[:, 2:514], tap[2], None, ALU.mult))
                            link(nc.vector.scalar_tensor_tensor(convT[:, i, :], z[:, 1:513], tap[1], convT[:, i, :], ALU.mult, ALU.add))
                            link(nc.vector.scalar_tensor_tensor(convT[:, i, :], z[:, 0:512], tap[0], convT[:, i, :], ALU.mult, ALU.add))
                            nc.vector.tensor_tensor(convT[:, i, :], convT[:, i, :], cx[:, 4 + i, 2:514], ALU.mult)
                        v.wait_ge(s["logged"], 1)
                        link(nc.vector.tensor_scalar(rb[0:96, 1, :], rb[0:96, 0, :], 0.0, None, ALU.min))
                        link(nc.vector.tensor_tensor(rb[0:96, 1, :], rb[0:96, 1, :], rb[0:96, 2, :], ALU.subtract))
                        link(nc.vector.tensor_tensor_scan(rb[0:96, 2, :], rb[0:96, 1, :], rb[0:96, 1, :], 0.0,
                                                          ALU.add, ALU.bypass))
                        nc.vector.tensor_scalar(rows[0:4, 0, :], rb[0:4, 2, :], -1.0, None, ALU.mult)
                        link(nc.vector.tensor_copy(rb[32:36, 1, :], rb[64:68, 2, :]))
                        link(nc.vector.tensor_tensor(rb[32:36, 0, :], rb[32:36, 0, :], rb[32:36, 1, :], ALU.subtract))
                        link(nc.vector.tensor_tensor_scan(rb[32:36, 2, :], rb[32:36, 0, :], rb[32:36, 0, :], 0.0,
                                                          ALU.max, ALU.bypass))
                        link(nc.vector.tensor_scalar(rows[32:36, 1, :], rb[32:36, 2, :], -1.0, None, ALU.mult))
                        nc.vector.tensor_tensor(rb[32:36, 1, :], rows[32:36, 1, :], rb[32:36, 1, :],
                                                ALU.subtract).then_inc(s["scanned"], 1)
                        v.wait_ge(s["turned"], 1)
                        for i in range(2):
                            nc.vector.tensor_copy(mcol[:, i, :, :], bank[2 + i][:, 0:16].rearrange("p (t h) -> p t h", h=4))

        small_stage()
        conv.close()

        toep = [sb(f"toep{i}", [P, SWA_H, 258], softmaxed, F32R) for i in range(2)]

        def bias_stage():
            with ExitStack() as sc:
                raw = sb("raw", [P, SWA_H, 256], sc)
                sinks = sb("sinks", [P, SWA_H], sc)
                raw_in, high = sem("raw_in", sc), sem("raw_high", sc)
                with nc.Block() as block:
                    @block.sync
                    def _(sp):
                        skew = bass.AP(tensor=scratch_bias.tensor, offset=scratch_bias.offset,
                                       ap=[[1, P], [384, SWA_H], [1, 256]])
                        sp.dma_start(raw[:, :, :], skew).then_inc(raw_in, 16)
                        sp.dma_start(sinks[:, :], w['swa_sinks'].to_broadcast([P, SWA_H])).then_inc(raw_in, 16)

                    @block.vector
                    def _(v):
                        v.wait_ge(raw_in, 32)
                        sink = sinks[:, :].unsqueeze(2)
                        nc.vector.tensor_copy(toep[0][:, :, 0:256], raw[:, :, :]).then_inc(high, 1)
                        nc.vector.tensor_copy(toep[0][:, :, 256:257], sink).then_inc(high, 1)
                        for part_ in toep:
                            nc.vector.tensor_scalar(part_[:, :, 257:258], sink, 0.0, None, ALU.mult)
                        v.wait_ge(high, 2)
                        nc.vector.tensor_tensor(toep[1][:, :, 0:256], raw[:, :, :], toep[0][:, :, 0:256], ALU.subtract)
                        nc.vector.tensor_tensor(toep[1][:, :, 256:257], sink, toep[0][:, :, 256:257], ALU.subtract)

        bias_stage()
        attn = ExitStack()
        scratch = (sb("prob", [P, 4, 258], attn), sb("probT", [P, 4, 256], attn, F32R),
                   sb("probL", [P, 3, 256], attn, F32R), sb("put", [P, 2, 2, P], attn))

        def part(h):
            return slice(HD * (h % 2), HD * (h % 2) + HD)

        def q_tile(t):
            return slice(t * P, (t + 1) * P)

        fox_units = []
        for t in range(NT):
            for h in range(FOX_H):
                wd = (t + 1) * P
                fox_units.append({
                    "width": wd,
                    "scores": [(0, wd, qkT[part(h), h // 2, q_tile(t)], qkT[part(h), 2 + h // 2, 0:wd]),
                               (0, wd, const[0:4, C_SEL + h * P:C_SEL + (h + 1) * P], rows[0:4, 0, 0:wd]),
                               (t * P, P, ident_r, mask_r)],
                    "keys": [(j * P, vfox[:, j, h, :]) for j in range(t + 1)],
                    "finish": finish_parts(yt[:, t, h * HD:(h + 1) * HD])})

        swa_units = []
        for t in range(NT):
            for h in range(SWA_H):
                g, i = h // 4, h % 4
                k0 = max(t - 1, 0)
                nk = (t + 1 - k0) * P
                hp = slice(HD * g, HD * g + HD)
                swa_units.append({
                    "width": nk + 1,
                    "scores": [(0, nk + 2, anti_r, toep[0][:, h, 256 - nk:258]),
                               (0, nk + 2, anti_r, toep[1][:, h, 256 - nk:258]),
                               (0, nk, qkT[hp, 4 + i, q_tile(t)], qkT[hp, 8, k0 * P:k0 * P + nk])],
                    "keys": [(j * P, vswa[:, k0 + j, g, :]) for j in range(nk // P)]})
        swa_pairs = [{"units": swa_units[2 * p:2 * p + 2], "gates": None,
                      "collect": collect_heads(yt[:, p // 4, 512 + (p % 4) * P:512 + (p % 4 + 1) * P]
                                               .rearrange("p (h d) -> p h d", d=HD))}
                     for p in range(NT * SWA_H // 2)]
        pair_attention_stage("swa", swa_pairs, scratch)
        attn.close()
        attn = ExitStack()
        scratch = (sb("fprob", [P, 3, S], attn), sb("fprobT", [P, 3, S], attn, F32R), sb("fprobL", [P, 2, S], attn, F32R))
        attention_stage("fox", fox_units, scratch)

        attn.close()
        softmaxed.close()
        ml = ExitStack()
        v1 = sb("v1", [P, NT, ML_H, HD + 1], ml)
        sw = sb("sw", [P, 2, 10 * P], ml)
        sw_at = [0, 4 * P, 7 * P, 9 * P]
        decay = sb("decay", [P, 2, S], ml)
        gain_h = sb("gain_h", [P, 256], ml)

        def mlstm_stage():
            n = ML_H * NT
            ocol = HD + 1
            with ExitStack() as sc:
                ones_in, qk, dec, dexp, weighted, summed, taken, gain_in = (
                    sem(f"ml_{k}", sc) for k in ("ones", "qk", "dec", "dexp", "weighted", "summed", "taken", "gain"))
                with nc.Block() as block:
                    @block.sync
                    def _(sp):
                        sp.dma_start(gain_h[:, :], w['mlstm_h_gain'].to_broadcast([P, 256])).then_inc(gain_in, 16)
                        sp.wait_ge(gain_in, 16)

                    @block.gpsimd
                    def _(g):
                        nc.gpsimd.tensor_copy(v1[:, :, :, 0:HD],
                                              tokv[:, :, 0:256].rearrange("p t (h d) -> p t h d", d=HD)).then_inc(ones_in, 1)
                        g.wait_ge(ones_in, 1)
                        nc.gpsimd.memset(v1[:, :, :, HD:HD + 1], 1.0).then_inc(ones_in, 1)

                    @block.tensor
                    def _(pe):
                        def values(h):
                            pe.wait_ge(weighted, NT * (h + 1))
                            if h >= 2:
                                pe.wait_ge(taken, h - 1)
                            for t in range(NT):
                                for j in range(t + 1):
                                    mm = nc.tensor.matmul(bank[4 + h % 2][:, t * ocol:(t + 1) * ocol],
                                                          lhsT=sw[:, h % 2, sw_at[j] + (t - j) * P:sw_at[j] + (t - j + 1) * P], rhs=v1[:, j, h, :],
                                                          start=(j == 0), stop=(j == t))
                            mm.then_inc(summed, 1)

                        pe.wait_ge(ones_in, 2)
                        for h in range(ML_H):
                            hp = part(h)
                            for j in range(NT):
                                u = h * NT + j
                                if u >= 2:
                                    pe.wait_ge(weighted, u - 1)
                                c0 = j * P
                                nc.tensor.matmul(bank[2 + u % 2][:, c0:S], lhsT=const[32:36, C_SEL + h * P:C_SEL + (h + 1) * P],
                                                 rhs=rows[32:36, 1, c0:S], start=True, stop=False)
                                nc.tensor.matmul(bank[2 + u % 2][:, c0:c0 + P], lhsT=ident, rhs=mask_t,
                                                 start=False, stop=True).then_inc(dec, 1)
                                nc.tensor.matmul(bank[u % 2][:, c0:S], lhsT=mqkT[hp, 2 + h // 2, q_tile(j)],
                                                 rhs=mqkT[hp, h // 2, c0:S], start=True, stop=True).then_inc(qk, 1)
                            if h >= 1:
                                values(h - 1)
                        values(ML_H - 1)

                    @block.scalar
                    def _(a):
                        for u in range(n):
                            h, j = u // NT, u % NT
                            a.wait_ge(dec, u + 1)
                            if u >= 2:
                                a.wait_ge(weighted, u - 1)
                            nc.scalar.activation(decay[:, u % 2, j * P:S], bank[2 + u % 2][:, j * P:S], ACT.Exp,
                                                 bias=mcol[:, 0, j, h:h + 1]).then_inc(dexp, 1)

                    @block.vector
                    def _(v):
                        def take(h):
                            v.wait_ge(summed, h + 1)
                            nc.vector.tensor_copy(ho[:, h, :, :],
                                                  bank[4 + h % 2][:, 0:NT * ocol].rearrange("p (t c) -> p t c", c=ocol)).then_inc(taken, 1)

                        for h in range(ML_H):
                            for j in range(NT):
                                u = h * NT + j
                                v.wait_ge(qk, u + 1)
                                v.wait_ge(dexp, u + 1)
                                if h >= 2:
                                    v.wait_ge(summed, h - 1)
                                nc.vector.tensor_tensor(sw[:, h % 2, sw_at[j]:sw_at[j] + S - j * P], bank[u % 2][:, j * P:S],
                                                        decay[:, u % 2, j * P:S], ALU.mult).then_inc(weighted, 1)
                            if h >= 2:
                                take(h - 2)
                        take(ML_H - 2)
                        take(ML_H - 1)

        ho = sb("ho", [P, ML_H, NT, HD + 1], ml)
        hh = sb("hh", [P, ML_H, NT, HD], ml)
        hs = sb("hs", [P, ML_H, NT, HD], ml)
        mlstm_stage()

        def mlstm_out_stage():
            nht = ML_H * NT
            with ExitStack() as sc:
                em, sums, root, sig, chain = (sem(f"mo_{k}", sc) for k in ("em", "sums", "root", "sig", "chain"))
                with nc.Block() as block:
                    @block.scalar
                    def _(a):
                        nc.scalar.activation(stat[:, 0:nht].rearrange("p (h t) -> p h t", t=NT),
                                             mcol[:, 1, :, :].rearrange("p t h -> p h t"), ACT.Exp).then_inc(em, 1)
                        den = ho[:, :, :, HD:HD + 1].rearrange("p h t o -> p (h t o)")
                        nc.scalar.activation(stat[:, 48:48 + nht], den, ACT.Abs).then_inc(em, 1)
                        a.wait_ge(sums, 1)
                        nc.scalar.activation(stat[:, 32:32 + nht], stat[:, 16:16 + nht], ACT.Sqrt, bias=eps,
                                             scale=1.0 / HD).then_inc(root, 1)
                        nc.scalar.activation(tokv[:, :, 256:512], tokv[:, :, 256:512], ACT.Sigmoid).then_inc(sig, 1)

                    @block.vector
                    def _(v):
                        link = Chain(v, chain)
                        v.wait_ge(em, 2)
                        link(nc.vector.tensor_tensor(stat[:, 48:48 + nht], stat[:, 48:48 + nht], stat[:, 0:nht], ALU.max))
                        link(nc.vector.reciprocal(stat[:, 64:64 + nht], stat[:, 48:48 + nht]))
                        num = ho[:, :, :, 0:HD].rearrange("p h t d -> p (h t) d")
                        hv = hh[:, :, :, :].rearrange("p h t d -> p (h t) d")
                        hq = hs[:, :, :, :].rearrange("p h t d -> p (h t) d")
                        link(nc.vector.tensor_tensor(hv, num, stat[:, 64:64 + nht].unsqueeze(2).to_broadcast([P, nht, HD]), ALU.mult))
                        link(nc.vector.tensor_tensor(hq, hv, hv, ALU.mult))
                        nc.vector.tensor_reduce(stat[:, 16:16 + nht], hq, AXX, ALU.add).then_inc(sums, 1)
                        v.wait_ge(root, 1)
                        link(nc.vector.reciprocal(stat[:, 80:80 + nht], stat[:, 32:32 + nht]))
                        link(nc.vector.tensor_tensor(hv, hv, stat[:, 80:80 + nht].unsqueeze(2).to_broadcast([P, nht, HD]), ALU.mult))
                        v.wait_ge(sig, 1)
                        for t in range(NT):
                            link(nc.vector.tensor_tensor(hs[:, :, t, :], hh[:, :, t, :],
                                                         gain_h[:, :].rearrange("p (h d) -> p h d", d=HD), ALU.mult))
                            nc.vector.tensor_tensor(yt[:, t, 256:512].rearrange("p (h d) -> p h d", d=HD), hs[:, :, t, :],
                                                    tokv[:, t, 256:512].rearrange("p (h d) -> p h d", d=HD), ALU.mult)

        mlstm_out_stage()
        ml.close()
        inner.close()

        merge = ExitStack()
        mT = sb("mT", [P, ND, S], merge, F32R)
        mL = sb("mL", [P, ND, S], merge, F32R)
        branches = ExitStack()
        yT = sb("yT", [P, 10, S], branches, F32R)
        yL = sb("yL", [P, 10, S], branches, F32R)
        turn_split_stage("yT", [(tok(yt, c * P), (yT[:, y, :], yL[:, y, :]))
                                for c, y in enumerate((0, 1, 4, 5, 6, 7, 8, 9))],
                         [(convT[:, i, :], (yT[:, 2 + i, :], yL[:, 2 + i, :])) for i in range(2)])
        gate = sb("gate", [P, 4, S], branches)
        branch_tiles = ((0, 1), (2, 3), (4, 5), (6, 7, 8, 9))
        branch_w = ('w_fox_out', 'w_conv_out', 'w_mlstm_out', 'w_swa_out')

        def merge_stage():
            n0 = state["used"]
            n = ND * N_BRANCH
            with ExitStack() as sc:
                sig, merged, total, high, low, chain = (
                    sem(f"mg_{k}", sc) for k in ("sig", "merged", "total", "high", "low", "chain"))

                def gate_tile(d, b):
                    return n0 + 8 * d + b

                def out_tile(d, b):
                    return n0 + 8 * d + 4 + b

                with nc.Block() as block:
                    @block.tensor
                    def _(pe):
                        for d in range(ND):
                            for b in range(N_BRANCH):
                                if d:
                                    pe.wait_ge(sig, (d - 1) * 4 + b + 1)
                                wh, wl = tile_for(pe, gate_tile(d, b), 'w_in')
                                for k in range(ND):
                                    mm = product(bank[b][:, :], (wh[:, k, :], wl[:, k, :]), (hT[:, k, :], hL[:, k, :]),
                                                 k == 0, k == ND - 1)
                                mm.then_inc(w_used, 1)
                            for b in range(N_BRANCH):
                                if d:
                                    pe.wait_ge(merged, (d - 1) * 4 + b + 1)
                                wh, wl = tile_for(pe, out_tile(d, b), branch_w[b])
                                kt = len(branch_tiles[b])
                                for k, y in enumerate(branch_tiles[b]):
                                    mm = product(bank[4 + b][:, :], (wh[:, k, :], wl[:, k, :]), (yT[:, y, :], yL[:, y, :]),
                                                 k == 0, k == kt - 1)
                                mm.then_inc(w_used, 1)

                    @block.scalar
                    def _(a):
                        def high_part(d):
                            a.wait_ge(total, d + 1)
                            copy(False, mT[:, d, :], gate[:, 0, :]).then_inc(high, 1)

                        for u in range(n):
                            d, b = u // 4, u % 4
                            if b == 0 and d:
                                split_high(a, out_tile(d - 1, 3) + SPLIT)
                                high_part(d - 1)
                                a.wait_ge(low, d)
                            split_high(a, gate_tile(d, b) + SPLIT)
                            a.wait_ge(w_used, gate_tile(d, b) + 1)
                            nc.scalar.activation(gate[:, b, :], bank[b][:, :], ACT.Sigmoid).then_inc(sig, 1)
                        split_high(a, out_tile(ND - 1, 3) + SPLIT)
                        high_part(ND - 1)
                        split_high(a, n0 + 8 * ND + SPLIT)

                    @block.gpsimd
                    def _(g):
                        split_low(g, n0 + 8 * ND + SPLIT)

                    @block.vector
                    def _(v):
                        link = Chain(v, chain)
                        for u in range(n):
                            d, b = u // 4, u % 4
                            v.wait_ge(sig, u + 1)
                            v.wait_ge(w_used, out_tile(d, b) + 1)
                            nc.vector.tensor_tensor(gate[:, b, :], gate[:, b, :], bank[4 + b][:, :], ALU.mult).then_inc(merged, 1)
                            v.wait_ge(merged, u + 1)
                            if b in (1, 2):
                                link(nc.vector.tensor_tensor(gate[:, 0, :], gate[:, 0, :], gate[:, b, :], ALU.add))
                            if b == 3:
                                nc.vector.tensor_tensor(gate[:, 0, :], gate[:, 0, :], gate[:, 3, :], ALU.add).then_inc(total, 1)
                                v.wait_ge(high, d + 1)
                                nc.vector.tensor_tensor(mL[:, d, :], gate[:, 0, :], mT[:, d, :], ALU.subtract).then_inc(low, 1)

                    @block.sync
                    def _(sp):
                        load_weights(sp, n0 + 8 * ND + SPLIT)
            state["used"] = n0 + 8 * ND

        merge_stage()
        branches.close()

        def all_v(c):
            return [True] * NT

        token_stage("wmerge", (mT, mL), ND, [('w_merge_out', BANK)] * 2, residual_add, all_v,
                    norm_gain=w['ffn_norm'], norm_dst=(hT, hL))
        merge.close()
        mixers.close()

        def ffn_stage(name, gate_w, up_w, actT, taps, f0):
            n0 = state["used"]
            with ExitStack() as sc:
                g = sb(f"{name}_g", [P, 2, S + 2], sc)
                cv = sb(f"{name}_cv", [P, 2, S], sc)
                sl = sb(f"{name}_sl", [P, 2, S], sc)
                ac = sb(f"{name}_ac", [P, 2, S], sc)
                silued, acted, copied, convd, high, low, chain = (
                    sem(f"{name}_{k}", sc) for k in ("silued", "acted", "copied", "convd", "high", "low", "chain"))
                with nc.Block() as block:
                    @block.tensor
                    def _(pe):
                        for f in range(FG):
                            for i, wname in enumerate((gate_w, up_w)):
                                if f >= 4:
                                    pe.wait_ge(acted, f - 3)
                                wh, wl = tile_for(pe, n0 + 2 * f + i, wname)
                                for k in range(ND):
                                    mm = product(bank[2 * (f % 4) + i][:, :], (wh[:, k, :], wl[:, k, :]),
                                                 (hT[:, k, :], hL[:, k, :]), k == 0, k == ND - 1)
                                mm.then_inc(w_used, 1)

                    @block.scalar
                    def _(a):
                        def high_part(f):
                            a.wait_ge(acted, f + 1)
                            copy(False, actT[0][:, f, :], ac[:, f % 2, :]).then_inc(high, 1)

                        for f in range(FG):
                            split_high(a, n0 + 2 * f + SPLIT)
                            a.wait_ge(w_used, n0 + 2 * f + 1)
                            src = bank[2 * (f % 4)][:, :]
                            if taps is not None:
                                if f >= 2:
                                    a.wait_ge(convd, f - 1)
                                nc.scalar.activation(g[:, f % 2, 2:], src, ACT.Copy).then_inc(copied, 1)
                                a.wait_ge(convd, f + 1)
                                src = cv[:, f % 2, :]
                            if f >= 2:
                                a.wait_ge(acted, f - 1)
                            nc.scalar.activation(sl[:, f % 2, :], src, ACT.Silu).then_inc(silued, 1)
                            split_high(a, n0 + 2 * f + 1 + SPLIT)
                            if f >= 1:
                                high_part(f - 1)
                        high_part(FG - 1)
                        split_high(a, n0 + 2 * FG + SPLIT)

                    @block.vector
                    def _(v):
                        link = Chain(v, chain)
                        if taps is not None:
                            link(nc.vector.memset(g[:, :, 0:2], 0.0))

                        def low_part(f):
                            v.wait_ge(high, f + 1)
                            nc.vector.tensor_tensor(actT[1][:, f, :], ac[:, f % 2, :], actT[0][:, f, :],
                                                    ALU.subtract).then_inc(low, 1)

                        for f in range(FG):
                            if taps is not None:
                                v.wait_ge(copied, f + 1)
                                if f >= 2:
                                    v.wait_ge(silued, f - 1)
                                c = cv[:, f % 2, :]
                                link(nc.vector.tensor_scalar(c, g[:, f % 2, 2:514], taps(2, f0 + f), None, ALU.mult))
                                link(nc.vector.scalar_tensor_tensor(c, g[:, f % 2, 1:513], taps(1, f0 + f), c, ALU.mult, ALU.add))
                                nc.vector.scalar_tensor_tensor(c, g[:, f % 2, 0:512], taps(0, f0 + f), c,
                                                               ALU.mult, ALU.add).then_inc(convd, 1)
                            v.wait_ge(silued, f + 1)
                            v.wait_ge(w_used, n0 + 2 * f + 2)
                            if f >= 2:
                                v.wait_ge(low, f - 1)
                            nc.vector.tensor_tensor(ac[:, f % 2, :], sl[:, f % 2, :], bank[2 * (f % 4) + 1][:, :],
                                                    ALU.mult).then_inc(acted, 1)
                            if f >= 1:
                                low_part(f - 1)
                        low_part(FG - 1)

                    @block.gpsimd
                    def _(g_):
                        split_low(g_, n0 + 2 * FG + SPLIT)

                    @block.sync
                    def _(sp):
                        load_weights(sp, n0 + 2 * FG + SPLIT)
            state["used"] = n0 + 2 * FG

        def ffn(name, gate_w, up_w, down_w, taps, norm_gain, norm_dst):
            with ExitStack() as sc:
                actT = tuple(sb(f"{name}_act{i}", [P, FG, S], sc, F32R) for i in range(2))
                for f0 in range(0, NF, FG):
                    ffn_stage(f"{name}u{f0}", gate_w, up_w, actT, taps, f0)
                    token_stage(f"{name}d{f0}", actT, FG, [(down_w, BANK)] * 2, residual_add, all_v,
                                norm_gain=norm_gain if f0 + FG == NF else None, norm_dst=norm_dst)

        ffn("ffn1", 'w_gate', 'w_up', 'w_down', None, w['norm_mix_w_2'], (hT, hL))

        clear_stage()

        nsa = ExitStack()
        ot = sb("ot", [P, NT, D], nsa)
        nq = sb("nq", [P, NSA_H, S], nsa, F32R)
        nv = sb("nv", [P, NT, 8, P], nsa, F32R)
        ngate = sb("ngate", [P, NT, 48], nsa)
        kcmp = [sb(f"kcmp{i}", [P, NSA_G, 32], nsa, F32R) for i in range(2)]
        vcmp = sb("vcmp", [P, NSA_G, 256], nsa)
        cmp_s = ExitStack()
        kcp = sb("kcp", [P, 2, 8, 132], cmp_s)
        blkh = sb("blkh", [P, 8, P], cmp_s, F32R)
        blkl = sb("blkl", [P, 8, P], cmp_s, F32R)
        hid = sb("hid", [P, 2, CMP_HID], cmp_s)
        hidT = sb("hidT", [P, 4, P], cmp_s)
        w2k = sb("w2k", [P, 2, P], cmp_s)
        w2v = sb("w2v", [P, 2, HD], cmp_s)

        def nsa_q_stage():
            n0 = state["used"]
            with ExitStack() as sc:
                out_v, out_a = sem("nq_outv", sc), sem("nq_outa", sc)
                with nc.Block() as block:
                    @block.tensor
                    def _(pe):
                        for a in range(2):
                            for s in range(4):
                                wh, wl = tile_for(pe, n0 + 4 * a + s, 'nsa_w_in_2')
                                for kk in range(2):
                                    k = 2 * s + kk
                                    for i in range(HPG):
                                        mm = product(bank[4 * a + i][:, :],
                                                     (wh[:, kk, i * P:(i + 1) * P], wl[:, kk, i * P:(i + 1) * P]),
                                                     (hT[:, k, :], hL[:, k, :]), k == 0, k == ND - 1)
                                mm.then_inc(w_used, 1)

                    def parts(a):
                        for i in range(HPG):
                            for j in range(2):
                                yield bank[4 * a + i][HD * j:HD * j + HD, :], (2 * a + j) * HPG + i

                    @block.vector
                    def _(v):
                        for a in range(2):
                            for k, (src, h) in enumerate(parts(a)):
                                v.wait_ge(out_a, 8 * a + k + 1)
                                nc.vector.scalar_tensor_tensor(nq[HD:P, h, :], src, HD ** -0.5, nq[0:HD, h, :],
                                                               ALU.mult, ALU.subtract).then_inc(out_v, 1)

                    @block.scalar
                    def _(e):
                        for a in range(2):
                            split_high(e, n0 + 4 * a + 3 + SPLIT)
                            e.wait_ge(w_used, n0 + 4 * a + 4)
                            for src, h in parts(a):
                                nc.scalar.activation(nq[0:HD, h, :], src, ACT.Copy, scale=HD ** -0.5).then_inc(out_a, 1)

                        split_high(e, n0 + 8 + SPLIT)

                    @block.gpsimd
                    def _(g):
                        split_low(g, n0 + 8 + SPLIT)

                    @block.sync
                    def _(sp):
                        load_weights(sp, n0 + 8 + SPLIT)
            state["used"] = n0 + 8

        nsa_q_stage()

        def evac_kc(i, ps, vector):
            kv, pair = i // 2, i % 2
            for j in range(2):
                g = 2 * pair + j
                src = ps[HD * j:HD * j + HD, :].rearrange("p (n q e) -> p e q n", q=8, e=2)
                for e in range(2):
                    ins = copy(vector, kcp[HD * e:HD * e + HD, kv, :, g * 32:(g + 1) * 32], src[:, e, :, :])
            return ins

        feature_stage("nsaC", (hT, hL), S, ['nsa_w_in_2'] * 4, evac_kc)
        def evac_nsa_tok(c, t, ps, link):
            src = ps[:, 0:256].rearrange("p (g d) -> p g d", d=HD)
            ins = split_values(link, nv[:, t, 4 * c:4 * c + 4, 0:HD], nv[:, t, 4 * c:4 * c + 4, HD:P], src)
            return ins if c == 0 else copy(True, ngate[:, t, :], ps[:, 256:304])

        token_stage("nsaV", (hT, hL), ND, [('nsa_w_in_2', 256), ('nsa_w_in_2', 304)], evac_nsa_tok, all_v)

        def nsa_key_stage():
            n0 = state["used"]
            with ExitStack() as sc:
                high = sem("nk_high", sc)
                with nc.Block() as block:
                    @block.tensor
                    def _(pe):
                        for i in range(4):
                            wh, wl = tile_for(pe, n0 + i, 'nsa_w_in_2')
                            for k in range(ND):
                                mm = product(bank[i][:, :], (wh[:, k, :], wl[:, k, :]), (hT[:, k, :], hL[:, k, :]),
                                             k == 0, k == ND - 1)
                            mm.then_inc(w_used, 1)

                    heads = [(bank[i][HD * j:HD * j + HD, :], 4 * (i // 2) + 2 * (i % 2) + j)
                             for i in range(4) for j in range(2)]

                    @block.scalar
                    def _(a):
                        split_high(a, n0 + 3 + SPLIT)
                        a.wait_ge(w_used, n0 + 4)
                        for src, kb in heads:
                            copy(False, hT[0:HD, kb, :], src).then_inc(high, 1)
                        split_high(a, n0 + 4 + SPLIT)

                    @block.vector
                    def _(v):
                        for k, (src, kb) in enumerate(heads):
                            v.wait_ge(high, k + 1)
                            nc.vector.tensor_tensor(hL[0:HD, kb, :], src, hT[0:HD, kb, :], ALU.subtract)

                    @block.gpsimd
                    def _(g):
                        split_low(g, n0 + 4 + SPLIT)

                    @block.sync
                    def _(sp):
                        load_weights(sp, n0 + 4 + SPLIT)
            state["used"] = n0 + 4

        nsa_key_stage()

        def compress_stage():
            n0 = state["used"]
            units = 32
            with ExitStack() as sc:
                w2_in, high, low, act, turned, taken, second, zeroed, gated = (
                    sem(f"cmp_{k}", sc) for k in ("w2", "high", "low", "act", "turned", "taken", "second", "zeroed", "gated"))

                def block_of(u):
                    kv, m = u // 16, u % 16
                    return kcp[:, kv, m % 8, m // 8:m // 8 + P], par[:, K_PEK + u:K_PEK + u + 1]

                with nc.Block() as block:
                    @block.sync
                    def _(sp):
                        kw = w['nsa_ck_w2_2'].rearrange("(k p) c -> p k c", p=P)
                        sp.dma_start(w2k[:, :, 0:HD], kw).then_inc(w2_in, 16)
                        sp.dma_start(w2k[:, :, HD:P], kw).then_inc(w2_in, 16)
                        sp.dma_start(w2v[:, :, :], w['nsa_cv_w2_2'].rearrange("(k p) c -> p k c", p=P)).then_inc(w2_in, 16)
                        for part_ in (hT, hL):
                            sp.dma_start(part_[HD:P, :, :].bitcast(F32), part_[0:HD, :, :].bitcast(F32)).then_inc(w2_in, 16)
                        load_weights(sp, n0 + 8 + SPLIT)
                        sp.wait_ge(w2_in, 80)

                    @block.gpsimd
                    def _(g):
                        nc.gpsimd.memset(kcp[:, :, :, P:P + 1], 0.0).then_inc(zeroed, 1)
                        g.wait_ge(zeroed, 1)
                        nc.gpsimd.memset(vcmp[:, :, :], 0.0).then_inc(zeroed, 1)
                        g.wait_ge(zeroed, 2)
                        split_low(g, n0 + 8 + SPLIT)

                    @block.tensor
                    def _(pe):
                        for u in range(units):
                            kv, s, kk = u // 16, u // 4, u % 4
                            if kk == 0:
                                wh, wl = tile_for(pe, n0 + s, ('nsa_ck_w1_2', 'nsa_cv_w1_2')[kv])
                            pe.wait_ge(low, u + 1)
                            mm = product(bank[kv][:, 0:CMP_HID], (blkh[:, u % 8, :], blkl[:, u % 8, :]),
                                         (wh[:, kk, :], wl[:, kk, :]), u % 16 == 0, u % 16 == 15)
                            if kk == 3:
                                mm.then_inc(w_used, 1)
                        for kv in range(2):
                            pe.wait_ge(act, kv + 1)
                            for h in range(2):
                                mm = nc.tensor.transpose(bank[2][:, (2 * kv + h) * P:(2 * kv + h + 1) * P],
                                                         hid[:, kv, h * P:(h + 1) * P], ident)
                        mm.then_inc(turned, 1)
                        pe.wait_ge(w2_in, 80)
                        pe.wait_ge(taken, 1)
                        for k in range(2):
                            nc.tensor.matmul(bank[3][:, 0:P], lhsT=w2k[:, k, :], rhs=hidT[:, k, :],
                                             start=(k == 0), stop=(k == 1))
                        for g in range(NSA_G):
                            for k in range(2):
                                mm = nc.tensor.matmul(bank[4][0:32, g * HD:(g + 1) * HD],
                                                      lhsT=hidT[:, 2 + k, g * 32:(g + 1) * 32], rhs=w2v[:, k, :],
                                                      start=(k == 0), stop=(k == 1))
                        mm.then_inc(second, 1)

                    @block.vector
                    def _(v):
                        for u in range(units):
                            v.wait_ge(high, u + 1)
                            blk, pos = block_of(u)
                            nc.vector.scalar_tensor_tensor(blkl[:, u % 8, :], blk, pos, blkh[:, u % 8, :],
                                                           ALU.add, ALU.subtract).then_inc(low, 1)
                        v.wait_ge(turned, 1)
                        nc.vector.tensor_copy(hidT[:, :, :], bank[2][:, :].rearrange("p (k c) -> p k c", c=P)).then_inc(taken, 1)
                        v.wait_ge(second, 1)
                        v.wait_ge(zeroed, 2)
                        src = bank[3][:, 0:P].rearrange("p (g n) -> p g n", n=32)
                        nc.vector.tensor_copy(kcmp[0][:, :, :], src).then_inc(taken, 1)
                        v.wait_ge(taken, 2)
                        nc.vector.tensor_tensor(kcmp[1][:, :, :], src, kcmp[0][:, :, :], ALU.subtract)
                        for i in range(HPG):
                            nc.vector.tensor_copy(vcmp[32 * i:32 * i + 32, :, i * HD:(i + 1) * HD],
                                                  bank[4][0:32, 0:256].rearrange("p (g d) -> p g d", d=HD))

                    @block.scalar
                    def _(a):
                        def hidden(kv):
                            a.wait_ge(w_used, n0 + 4 * kv + 4)
                            nc.scalar.activation(hid[:, kv, :], bank[kv][:, 0:CMP_HID], ACT.Gelu_apprx_tanh).then_inc(act, 1)

                        a.wait_ge(zeroed, 1)
                        for s in range(8):
                            if s >= 2:
                                a.wait_ge(w_used, n0 + s - 1)
                            for u in range(4 * s, 4 * s + 4):
                                blk, pos = block_of(u)
                                nc.scalar.activation(blkh[:, u % 8, :], blk, ACT.Identity, bias=pos).then_inc(high, 1)
                            split_high(a, n0 + s + SPLIT)
                        for kv in range(2):
                            hidden(kv)
                        nc.scalar.activation(ngate[:, :, :], ngate[:, :, :], ACT.Sigmoid).then_inc(gated, 1)
                        split_high(a, n0 + 8 + SPLIT)
            state["used"] = n0 + 8

        compress_stage()
        cmp_s.close()

        attn = ExitStack()
        gates = ngate[:, :, :].rearrange("p t (h b) -> p t h b", b=3)

        def cmp_attention_stage():
            with ExitStack() as sc:
                scores = sb("cscores", [P, 2, NSA_H, 32], sc)
                probT = sb("cpT", [P, 2, S], sc)
                scored, masked, exped, turned, copied, summed, done, chain = (
                    sem(f"ca_{k}", sc) for k in ("scored", "masked", "exped", "turned", "copied", "summed", "done", "chain"))
                with nc.Block() as block:
                    @block.tensor
                    def _(pe):
                        def products(t):
                            if t >= 2:
                                pe.wait_ge(masked, t - 1)
                            for h in range(NSA_H):
                                for k in range(2):
                                    mm = nc.tensor.matmul(bank[t % 2][:, 32 * h:32 * h + 32], lhsT=nq[:, h, q_tile(t)],
                                                          rhs=kcmp[k][:, h // HPG, :], start=(k == 0), stop=(k == 1))
                            mm.then_inc(scored, 1)

                        def turn(t):
                            pe.wait_ge(exped, t + 1)
                            if t >= 2:
                                pe.wait_ge(copied, t - 1)
                            for g in range(NSA_G):
                                mm = nc.tensor.transpose(bank[2 + t % 2][:, g * P:(g + 1) * P],
                                                         scores[:, t % 2, 4 * g:4 * g + 4, :].rearrange("p h n -> p (h n)"),
                                                         ident)
                            mm.then_inc(turned, 1)

                        def values(t):
                            pe.wait_ge(copied, t + 1)
                            if t >= 2:
                                pe.wait_ge(done, t - 1)
                            for g in range(NSA_G):
                                to = bank[4 + 2 * (t % 2) + g // 2]
                                mm = nc.tensor.matmul(to[:, (g % 2) * 256:(g % 2) * 256 + 256],
                                                      lhsT=probT[:, t % 2, g * P:(g + 1) * P], rhs=vcmp[:, g, :],
                                                      start=True, stop=True)
                            mm.then_inc(summed, 1)

                        products(0)
                        for t in range(NT):
                            if t + 1 < NT:
                                products(t + 1)
                            turn(t)
                            if t >= 1:
                                values(t - 1)
                        values(NT - 1)

                    @block.scalar
                    def _(a):
                        for t in range(NT):
                            a.wait_ge(masked, t + 1)
                            nc.scalar.activation(scores[:, t % 2, :, :], scores[:, t % 2, :, :], ACT.Exp).then_inc(exped, 1)
                            a.wait_ge(turned, t + 1)
                            if t >= 2:
                                a.wait_ge(summed, t - 1)
                            nc.scalar.activation(probT[:, t % 2, :], bank[2 + t % 2], ACT.Copy).then_inc(copied, 1)

                    @block.vector
                    def _(v):
                        link = Chain(v, chain)

                        def soften(t):
                            sv_ = scores[:, t % 2, :, :]
                            v.wait_ge(scored, t + 1)
                            if t >= 2:
                                v.wait_ge(turned, t - 1)
                            mask = const[:, C_CMP + 32 * t:C_CMP + 32 * t + 32].unsqueeze(1).to_broadcast([P, NSA_H, 32])
                            link(nc.vector.tensor_tensor(sv_, bank[t % 2].rearrange("p (h n) -> p h n", n=32), mask, ALU.add))
                            link(nc.vector.tensor_reduce(stat[:, 40:56], sv_, AXX, ALU.max))
                            nc.vector.tensor_tensor(sv_, sv_, stat[:, 40:56].unsqueeze(2).to_broadcast([P, NSA_H, 32]),
                                                    ALU.subtract).then_inc(masked, 1)

                        def finish(t):
                            v.wait_ge(exped, t + 1)
                            link(nc.vector.tensor_reduce(stat[:, 60:76], scores[:, t % 2, :, :], AXX, ALU.add))
                            link(nc.vector.reciprocal(stat[:, 80:96], stat[:, 60:76]))
                            link(nc.vector.tensor_scalar(stat[:, 80:96], stat[:, 80:96],
                                                         const[:, C_VALID + t:C_VALID + t + 1], None, ALU.mult))
                            link(nc.vector.tensor_tensor(stat[:, 100:116], stat[:, 80:96], gates[:, t, :, 0], ALU.mult))
                            v.wait_ge(summed, t + 1)
                            for b in range(2):
                                ins = nc.vector.tensor_tensor(
                                    ot[:, t, b * BANK:(b + 1) * BANK].rearrange("p (h d) -> p h d", d=HD),
                                    bank[4 + 2 * (t % 2) + b].rearrange("p (h d) -> p h d", d=HD),
                                    stat[:, 100 + 8 * b:108 + 8 * b].unsqueeze(2).to_broadcast([P, 8, HD]), ALU.mult)
                            ins.then_inc(done, 1)
                            v.wait_ge(done, t + 1)

                        for t in range(NT + 1):
                            if t < NT:
                                soften(t)
                            if t >= 1:
                                finish(t - 1)

        cmp_attention_stage()

        nsa_pairs = []
        for h in range(NSA_H):
            for t in range(NT):
                wd = (t + 1) * P
                nsa_pairs.append({
                    "units": [{
                        "width": wd,
                        "scores": [(0, wd, nq[:, h, q_tile(t)], hT[:, kb, 0:wd]),
                                   (0, wd, nq[:, h, q_tile(t)], hL[:, kb, 0:wd]),
                                   (t * P, P, ident_r, mask_r)],
                        "keys": [(j * P, nv[:, j, kb, :]) for j in range(t + 1)]}
                        for kb in (h // HPG, 4 + h // HPG)],
                    "gates": gates[:, t, h, 1:3],
                    "collect": collect_branches(ot[:, t, h * HD:(h + 1) * HD])})
        scratch = (sb("nprob", [P, 4, S], attn), sb("nprobT", [P, 4, S], attn, F32R),
                   sb("nprobL", [P, 3, S], attn, F32R), sb("nput", [P, 2, 2, P], attn))
        pair_attention_stage("nsa", nsa_pairs, scratch)
        attn.close()

        turn_split_stage("oT", [(tok(ot, c * P), (hT[:, c, :], hL[:, c, :])) for c in range(8)])
        token_stage("nsaO", (hT, hL), ND, [('nsa_w_out_2', BANK)] * 2, residual_add, all_v,
                    norm_gain=w['norm_cross_w_2'], norm_dst=(hT, hL))
        nsa.close()

        cross = ExitStack()
        cq = sb("cq", [P, ND, S], cross)
        ckT = sb("ckT", [P, ND, MEM], cross)
        cv_ = sb("cv", [P, 2, D], cross)
        co = sb("co", [P, NT, D], cross)
        memx = ExitStack()
        mem = sb("mem", [P, 2, D], memx)
        memT = sb("memT", [P, ND, MEM], memx, F32R)
        memL = sb("memL", [P, ND, MEM], memx, F32R)

        norm_stage("memn", mem, 2, w['mem_norm_w_2'].unsqueeze(0), (memT, memL), w['mem_2'])
        feature_stage("ckT", (memT, memL), MEM, ['ca_wkv_2'] * 8, lambda i, ps, vec: copy(vec, ckT[:, i, :], ps))
        token_stage("cv", (memT, memL), ND, [('ca_wkv_2', BANK)] * 2,
                    lambda c, t, ps, link: copy(link is not None, cv_[:, t, c * BANK:(c + 1) * BANK], ps), half, tiles=2)
        memx.close()
        feature_stage("cqT", (hT, hL), S, ['ca_wq_2'] * 8,
                      lambda i, ps, vec: scaled(vec, cq[:, i, :], ps, CA_D ** -0.5) if vec else
                      nc.scalar.activation(cq[:, i, :], ps, ACT.Copy, scale=CA_D ** -0.5))
        attn = ExitStack()
        prob = sb("cprob", [P, 3, 514], attn)
        probT = sb("cprobT", [P, 3, S], attn)
        ca_units = []
        for t in range(NT):
            for h in range(CA_H):
                ca_units.append({
                    "width": MEM,
                    "scores": [(0, MEM, cq[:, 2 * h + k, q_tile(t)], ckT[:, 2 * h + k, :]) for k in range(2)],
                    "keys": [(j * P, cv_[:, j, h * CA_D:(h + 1) * CA_D]) for j in range(2)],
                    "finish": finish_plain(co[:, t, h * CA_D:(h + 1) * CA_D])})
        attention_stage("xattn", ca_units, (prob, probT))
        attn.close()
        turn_split_stage("coT", [(tok(co, c * P), (hT[:, c, :], hL[:, c, :])) for c in range(8)])
        token_stage("cao", (hT, hL), ND, [('ca_wo_2', BANK)] * 2, residual_add, all_v,
                    norm_gain=w['norm_ffn_w_2'], norm_dst=(hT, hL))
        cross.close()

        ffn("ffn2", 'ffn_w_up_2', 'ffn_w_up_2', 'ffn_w_down_2',
            lambda j, f: par[:, K_CONV2 + 22 * j + f:K_CONV2 + 22 * j + f + 1],
            w['final_norm_w_2'].unsqueeze(0), None)
        assert state["used"] == len(plan)



_WEIGHTS = ['w_in', 'w_fox_out', 'w_conv_out', 'w_mlstm_out', 'w_swa_out', 'w_merge_out', 'w_gate', 'w_up', 'w_down',
            'nsa_w_in_2', 'nsa_ck_w1_2', 'nsa_ck_w2_2', 'nsa_cv_w1_2', 'nsa_cv_w2_2', 'nsa_w_out_2', 'ca_wq_2',
            'ca_wkv_2', 'ca_wo_2', 'ffn_w_up_2', 'ffn_w_down_2']
_OTHERS = ['x', 'mem_2', 'rel_bias', 'mlstm_h_gain', 'swa_sinks', 'attn_norm', 'ffn_norm', 'norm_mix_w_2',
           'norm_cross_w_2', 'norm_ffn_w_2', 'mem_norm_w_2', 'final_norm_w_2']


def kernel(**inputs):
    import concourse.bacc as bacc
    from concourse.bass_utils import run_bass_kernel_spmd

    nc = bacc.Bacc("TRN2", target_bir_lowering=False, num_devices=1)
    a = {k: np.asarray(v) for k, v in inputs.items()}
    send = {k: np.ascontiguousarray(a[k][0]) for k in _WEIGHTS}
    send.update({k: np.ascontiguousarray(a[k]) for k in _OTHERS})
    send['w_in'] = pair_heads(send['w_in'], SQ, 1, SWA_H // 2)
    send['nsa_w_in_2'] = pair_heads(send['nsa_w_in_2'], NQ, 2, HPG)
    send['const'] = shape_constants()
    send['par'] = pack_params(a)
    arrays, w = {}, {}
    for name, v in send.items():
        arrays[f"in_{name}"] = v
        w[name] = nc.dram_tensor(f"in_{name}", v.shape, F32, kind="ExternalInput").ap()
    w['bias_rows'] = nc.dram_tensor("bias_rows", [SWA_H, 384], F32, kind="Internal").ap()
    out = nc.dram_tensor("out", [1, S, D], F32, kind="ExternalOutput").ap()
    build(nc, w, out)
    r = run_bass_kernel_spmd(nc, [arrays], core_ids=[0])
    return np.asarray(r.results[0]["out"]).reshape(1, S, D)
```
